# Optimizing a Trainium2 kernel written in Bass

```python
import math
import jax, jax.numpy as jnp
from jax import lax
import numpy as np

D_MODEL = 1024
BATCH = 1
SEQ = 256
DEPTH = 2

CHUNK = 64
Q_BLOCK = 128
HEAD_DIM = 64
EPS = 1e-6
ROPE_THETA = 500000.0
ROPE_DIMS = HEAD_DIM // 4

A_HEADS = 4
A_VDIM = 2 * HEAD_DIM
B_HEADS = 8
B_LEFT_CHUNKS = 8
B_BAND = (B_LEFT_CHUNKS + 1) * CHUNK
REL_CLIP = 128
C_HEADS = 8

BRANCH_WIDTH = 512
N_BRANCH = 3

PEER_HEADS = 8
N_KEYS = 128
N_EXPERTS = N_KEYS * N_KEYS
PEER_QDIM = 256
PEER_HALF = PEER_QDIM // 2
PEER_TOPK = 16
PEER_TOKEN_BLOCK = 128

A_QK_W = A_HEADS * 2 * HEAD_DIM
A_V_W = A_HEADS * A_VDIM
B_W = B_HEADS * HEAD_DIM
C_W = C_HEADS * HEAD_DIM
GATE_W = N_BRANCH * D_MODEL
SPLIT_SIZES = (A_QK_W, A_QK_W, A_V_W, B_W, B_W, B_W, C_W, C_W, C_W, GATE_W)
SPLIT_POINTS = tuple(int(v) for v in np.cumsum(SPLIT_SIZES)[:-1])
IN_COLS = sum(SPLIT_SIZES)

kernel_name = 'hybrid_diff_band_stickbreak_peer'

def rms_norm(x, g):
    xf = x.astype(jnp.float32)
    y = xf * lax.rsqrt(jnp.mean(xf * xf, axis=-1, keepdims=True) + EPS)
    return (y * g.astype(jnp.float32)).astype(x.dtype)

def rope_tables(seq):
    inv = 1.0 / (ROPE_THETA ** (jnp.arange(0, ROPE_DIMS, 2, dtype=jnp.float32) / ROPE_DIMS))
    ang = jnp.arange(seq, dtype=jnp.float32)[:, None] * inv[None, :]
    return jnp.cos(ang), jnp.sin(ang)

def apply_partial_rope(x, cos, sin):
    half = ROPE_DIMS // 2
    x1, x2, xp = x[..., :half], x[..., half:ROPE_DIMS], x[..., ROPE_DIMS:]
    c = cos.astype(x.dtype)
    s = sin.astype(x.dtype)
    return jnp.concatenate([x1 * c - x2 * s, x2 * c + x1 * s, xp], axis=-1)

def diff_attention(q, k, v, lam, subln_g, lam_init):
    B, H, _, S, d = q.shape
    nb = S // Q_BLOCK
    qb = jnp.moveaxis(q.reshape(B, H, 2, nb, Q_BLOCK, d), 3, 0)
    key_chunk = jnp.arange(S) // CHUNK
    scale = d ** -0.5

    def one_block(args):
        qblk, i = args
        s = jnp.einsum('bhcqd,bhckd->bhcqk', qblk, k).astype(jnp.float32) * scale
        q_chunk = (i * Q_BLOCK + jnp.arange(Q_BLOCK)) // CHUNK
        mask = key_chunk[None, :] <= q_chunk[:, None]
        s = jnp.where(mask, s, -jnp.inf)
        p = jax.nn.softmax(s, axis=-1)
        w = p[:, :, 0] - lam * p[:, :, 1]
        return jnp.einsum('bhqk,bhkv->bhqv', w.astype(v.dtype), v)

    o = lax.map(one_block, (qb, jnp.arange(nb)))
    o = jnp.moveaxis(o, 0, 2).reshape(B, H, S, v.shape[-1])
    return rms_norm(o, subln_g) * (1.0 - lam_init)

def chunk_band_attention(q, k, v, rel_bias):
    B, H, S, d = q.shape
    nc = S // CHUNK
    qc = q.reshape(B, H, nc, CHUNK, d)

    def band(t):
        tc = t.reshape(B, H, nc, CHUNK, d)
        tp = jnp.pad(tc, ((0, 0), (0, 0), (B_LEFT_CHUNKS, 0), (0, 0), (0, 0)))
        return jnp.concatenate([tp[:, :, j:j + nc] for j in range(B_LEFT_CHUNKS + 1)], axis=3)

    kb, vb = band(k), band(v)
    s = jnp.einsum('bhcqd,bhckd->bhcqk', qc, kb).astype(jnp.float32) * (d ** -0.5)
    qi = jnp.arange(CHUNK)[:, None]
    m = jnp.arange(B_BAND)[None, :]
    dist = qi + B_LEFT_CHUNKS * CHUNK - m
    rel_idx = jnp.clip(dist, -REL_CLIP, REL_CLIP) + REL_CLIP
    bias = rel_bias[:, rel_idx].astype(jnp.float32)
    valid = (jnp.arange(nc)[:, None] + (jnp.arange(B_BAND) // CHUNK)[None, :] - B_LEFT_CHUNKS) >= 0
    s = jnp.where(valid[None, None, :, None, :], s + bias[None, :, None], -jnp.inf)
    p = jax.nn.softmax(s, axis=-1)
    o = jnp.einsum('bhcqk,bhckd->bhcqd', p.astype(vb.dtype), vb)
    return o.reshape(B, H, S, d)

def stick_breaking_attention(q, k, v):
    B, H, S, d = q.shape
    nb = S // Q_BLOCK
    qb = jnp.moveaxis(q.reshape(B, H, nb, Q_BLOCK, d), 2, 0)
    key_pos = jnp.arange(S)
    scale = d ** -0.5

    def one_block(args):
        qblk, i = args
        z = jnp.einsum('bhqd,bhkd->bhqk', qblk, k).astype(jnp.float32) * scale
        q_pos = i * Q_BLOCK + jnp.arange(Q_BLOCK)
        strict = key_pos[None, :] < q_pos[:, None]
        log_keep = jnp.where(strict, jax.nn.log_sigmoid(-z), 0.0)
        later = lax.cumsum(log_keep, axis=3, reverse=True) - log_keep
        a = jnp.where(strict, jnp.exp(jax.nn.log_sigmoid(z) + later), 0.0)
        return jnp.einsum('bhqk,bhkd->bhqd', a.astype(v.dtype), v)

    o = lax.map(one_block, (qb, jnp.arange(nb)))
    return jnp.moveaxis(o, 0, 2).reshape(B, H, S, d)

def peer(xn, wq, subkeys, u, v):
    B, S, D = xn.shape
    T = B * S
    xt = xn.reshape(T, D)
    q = (xt @ wq).reshape(T, PEER_HEADS, 2, PEER_HALF)
    s = jnp.einsum('thpc,phnc->thpn', q, subkeys).astype(jnp.float32)
    top_s, top_i = lax.top_k(s, PEER_TOPK)
    cand_s = top_s[:, :, 0, :, None] + top_s[:, :, 1, None, :]
    cand_i = top_i[:, :, 0, :, None] * N_KEYS + top_i[:, :, 1, None, :]
    best_s, best_pos = lax.top_k(cand_s.reshape(T, PEER_HEADS, PEER_TOPK * PEER_TOPK), PEER_TOPK)
    expert = jnp.take_along_axis(cand_i.reshape(T, PEER_HEADS, PEER_TOPK * PEER_TOPK), best_pos, axis=-1)
    g = jax.nn.softmax(best_s, axis=-1)
    nb = T // PEER_TOKEN_BLOCK

    def one_block(args):
        xb, eb, gb = args
        ub = u[eb]
        hid = jax.nn.gelu(jnp.einsum('td,thkd->thk', xb, ub), approximate=False)
        vb = v[eb]
        return jnp.einsum('thk,thkd->td', (gb * hid).astype(vb.dtype), vb)

    out = lax.map(one_block, (xt.reshape(nb, PEER_TOKEN_BLOCK, D),
                              expert.reshape(nb, PEER_TOKEN_BLOCK, PEER_HEADS, PEER_TOPK),
                              g.reshape(nb, PEER_TOKEN_BLOCK, PEER_HEADS, PEER_TOPK)))
    return out.reshape(B, S, D)

def setup_inputs(seed: int = 0) -> dict:
    key = jax.random.key(seed)
    ks = jax.random.split(key, 20)
    nrm = lambda k, shape, sc: jax.random.normal(k, shape, jnp.float32) * sc
    gain = lambda k, shape: 1.0 + 0.02 * jax.random.normal(k, shape, jnp.float32)
    return {
        'x': nrm(ks[0], (BATCH, SEQ, D_MODEL), 1.0),
        'norm1_g': gain(ks[1], (DEPTH, D_MODEL)),
        'w_in': nrm(ks[2], (DEPTH, D_MODEL, IN_COLS), D_MODEL ** -0.5),
        'a_qnorm_g': gain(ks[3], (DEPTH, HEAD_DIM)),
        'a_knorm_g': gain(ks[4], (DEPTH, HEAD_DIM)),
        'lam_q1': nrm(ks[5], (DEPTH, HEAD_DIM), 0.1),
        'lam_k1': nrm(ks[6], (DEPTH, HEAD_DIM), 0.1),
        'lam_q2': nrm(ks[7], (DEPTH, HEAD_DIM), 0.1),
        'lam_k2': nrm(ks[8], (DEPTH, HEAD_DIM), 0.1),
        'a_subln_g': gain(ks[9], (DEPTH, A_VDIM)),
        'b_qnorm_g': gain(ks[10], (DEPTH, HEAD_DIM)),
        'b_knorm_g': gain(ks[11], (DEPTH, HEAD_DIM)),
        'b_rel_bias': nrm(ks[12], (DEPTH, B_HEADS, 2 * REL_CLIP + 1), 0.1),
        'w_branch': nrm(ks[13], (DEPTH, N_BRANCH, BRANCH_WIDTH, D_MODEL), BRANCH_WIDTH ** -0.5),
        'w_out': nrm(ks[14], (DEPTH, D_MODEL, D_MODEL), D_MODEL ** -0.5),
        'norm2_g': gain(ks[15], (DEPTH, D_MODEL)),
        'peer_wq': nrm(ks[16], (DEPTH, D_MODEL, PEER_HEADS * PEER_QDIM), D_MODEL ** -0.5),
        'peer_subkeys': nrm(ks[17], (DEPTH, 2, PEER_HEADS, N_KEYS, PEER_HALF), PEER_HALF ** -0.5),
        'peer_u': nrm(ks[18], (DEPTH, N_EXPERTS, D_MODEL), D_MODEL ** -0.5),
        'peer_v': nrm(ks[19], (DEPTH, N_EXPERTS, D_MODEL), PEER_HEADS ** -0.5),
    }

def reference(x, norm1_g, w_in, a_qnorm_g, a_knorm_g, lam_q1, lam_k1, lam_q2, lam_k2,
              a_subln_g, b_qnorm_g, b_knorm_g, b_rel_bias, w_branch, w_out, norm2_g,
              peer_wq, peer_subkeys, peer_u, peer_v):
    B, S, D = x.shape
    cos, sin = rope_tables(S)
    for layer in range(DEPTH):
        lam_init = 0.8 - 0.6 * math.exp(-0.3 * layer)
        h = rms_norm(x, norm1_g[layer])
        proj = h @ w_in[layer]
        (aq, ak, av, bq, bk, bv, cq, ck, cv, gl) = jnp.split(proj, SPLIT_POINTS, axis=-1)

        aq = jnp.transpose(aq.reshape(B, S, A_HEADS, 2, HEAD_DIM), (0, 2, 3, 1, 4))
        ak = jnp.transpose(ak.reshape(B, S, A_HEADS, 2, HEAD_DIM), (0, 2, 3, 1, 4))
        av = jnp.transpose(av.reshape(B, S, A_HEADS, A_VDIM), (0, 2, 1, 3))
        aq = apply_partial_rope(rms_norm(aq, a_qnorm_g[layer]), cos, sin)
        ak = apply_partial_rope(rms_norm(ak, a_knorm_g[layer]), cos, sin)
        lam = (jnp.exp(jnp.sum(lam_q1[layer].astype(jnp.float32) * lam_k1[layer].astype(jnp.float32)))
               - jnp.exp(jnp.sum(lam_q2[layer].astype(jnp.float32) * lam_k2[layer].astype(jnp.float32)))
               + lam_init)
        ya = diff_attention(aq, ak, av, lam, a_subln_g[layer], lam_init)
        ya = jnp.transpose(ya, (0, 2, 1, 3)).reshape(B, S, A_V_W)

        to_heads = lambda t, nh: jnp.transpose(t.reshape(B, S, nh, HEAD_DIM), (0, 2, 1, 3))
        bq = rms_norm(to_heads(bq, B_HEADS), b_qnorm_g[layer])
        bk = rms_norm(to_heads(bk, B_HEADS), b_knorm_g[layer])
        yb = chunk_band_attention(bq, bk, to_heads(bv, B_HEADS), b_rel_bias[layer])
        yb = jnp.transpose(yb, (0, 2, 1, 3)).reshape(B, S, B_W)

        yc = stick_breaking_attention(to_heads(cq, C_HEADS), to_heads(ck, C_HEADS), to_heads(cv, C_HEADS))
        yc = jnp.transpose(yc, (0, 2, 1, 3)).reshape(B, S, C_W)

        branches = jnp.stack([ya, yb, yc], axis=2)
        up = jnp.einsum('bsnw,nwd->bsnd', branches, w_branch[layer])
        gates = jax.nn.sigmoid(gl.reshape(B, S, N_BRANCH, D).astype(jnp.float32)).astype(up.dtype)
        merged = jnp.sum(gates * up, axis=2)
        x = x + merged @ w_out[layer]

        h2 = rms_norm(x, norm2_g[layer])
        x = x + peer(h2, peer_wq[layer], peer_subkeys[layer], peer_u[layer], peer_v[layer])
    return x


_drawn_inputs = setup_inputs


def setup_inputs(seed=0):
    import zlib

    import numpy as np

    out = dict(_drawn_inputs(seed))
    spreads = {}
    factors = {'b_qnorm_g': 4.161, 'b_knorm_g': 4.197}
    for name, (base, spread) in spreads.items():
        noise = np.random.default_rng([zlib.crc32(name.encode()), seed]).standard_normal(out[name].shape)
        drawn = base * np.exp(spread * noise) if base else spread * noise
        out[name] = __import__('jax').numpy.asarray(drawn.astype(out[name].dtype))
    for name, factor in factors.items():
        out[name] = (out[name] * factor).astype(out[name].dtype)
    return out
```

```python
import math
from contextlib import ExitStack

import numpy as np
import concourse.bass as bass
from concourse import mybir

D, T, LAYERS = 1024, 256, 2
P = 128
TT = T // P
KC = D // P
HD = 64
A_HEADS, B_HEADS, C_HEADS = 4, 8, 8
PEER_HEADS, KEYS, TOPK = 8, 128, 16
REL = 128
SLOTS, SLOT = 4, 2048
N_QKV, N_GATE, N_BR, N_OUT, N_WQ = 18, 12, 6, 4, 8
N_STREAM = N_QKV + N_GATE + N_BR + N_OUT + N_WQ
PAIRS = KEYS // 2
ROUNDS_STREAM = N_STREAM // SLOTS
ROUNDS = (N_STREAM + 2 * PAIRS) // SLOTS
EPS = 1e-6
SCALE = HD ** -0.5
NEG = -1e30

C_N1, C_N2, C_SUB, C_LAMI, C_OML, C_COS, C_SIN = 0, 8, 16, 17, 18, 19, 35
C_GAIN, C_LAM = 51, 307
N_PAR = 563

TOK, VV, QKT, GATE, YT, MRG, BIAS, SCR = 0, 6144, 9216, 15360, 21504, 24576, 26624, 28672
SRING, PTR, YSQ, YAN, UPT = 0, 1536, 2560, 3584, 4608
PQT, SSB, CAND, EQ, TOPV, TOPI, TOPF, BV, BP, PAB, PABF, BEST_D = (
    0, 4096, 9216, 11264, 13312, 13824, 14336, 14848, 15104, 15360, 15872, 16384)
EQ2 = 16896


class Signal:

    def __init__(self, sem, per_layer, start=0):
        self.sem, self.per_layer, self.start = sem, per_layer, start

    def at(self, layer, n):
        return layer * self.per_layer + (self.start + n)


class Count:

    def __init__(self):
        self.n = 0

    def one(self, ins):
        self.n += 1


def build(nc, x_in, stream, w_u, w_v, subk, params, bias_in, out):
    F = mybir.dt.float32
    U32 = mybir.dt.uint32
    ALU = mybir.AluOpType
    ACT = mybir.ActivationFunctionType
    AX = mybir.AxisListType
    ctx = ExitStack()
    with ctx:
        def sb(name, shape, dt=F):
            return ctx.enter_context(nc.sbuf_tensor(name, shape, dt))

        def sem(name):
            return ctx.enter_context(nc.semaphore(name))

        x = sb("x", [P, TT, D])
        hT = sb("hT", [P, KC, T])
        ring = sb("ring", [P, SLOTS, SLOT])
        par = sb("par", [P, N_PAR])
        arena = sb("arena", [P, KEYS * T])
        ident = sb("ident", [P, P])
        iota = sb("iota", [P, P])
        blockmask = sb("blockmask", [P, 2 * P])
        strict = sb("strict", [P, P])
        below = sb("below", [P, P])
        ones = sb("ones", [P, P])
        route = sb("route", [P, 3, T])
        hot_i = sb("hot_i", [P, 2, 4, P])
        hot_j = sb("hot_j", [P, 2, 4, P])
        act_h = sb("act_h", [P, 2, 512])
        wgt = sb("wgt", [P, 2, 512])
        half_neg = sb("half_neg", [P, 8])
        ssq = sb("ssq", [P, 2])
        rstd = sb("rstd", [P, 2])
        qk_ss = sb("qk_ss", [P, 8, 8])
        qk_rs = sb("qk_rs", [P, 8, 8])
        ya_ss = sb("ya_ss", [P, 2, 4])
        ya_rs = sb("ya_rs", [P, 2, 4])
        nmax = sb("nmax", [P, 16, 2])
        rsum = sb("rsum", [P, 16, 2])
        rinv = sb("rinv", [P, 16, 2])
        lam = sb("lam", [P, 8])
        rope_t = sb("rope_t", [P, 2, 8, 16])
        gsum = sb("gsum", [P, 8])
        ginv = sb("ginv", [P, 8])
        lam_w = sb("lam_w", [P, 2, HD])
        ps = ctx.enter_context(nc.psum_tensor("ps", [P, 8, 512], F))

        def view(off, *shape):
            n = int(np.prod(shape))
            v = arena[:, off:off + n]
            names = "abcd"[:len(shape)]
            if len(shape) == 1:
                return v
            spec = f"p ({' '.join(names)}) -> p {' '.join(names)}"
            return v.rearrange(spec, **dict(zip(names, shape)))

        tok = view(TOK, 6, TT, 512)
        vals = view(VV, 3, TT, 512)
        qkT = view(QKT, 6, 4, T)
        gates = view(GATE, 24, T)
        yT = view(YT, 3, 4, T)
        merged = view(MRG, KC, T)
        xs = view(MRG, TT, D)
        bias = view(BIAS, B_HEADS, T)
        subT = view(BIAS, 16, P)
        sq = view(SCR, 8, 512)
        nsq = view(SCR, TT, D)
        cz = view(SCR, 6, 512)
        ctmp = view(TOK + 4096, 3, 512)
        ce = view(YT, 6, 512)
        sring = view(SRING, 3, 2, 256)
        ptr = view(PTR, 2, 512)
        ysq = view(YSQ, 2, 512)
        yan = view(YAN, 2, 512)
        upt = view(UPT, 2, 512)
        pqT = view(PQT, 16, T)
        scores = view(SSB, TT, 16, P)
        cand = view(CAND, 8, 16, 16)
        eq = view(EQ, 8, 16, 16)
        eq2 = view(EQ2, 8, 16, 16)
        topv = view(TOPV, TT, 16, 16)
        topi = view(TOPI, TT, 16, 16).bitcast(U32)
        topf = view(TOPF, TT, 16, 16)
        bestv = view(BV, TT, 8, 16)
        bestp = view(BP, TT, 8, 16).bitcast(U32)
        pab = view(PAB, 2, 8, 16).bitcast(U32)
        pabf = view(PABF, 2, 8, 16)
        bd = view(BEST_D, TT, 128)
        rt_tok = view(EQ2 + 2048, TT, 3, P)
        G = view(0, KEYS, T)

        x_loaded = sem("x_loaded")
        w_loaded = [Signal(sem(f"w_loaded{s}"), ROUNDS * 16) for s in range(SLOTS)]
        par_loaded = Signal(sem("par_loaded"), 16)
        bias_loaded = Signal(sem("bias_loaded"), 16)
        subk_loaded = Signal(sem("subk_loaded"), 16)
        constants = sem("constants")
        layer_done = Signal(sem("layer_done"), 1, 1)
        squared = Signal(sem("squared"), 4)
        rstd_ready = Signal(sem("rstd_ready"), 4)
        xs_ready = Signal(sem("xs_ready"), 4)
        normT_mm = Signal(sem("normT_mm"), 8)
        hT_ready = Signal(sem("hT_ready"), 8)
        proj_mm = Signal(sem("proj_mm"), 48)
        proj_ev = Signal(sem("proj_ev"), 48)
        sq_ready = Signal(sem("sq_ready"), 8)
        ss_ready = Signal(sem("ss_ready"), 8)
        qkrs_ready = Signal(sem("qkrs_ready"), 8)
        qk_normed = Signal(sem("qk_normed"), 8)
        logs_ready = Signal(sem("logs_ready"), 2)
        keep_ready = Signal(sem("keep_ready"), 2)
        later_mm = Signal(sem("later_mm"), 6)
        loga_ready = Signal(sem("loga_ready"), 6)
        a_exp = Signal(sem("a_exp"), 6)
        a_ready = Signal(sem("a_ready"), 6)
        cout_mm = Signal(sem("cout_mm"), 2)
        yc_ready = Signal(sem("yc_ready"), 2)
        score_mm = Signal(sem("score_mm"), 16)
        smax_ready = Signal(sem("smax_ready"), 16)
        exp_ready = Signal(sem("exp_ready"), 16)
        prob_ready = Signal(sem("prob_ready"), 16)
        probT_mm = Signal(sem("probT_mm"), 16)
        probT_ready = Signal(sem("probT_ready"), 16)
        mix_mm = Signal(sem("mix_mm"), 16)
        ya_sq = Signal(sem("ya_sq"), 2)
        ya_ssr = Signal(sem("ya_ssr"), 2)
        ya_rsr = Signal(sem("ya_rsr"), 2)
        ya_normed = Signal(sem("ya_normed"), 2)
        yaT_mm = Signal(sem("yaT_mm"), 2)
        ya_ready = Signal(sem("ya_ready"), 2)
        yb_ready = Signal(sem("yb_ready"), 2)
        lam_sum = Signal(sem("lam_sum"), 1)
        lam_exp = Signal(sem("lam_exp"), 1)
        bias_ready = Signal(sem("bias_ready"), 1)
        gate_ready = Signal(sem("gate_ready"), 3)
        up_mm = Signal(sem("up_mm"), 12)
        up_taken = Signal(sem("up_taken"), 12)
        merged_ready = Signal(sem("merged_ready"), 1)
        wout_mm = Signal(sem("wout_mm"), 4)
        x_mid = Signal(sem("x_mid"), 4)
        pq_mm = Signal(sem("pq_mm"), 8)
        pq_ready = Signal(sem("pq_ready"), 8)
        s_mm = Signal(sem("s_mm"), 8)
        s_ready = Signal(sem("s_ready"), 8)
        best_ready = Signal(sem("best_ready"), 2)
        best_exp = Signal(sem("best_exp"), 2)
        rt_ready = Signal(sem("rt_ready"), 2)
        rtT_mm = Signal(sem("rtT_mm"), 2)
        route_ready = Signal(sem("route_ready"), 2)
        hot_ready = Signal(sem("hot_ready"), 64)
        g_mm = Signal(sem("g_mm"), 64, 2)
        g_ready = Signal(sem("g_ready"), 64, 4)
        h_mm = Signal(sem("h_mm"), PAIRS, 2)
        gelu_ready = Signal(sem("gelu_ready"), PAIRS, 2)
        wgt_ready = Signal(sem("wgt_ready"), PAIRS, 2)
        v_mm = Signal(sem("v_mm"), PAIRS, 2)
        dve_chain, act_chain, pool_chain = sem("dve_chain"), sem("act_chain"), sem("pool_chain")
        seen_sp, seen_dve, seen_pool = sem("seen_sp"), sem("seen_dve"), sem("seen_pool")
        stored = sem("stored")

        def loads(layer, n):
            signal = w_loaded[n % SLOTS]
            return signal.sem, signal.at(layer, 16 * (n // SLOTS + 1))

        SCORE_BANK = (2, 6)

        def by_head(i):
            return (i % 8) // 4, i % 4

        def c_heads(c):
            if c < 2:
                return 1, c, [c + 2 * j for j in range(4)]
            par_, g = (c - 2) % 2, (c - 2) // 2
            return 0, par_, [par_ + 4 * g, par_ + 4 * g + 2]

        block = ctx.enter_context(nc.Block())

        M_CT, M_G0, M_CZ, M_G4, M_G8, M_ABT = 18, 22, 26, 32, 36, 40

        def proj_bank(m):
            return m % 8 if m < 18 else (m - 18) % 4

        def gate_m(g):
            return (M_G0, M_G4, M_G8)[g // 4] + g % 4

        @block.sync
        def _(sp):
            sp.dma_start(x[:], x_in).then_inc(x_loaded, 16)

            def slot_of(n):
                if n < N_QKV:
                    return proj_mm, 2 * (n // 2) + 2
                n -= N_QKV
                if n < N_GATE:
                    return proj_mm, gate_m(n) + 1
                n -= N_GATE
                if n < N_BR:
                    return up_mm, 2 * n + 2
                n -= N_BR
                if n < N_OUT:
                    return wout_mm, 2 * (n // 2) + 2
                return pq_mm, n - N_OUT + 1

            with sp.Fori(0, LAYERS) as layer:
                for n in range(N_STREAM):
                    if n < SLOTS:
                        sig = h_mm if n % 2 == 0 else v_mm
                        sp.wait_ge(sig.sem, sig.at(layer, 0))
                    else:
                        sig, used = slot_of(n - SLOTS)
                        sp.wait_ge(sig.sem, sig.at(layer, used))
                    sp.sem_inc(seen_sp, 1)
                    sp.dma_start(ring[:, n % SLOTS, :],
                                 stream[bass.ds(layer * N_STREAM + n, 1), :, :].rearrange("a p n -> p (a n)")
                                 ).then_inc(w_loaded[n % SLOTS].sem, 16)

                def load_pairs(first, it):
                    for k in range(2):
                        p = it * 2 + k
                        if first:
                            sig, n = slot_of(N_STREAM - SLOTS + 2 * k)
                            sp.wait_ge(sig.sem, sig.at(layer, n))
                            sp.sem_inc(seen_sp, 1)
                        sp.wait_ge(h_mm.sem, h_mm.at(layer, p - 1))
                        sp.sem_inc(seen_sp, 1)
                        sp.dma_start(ring[:, 2 * k, :],
                                     w_u[bass.ds(layer * PAIRS + p, 1), :, :].rearrange("a p n -> p (a n)")
                                     ).then_inc(w_loaded[2 * k].sem, 16)
                        if first:
                            sig, n = slot_of(N_STREAM - SLOTS + 2 * k + 1)
                            sp.wait_ge(sig.sem, sig.at(layer, n))
                            sp.sem_inc(seen_sp, 1)
                        sp.wait_ge(v_mm.sem, v_mm.at(layer, p - 1))
                        sp.sem_inc(seen_sp, 1)
                        sp.dma_start(ring[:, 2 * k + 1, :],
                                     w_v[bass.ds(layer, 1), :, bass.ds(p, 1), :].rearrange("a p b n -> p (a b n)")
                                     ).then_inc(w_loaded[2 * k + 1].sem, 16)

                load_pairs(True, 0)
                with sp.Fori(1, PAIRS // 2) as it:
                    load_pairs(False, it)
            sp.wait_ge(layer_done.sem, layer_done.at(LAYERS, 0))
            sp.dma_start(out, x[:]).then_inc(stored, 16)
            sp.wait_ge(stored, 16)

        @block.gpsimd
        def _(pool):
            own = Count()

            def fill(t, value):
                own.one(nc.gpsimd.memset(t, value).then_inc(pool_chain, 1))

            fill(ident[:], 0.0)
            fill(ones[:], 1.0)
            fill(strict[:], 1.0)
            fill(below[:], 1.0)
            fill(blockmask[:], 0.0)
            fill(half_neg[:], -0.5)
            pool.wait_ge(pool_chain, own.n)
            own.one(nc.gpsimd.affine_select(out=ident[:], in_=ident[:], compare_op=ALU.not_equal, fill=1.0,
                                              base=0, pattern=[[-1, P]], channel_multiplier=1).then_inc(pool_chain, 1))
            own.one(nc.gpsimd.affine_select(out=strict[:], in_=strict[:], compare_op=ALU.is_gt, fill=0.0,
                                              base=0, pattern=[[1, P]], channel_multiplier=-1).then_inc(pool_chain, 1))
            own.one(nc.gpsimd.affine_select(out=below[:], in_=below[:], compare_op=ALU.is_gt, fill=0.0,
                                              base=0, pattern=[[-1, P]], channel_multiplier=1).then_inc(pool_chain, 1))
            own.one(nc.gpsimd.memset(blockmask[0:64, P + 64:2 * P], NEG).then_inc(pool_chain, 1))
            own.one(nc.gpsimd.iota(iota[:], pattern=[[1, P]], base=0, channel_multiplier=0,
                                     allow_small_or_imprecise_dtypes=True).then_inc(pool_chain, 1))
            pool.wait_ge(pool_chain, own.n)
            pool.sem_inc(constants, 1)
            pool.wait_ge(pool_chain, own.n)
            pool.sem_clear(pool_chain)
            own.n = 0

            with pool.Fori(0, LAYERS) as layer:
                def inverse_root(dst, src, count, wait_for, n, ready):
                    pool.wait_ge(wait_for.sem, wait_for.at(layer, n))
                    pool.sem_inc(seen_pool, 1)
                    own.one(nc.gpsimd.tensor_scalar(dst, src, 1.0 / count, EPS, ALU.mult, ALU.add).then_inc(pool_chain, 1))
                    pool.wait_ge(pool_chain, own.n)
                    nc.gpsimd.tensor_tensor(dst, dst, half_neg[:, 0:dst.shape[-1]], ALU.pow
                                            ).then_inc(ready.sem, 1)

                for t in range(TT):
                    inverse_root(rstd[:, t:t + 1], ssq[:, t:t + 1], D, squared, t + 1, rstd_ready)
                pool.wait_ge(bias_loaded.sem, bias_loaded.at(layer, 16))
                pool.sem_inc(seen_pool, 1)
                nc.gpsimd.tensor_tensor(bias[:], bias[:],
                                        blockmask[:].unsqueeze(1).broadcast_to([P, B_HEADS, 2 * P]),
                                        ALU.add).then_inc(bias_ready.sem, 1)
                for i in range(8):
                    inverse_root(qk_rs[:, i, :], qk_ss[:, i, :], HD, ss_ready, i + 1, qkrs_ready)
                for t in range(TT):
                    inverse_root(ya_rs[:, t, :], ya_ss[:, t, :], P, ya_ssr, t + 1, ya_rsr)
                for t in range(TT):
                    inverse_root(rstd[:, t:t + 1], ssq[:, t:t + 1], D, squared, TT + t + 1, rstd_ready)
                pool.wait_ge(pool_chain, own.n)
                pool.sem_clear(pool_chain)
                own.n = 0

        @block.tensor
        def _(pe):
            mm = nc.tensor.matmul
            for s in (h_mm, v_mm, g_mm):
                pe.sem_inc(s.sem, s.start)
            pe.wait_ge(constants, 1)

            def transposes(dst, src, count):
                for q in range(count):
                    last = nc.tensor.transpose(dst[:, q * P:(q + 1) * P], src[:, q * P:(q + 1) * P], ident[:])
                return last

            with pe.Fori(0, LAYERS) as layer:
                def norm_transposes(which):
                    for n in range(4):
                        t, half = n // 2, n % 2
                        if half == 0:
                            pe.wait_ge(xs_ready.sem, xs_ready.at(layer, 2 * which + t + 1))
                        transposes(ps[:, n, :], xs[:, t, half * 512:(half + 1) * 512], 4
                                   ).then_inc(normT_mm.sem, 1)

                def by_token(lhs, bank, n0, signal, first_wait):
                    for kh in range(2):
                        pe.wait_ge(*loads(layer, n0 + kh))
                        for t in range(TT):
                            if kh == 0:
                                first_wait(t)
                            for kc in range(4):
                                last = mm(ps[:, bank(t), :], lhs[:, kh * 4 + kc, t * P:(t + 1) * P],
                                          ring[:, (n0 + kh) % SLOTS, kc * 512:(kc + 1) * 512],
                                          start=(kh == 0 and kc == 0), stop=(kh == 1 and kc == 3))
                            if kh == 1:
                                last.then_inc(signal.sem, 1)

                def by_feature(bank, n, signal):
                    pe.wait_ge(*loads(layer, n))
                    for c2 in range(2):
                        for kc in range(KC):
                            last = mm(ps[:, bank, c2 * T:(c2 + 1) * T],
                                      ring[:, n % SLOTS, kc * 256 + c2 * P:kc * 256 + (c2 + 1) * P],
                                      hT[:, kc, :], start=(kc == 0), stop=(kc == KC - 1))
                    last.then_inc(signal.sem, 1)

                norm_transposes(0)
                pe.wait_ge(hT_ready.sem, hT_ready.at(layer, 4))
                for cb in range(9):
                    def bank_free(t):
                        if 2 * cb + t >= 8:
                            pe.wait_ge(proj_ev.sem, proj_ev.at(layer, 2 * cb + t - 7))
                    by_token(hT, lambda t: proj_bank(2 * cb + t), 2 * cb, proj_mm, bank_free)

                def feature_tile(m, ten, t):
                    transposes(ps[:, proj_bank(m), :], tok[:, ten, t, :], 4).then_inc(proj_mm.sem, 1)

                for r in range(4):
                    pe.wait_ge(proj_ev.sem, proj_ev.at(layer, 18))
                    feature_tile(M_CT + r, 4 + r // 2, r % 2)

                def gate_tiles(g0):
                    for g in range(g0, g0 + 4):
                        pe.wait_ge(proj_ev.sem, proj_ev.at(layer, gate_m(g) - 3))
                        by_feature(proj_bank(gate_m(g)), N_QKV + g, proj_mm)

                gate_tiles(0)
                for c in range(6):
                    kt, par_, heads = c_heads(c)
                    pe.wait_ge(proj_ev.sem, proj_ev.at(layer, M_CZ + c - 3))
                    n = (2 - kt) * P
                    for j, h in enumerate(heads):
                        rows = slice(64 * par_, 64 * par_ + 64)
                        last = mm(ps[:, proj_bank(M_CZ + c), j * n:(j + 1) * n],
                                  qkT[rows, 5, h // 2, kt * P:(kt + 1) * P], qkT[rows, 4, h // 2, kt * P:T],
                                  start=True, stop=True)
                    last.then_inc(proj_mm.sem, 1)
                gate_tiles(4)
                for c in range(6):
                    kt, par_, heads = c_heads(c)
                    pe.wait_ge(keep_ready.sem, keep_ready.at(layer, 1 if c < 3 else 2))
                    if c >= 2:
                        pe.wait_ge(loga_ready.sem, loga_ready.at(layer, c - 1))
                    last = mm(ps[:, 4 + c % 2, :], below[:], ce[:, c, :], start=True, stop=(kt == 1))
                    if kt == 0:
                        g = (c - 2) // 2
                        last = mm(ps[:, 4 + c % 2, :].rearrange("p (h q) -> p h q", h=2)[:, :, P:T], ones[:],
                                  ce[:, par_, 2 * g * P:(2 * g + 2) * P].rearrange("p (h q) -> p h q", h=2),
                                  start=False, stop=True)
                    last.then_inc(later_mm.sem, 1)
                gate_tiles(8)
                for r in range(8):
                    pe.wait_ge(proj_ev.sem, proj_ev.at(layer, M_ABT + r - 3))
                    pe.wait_ge(qk_normed.sem, qk_normed.at(layer, r + 1))
                    feature_tile(M_ABT + r, r // 2, r % 2)
                pe.wait_ge(a_ready.sem, a_ready.at(layer, 6))
                for o in range(2):
                    for h in range(4 * o, 4 * o + 4):
                        par_, rows = h % 2, slice(64 * (h % 2), 64 * (h % 2) + 64)
                        at = ((h // 2) % 2) * T
                        mm(ps[rows, 4 + o, at:at + T], vals[:, 2, 0, h * HD:(h + 1) * HD],
                           cz[:, 2 + par_ + 2 * (h // 4), ((h // 2) % 2) * T:((h // 2) % 2 + 1) * T],
                           start=True, stop=False)
                        last = mm(ps[rows, 4 + o, at + P:at + T], vals[:, 2, 1, h * HD:(h + 1) * HD],
                                  cz[:, par_, (h // 2) * P:(h // 2 + 1) * P], start=False, stop=True)
                    last.then_inc(cout_mm.sem, 1)

                def score(i):
                    t, ch = by_head(i)
                    q_, k_ = (0, 1) if i < 8 else (2, 3)
                    for c in range(2):
                        rows = slice(64 * c, 64 * c + 64)
                        last = mm(ps[:, SCORE_BANK[i % 2] + c, 0:(t + 1) * P],
                                  qkT[rows, q_, ch, t * P:(t + 1) * P], qkT[rows, k_, ch, 0:(t + 1) * P],
                                  start=True, stop=True)
                    last.then_inc(score_mm.sem, 1)

                def prob_transposes(i):
                    t, _ = by_head(i)
                    pe.wait_ge(prob_ready.sem, prob_ready.at(layer, i + 1))
                    if i >= 2:
                        pe.wait_ge(probT_ready.sem, probT_ready.at(layer, i - 1))
                    elif i == 0:
                        pe.wait_ge(yc_ready.sem, yc_ready.at(layer, 2))
                    for c in range(1 if i < 8 else 2):
                        last = transposes(ps[:, 4 + i % 2, c * (t + 1) * P:(c + 1) * (t + 1) * P],
                                          sring[:, i % 3, c, :], t + 1)
                    last.then_inc(probT_mm.sem, 1)

                def mix(i):
                    t, ch = by_head(i)
                    pe.wait_ge(probT_ready.sem, probT_ready.at(layer, i + 1))
                    if i >= 8 and ch == 0:
                        pe.wait_ge(ya_normed.sem, ya_normed.at(layer, t + 1))
                    if i < 8:
                        for kt in range(t + 1):
                            last = mm(ps[:, t, ch * P:(ch + 1) * P], ptr[:, i % 2, kt * P:(kt + 1) * P],
                                      vals[:, 0, kt, ch * P:(ch + 1) * P], start=(kt == 0), stop=(kt == t))
                    else:
                        for c in range(2):
                            h = 2 * ch + c
                            for kt in range(t + 1):
                                at = (c * (t + 1) + kt) * P
                                last = mm(ps[64 * c:64 * c + 64, t, ch * P:(ch + 1) * P],
                                          vals[:, 1, kt, h * HD:(h + 1) * HD], ptr[:, i % 2, at:at + P],
                                          start=(kt == 0), stop=(kt == t))
                    last.then_inc(mix_mm.sem, 1)

                pe.wait_ge(proj_ev.sem, proj_ev.at(layer, 48))
                score(0)
                score(1)
                for i in range(16):
                    prob_transposes(i)
                    if i + 2 < 16:
                        score(i + 2)
                    if i:
                        mix(i - 1)
                mix(15)
                pe.wait_ge(probT_ready.sem, probT_ready.at(layer, 16))
                for t in range(TT):
                    pe.wait_ge(ya_normed.sem, ya_normed.at(layer, t + 1))
                    transposes(ps[:, 4 + t, :], yan[:, t, :], 4).then_inc(yaT_mm.sem, 1)

                pe.wait_ge(ya_ready.sem, ya_ready.at(layer, 2))
                pe.wait_ge(yb_ready.sem, yb_ready.at(layer, 2))
                for u in range(12):
                    n = N_QKV + N_GATE + u // 2
                    if u >= 4:
                        pe.wait_ge(up_taken.sem, up_taken.at(layer, u - 3))
                    pe.wait_ge(*loads(layer, n))
                    for c2 in range(2):
                        for wc in range(4):
                            at = wc * 512 + ((u % 2) * 2 + c2) * P
                            last = mm(ps[:, u % 4, c2 * T:(c2 + 1) * T], ring[:, n % SLOTS, at:at + P],
                                      yT[:, u // 4, wc, :], start=(wc == 0), stop=(wc == 3))
                    last.then_inc(up_mm.sem, 1)
                pe.wait_ge(merged_ready.sem, merged_ready.at(layer, 1))
                for c in range(2):
                    by_token(merged, lambda t: 4 + 2 * c + t, N_STREAM - N_WQ - N_OUT + 2 * c, wout_mm,
                             lambda t: None)

                norm_transposes(1)
                pe.wait_ge(hT_ready.sem, hT_ready.at(layer, 8))
                for n in range(N_WQ):
                    if n >= 4:
                        pe.wait_ge(pq_ready.sem, pq_ready.at(layer, n - 3))
                    by_feature(4 + n % 4, N_STREAM - N_WQ + n, pq_mm)
                pe.wait_ge(subk_loaded.sem, subk_loaded.at(layer, 16))
                pe.wait_ge(pq_ready.sem, pq_ready.at(layer, 8))
                for n in range(8):
                    for q in range(4):
                        ch = (n % 4) * 4 + q
                        last = mm(ps[:, n, q * P:(q + 1) * P], pqT[:, ch, (n // 4) * P:(n // 4 + 1) * P],
                                  subT[:, ch, :], start=True, stop=True)
                    last.then_inc(s_mm.sem, 1)
                for t in range(TT):
                    pe.wait_ge(rt_ready.sem, rt_ready.at(layer, t + 1))
                    transposes(ps[:, t, :], rt_tok[:, t, :, :].rearrange("p a b -> p (a b)"), 3
                               ).then_inc(rtT_mm.sem, 1)

                with pe.Fori(0, T // 16) as it:
                    for b in range(4):
                        pe.wait_ge(hot_ready.sem, hot_ready.at(layer, it * 4 + (b + 1)))
                        pe.wait_ge(g_ready.sem, g_ready.at(layer, it * 4 + (b - 3)))
                        for q in range(4):
                            last = mm(ps[:, 4 + b, q * P:(q + 1) * P], hot_i[:, b % 2, q, :],
                                      hot_j[:, b % 2, q, :], start=True, stop=True)
                        last.then_inc(g_mm.sem, 1)

                def hidden(p, k):
                    pe.wait_ge(gelu_ready.sem, gelu_ready.at(layer, p - 1))
                    pe.wait_ge(w_loaded[2 * k].sem, w_loaded[2 * k].at(layer, (p + 2 * (N_STREAM // SLOTS) - k) * 8 + 16))
                    for e in range(2):
                        for kc in range(KC):
                            last = mm(ps[:, k, e * T:(e + 1) * T],
                                      ring[:, 2 * k, (e * KC + kc) * P:(e * KC + kc + 1) * P],
                                      hT[:, kc, :], start=(kc == 0), stop=(kc == KC - 1))
                    last.then_inc(h_mm.sem, 1)

                def expert_out(p, k, first=False, final=False):
                    pe.wait_ge(wgt_ready.sem, wgt_ready.at(layer, p + 1))
                    pe.wait_ge(w_loaded[2 * k + 1].sem, w_loaded[2 * k + 1].at(layer, (p + 2 * (N_STREAM // SLOTS) - k) * 8 + 16))
                    for e in range(2):
                        for t in range(TT):
                            for half in range(2):
                                last = mm(ps[:, 4 + 2 * t + half, :],
                                          wgt[:, k, e * T + t * P:e * T + (t + 1) * P],
                                          ring[:, 2 * k + 1, e * D + half * 512:e * D + (half + 1) * 512],
                                          start=(first and e == 0), stop=(final and e == 1),
                                          skip_group_check=True)
                    last.then_inc(v_mm.sem, 1)

                hidden(0, 0)
                hidden(1, 1)
                expert_out(0, 0, first=True)
                hidden(2, 0)
                expert_out(1, 1)
                with pe.Fori(1, PAIRS // 2 - 1) as it:
                    hidden(it * 2 + 1, 1)
                    expert_out(it * 2, 0)
                    hidden(it * 2 + 2, 0)
                    expert_out(it * 2 + 1, 1)
                hidden(PAIRS - 1, 1)
                expert_out(PAIRS - 2, 0)
                expert_out(PAIRS - 1, 1, final=True)

        @block.scalar
        def _(act):
            f = nc.scalar.activation
            own = Count()
            for s in (g_ready, gelu_ready):
                act.sem_inc(s.sem, s.start)
            act.wait_ge(x_loaded, 16)
            act.wait_ge(constants, 1)

            with act.Fori(0, LAYERS) as layer:
                act.wait_ge(layer_done.sem, layer_done.at(layer, 0))
                act.dma_start(par[:], params[bass.ds(layer, 1), :, :].rearrange("a p n -> p (a n)")
                              ).then_inc(par_loaded.sem, 16)
                act.dma_start(bias[:].rearrange("p a b -> p (a b)"),
                              bias_in[bass.ds(layer, 1), :, :].rearrange("a p n -> p (a n)")).then_inc(bias_loaded.sem, 16)

                def square_sums():
                    for t in range(TT):
                        f(nsq[:, t, :], x[:, t, :], ACT.Square, accum_out=ssq[:, t:t + 1]
                          ).then_inc(squared.sem, 1)

                square_sums()
                act.wait_ge(lam_sum.sem, lam_sum.at(layer, 1))
                f(lam[:, 2:4], lam[:, 0:2], ACT.Exp).then_inc(lam_exp.sem, 1)
                normed = {0: 0, 1: 1, 3: 2, 4: 3}
                where = {0: tok[:, 0], 1: tok[:, 1], 2: vals[:, 0], 3: tok[:, 2], 4: tok[:, 3],
                         5: vals[:, 1], 6: tok[:, 4], 7: tok[:, 5], 8: vals[:, 2]}
                for m in range(18):
                    cb, t = m // 2, m % 2
                    act.wait_ge(proj_mm.sem, proj_mm.at(layer, m + 1))
                    if cb in normed:
                        f(sq[:, 2 * normed[cb] + t, :], ps[:, proj_bank(m), :], ACT.Square
                          ).then_inc(sq_ready.sem, 1)
                    f(where[cb][:, t, :], ps[:, proj_bank(m), :], ACT.Copy).then_inc(proj_ev.sem, 1)

                def take_feature_tile(m, ten, t):
                    act.wait_ge(proj_mm.sem, proj_mm.at(layer, m + 1))
                    f(qkT[:, ten, :, t * P:(t + 1) * P], ps[:, proj_bank(m), :].rearrange("p (a b) -> p a b", a=4),
                      ACT.Copy).then_inc(proj_ev.sem, 1)

                def take_gates(g0):
                    for g in range(g0, g0 + 4):
                        act.wait_ge(proj_mm.sem, proj_mm.at(layer, gate_m(g) + 1))
                        f(gates[:, 2 * g:2 * g + 2, :], ps[:, proj_bank(gate_m(g)), :].rearrange(
                            "p (a b) -> p a b", a=2), ACT.Copy).then_inc(proj_ev.sem, 1)

                for r in range(4):
                    take_feature_tile(M_CT + r, 4 + r // 2, r % 2)
                take_gates(0)
                act.wait_ge(ss_ready.sem, ss_ready.at(layer, 8))
                for c in range(6):
                    act.wait_ge(proj_mm.sem, proj_mm.at(layer, M_CZ + c + 1))
                    own.one(f(ce[:, c, :], ps[:, proj_bank(M_CZ + c), :], ACT.Abs, scale=SCALE).then_inc(act_chain, 1))
                    f(cz[:, c, :], ps[:, proj_bank(M_CZ + c), :], ACT.Copy, scale=SCALE
                      ).then_inc(proj_ev.sem, 1)
                act.wait_ge(act_chain, own.n)
                for i in range(2):
                    own.one(f(ce[:, 3 * i:3 * i + 3, :], ce[:, 3 * i:3 * i + 3, :], ACT.Exp, scale=-1.0).then_inc(act_chain, 1))
                act.wait_ge(act_chain, own.n)
                for i in range(2):
                    f(ce[:, 3 * i:3 * i + 3, :], ce[:, 3 * i:3 * i + 3, :], ACT.Ln, bias=1.0
                      ).then_inc(logs_ready.sem, 1)
                take_gates(4)
                for c in range(6):
                    act.wait_ge(loga_ready.sem, loga_ready.at(layer, c + 1))
                    f(cz[:, c, :], cz[:, c, :], ACT.Exp).then_inc(a_exp.sem, 1)
                take_gates(8)
                for r in range(8):
                    take_feature_tile(M_ABT + r, r // 2, r % 2)
                for o in range(2):
                    act.wait_ge(cout_mm.sem, cout_mm.at(layer, o + 1))
                    f(yT[:, 2, 2 * o:2 * o + 2, :], ps[:, 4 + o, :].rearrange("p (a b) -> p a b", a=2),
                      ACT.Copy).then_inc(yc_ready.sem, 1)

                def take_probT(i):
                    t, _ = by_head(i)
                    n = (1 if i < 8 else 2) * (t + 1) * P
                    act.wait_ge(probT_mm.sem, probT_mm.at(layer, i + 1))
                    if i >= 2:
                        act.wait_ge(mix_mm.sem, mix_mm.at(layer, i - 1))
                    f(ptr[:, i % 2, 0:n], ps[:, 4 + i % 2, 0:n], ACT.Copy).then_inc(probT_ready.sem, 1)

                def take_yb(t):
                    act.wait_ge(mix_mm.sem, mix_mm.at(layer, 12 + 4 * t))
                    f(yT[:, 1, :, t * P:(t + 1) * P], ps[:, t, :].rearrange("p (a b) -> p a b", a=4), ACT.Copy
                      ).then_inc(yb_ready.sem, 1)

                for i in range(16):
                    t, _ = by_head(i)
                    act.wait_ge(smax_ready.sem, smax_ready.at(layer, i + 1))
                    for c in range(2):
                        s = sring[:, i % 3, c, 0:(t + 1) * P]
                        last = f(s, s, ACT.Exp, bias=nmax[:, i, c:c + 1], accum_out=rsum[:, i, c:c + 1])
                    last.then_inc(exp_ready.sem, 1)
                    if i:
                        take_probT(i - 1)
                    if i in (5, 9):
                        t = (i - 5) // 4
                        act.wait_ge(mix_mm.sem, mix_mm.at(layer, 4 * (t + 1)))
                        f(ysq[:, t, :], ps[:, t, :], ACT.Square).then_inc(ya_sq.sem, 1)
                    if i == 14:
                        take_yb(0)
                act.dma_start(subT[:].rearrange("p a b -> p (a b)"),
                              subk[bass.ds(layer, 1), :, :].rearrange("a p n -> p (a n)")
                              ).then_inc(subk_loaded.sem, 16)
                take_probT(15)
                take_yb(1)
                act.wait_ge(proj_ev.sem, proj_ev.at(layer, 48))
                for b in range(3):
                    f(gates[:, 8 * b:8 * b + 8, :], gates[:, 8 * b:8 * b + 8, :], ACT.Sigmoid
                      ).then_inc(gate_ready.sem, 1)
                act.wait_ge(x_mid.sem, x_mid.at(layer, 4))
                square_sums()
                for n in range(N_WQ):
                    act.wait_ge(pq_mm.sem, pq_mm.at(layer, n + 1))
                    f(pqT[:, 2 * n:2 * n + 2, :], ps[:, 4 + n % 4, :].rearrange("p (a b) -> p a b", a=2),
                      ACT.Copy).then_inc(pq_ready.sem, 1)
                for n in range(8):
                    act.wait_ge(s_mm.sem, s_mm.at(layer, n + 1))
                    f(scores[:, n // 4, (n % 4) * 4:(n % 4) * 4 + 4, :],
                      ps[:, n, :].rearrange("p (a b) -> p a b", a=4), ACT.Copy).then_inc(s_ready.sem, 1)
                for t in range(TT):
                    act.wait_ge(best_ready.sem, best_ready.at(layer, t + 1))
                    f(bd[:, t, :], bd[:, t, :], ACT.Exp).then_inc(best_exp.sem, 1)
                    act.wait_ge(rtT_mm.sem, rtT_mm.at(layer, t + 1))
                    f(route[:, :, t * P:(t + 1) * P], ps[:, t, 0:3 * P].rearrange("p (a b) -> p a b", a=3),
                      ACT.Copy).then_inc(route_ready.sem, 1)
                with act.Fori(0, T // 16) as it:
                    for b in range(4):
                        act.wait_ge(g_mm.sem, g_mm.at(layer, it * 4 + (b + 1)))
                        f(G[:, :, bass.ds(it * 16 + b * 4, 4)],
                          ps[:, 4 + b, :].rearrange("p (t j) -> p j t", t=4), ACT.Copy
                          ).then_inc(g_ready.sem, 1)
                with act.Fori(0, PAIRS // 2) as it:
                    for k in range(2):
                        act.wait_ge(h_mm.sem, h_mm.at(layer, it * 2 + (k + 1)))
                        act.wait_ge(wgt_ready.sem, wgt_ready.at(layer, it * 2 + (k - 1)))
                        f(act_h[:, k, :], ps[:, k, :], ACT.Gelu).then_inc(gelu_ready.sem, 1)
                act.wait_ge(act_chain, own.n)
                act.sem_clear(act_chain)
                own.n = 0

        @block.vector
        def _(dve):
            v = nc.vector
            own = Count()
            for s in (wgt_ready, layer_done):
                dve.sem_inc(s.sem, s.start)
            dve.wait_ge(x_loaded, 16)
            dve.wait_ge(constants, 1)

            with dve.Fori(0, LAYERS) as layer:
                def norm(which):
                    for t in range(TT):
                        dve.wait_ge(rstd_ready.sem, rstd_ready.at(layer, 2 * which + t + 1))
                        v.tensor_scalar(xs[:, t, :], x[:, t, :], rstd[:, t:t + 1], None, ALU.mult
                                        ).then_inc(xs_ready.sem, 1)
                    for n in range(4):
                        t, half = n // 2, n % 2
                        dve.wait_ge(normT_mm.sem, normT_mm.at(layer, 4 * which + n + 1))
                        gain = par[:, (C_N1, C_N2)[which] + 4 * half:(C_N1, C_N2)[which] + 4 * half + 4]
                        v.tensor_tensor(hT[:, 4 * half:4 * half + 4, t * P:(t + 1) * P],
                                        ps[:, n, :].rearrange("p (a b) -> p a b", a=4),
                                        gain.unsqueeze(2).broadcast_to([P, 4, P]), ALU.mult
                                        ).then_inc(hT_ready.sem, 1)

                dve.wait_ge(par_loaded.sem, par_loaded.at(layer, 16))
                own.one(v.tensor_tensor(lam_w[:], par[:, C_LAM:C_LAM + 128].rearrange("p (a b) -> p a b", a=2),
                                          par[:, C_LAM + 128:C_LAM + 256].rearrange("p (a b) -> p a b", a=2),
                                          ALU.mult).then_inc(dve_chain, 1))
                dve.wait_ge(dve_chain, own.n)
                v.tensor_reduce(lam[:, 0:2], lam_w[:], AX.X, ALU.add).then_inc(lam_sum.sem, 1)
                norm(0)
                dve.wait_ge(lam_exp.sem, lam_exp.at(layer, 1))
                own.one(v.tensor_tensor(lam[:, 4:5], lam[:, 2:3], lam[:, 3:4], ALU.subtract).then_inc(dve_chain, 1))
                dve.wait_ge(dve_chain, own.n)
                own.one(v.tensor_scalar(lam[:, 5:6], lam[:, 4:5], par[:, C_LAMI:C_LAMI + 1], -1.0,
                                          ALU.add, ALU.mult).then_inc(dve_chain, 1))

                def head_sums(i):
                    dve.wait_ge(sq_ready.sem, sq_ready.at(layer, i + 1))
                    v.tensor_reduce(qk_ss[:, i, :], sq[:, i, :].rearrange("p (h d) -> p h d", h=8), AX.X, ALU.add
                                    ).then_inc(ss_ready.sem, 1)

                evacuated = [1, 2, 3, 4, 7, 8, 9, 10]

                def head_norm(i):
                    ten, t = i // 2, i % 2
                    z = tok[:, ten, t, :].rearrange("p (h d) -> p h d", h=8)
                    dve.wait_ge(qkrs_ready.sem, qkrs_ready.at(layer, i + 1))
                    dve.wait_ge(proj_ev.sem, proj_ev.at(layer, evacuated[i]))
                    own.one(v.tensor_tensor(z, z, qk_rs[:, i, :].unsqueeze(2).broadcast_to([P, 8, HD]), ALU.mult).then_inc(dve_chain, 1))
                    dve.wait_ge(dve_chain, own.n)
                    gain = par[:, C_GAIN + HD * ten:C_GAIN + HD * (ten + 1)]
                    last = v.tensor_tensor(z, z, gain.unsqueeze(1).broadcast_to([P, 8, HD]), ALU.mult)
                    if ten < 2:
                        own.one(last.then_inc(dve_chain, 1))
                        dve.wait_ge(dve_chain, own.n)
                        pair = tok[:, ten, t, :].rearrange("p (h d) -> p h d", h=8)[:, :, 0:16].rearrange(
                            "p h (a d) -> p h a d", a=2)
                        if i:
                            dve.wait_ge(qk_normed.sem, qk_normed.at(layer, i))
                        for j, col in enumerate((C_COS, C_SIN)):
                            tab = par[:, col + 8 * t:col + 8 * t + 8]
                            own.one(v.tensor_tensor(rope_t[:, j, :, :].rearrange("p h (a d) -> p h a d", a=2), pair,
                                                      tab.unsqueeze(1).unsqueeze(1).broadcast_to([P, 8, 2, 8]),
                                                      ALU.mult).then_inc(dve_chain, 1))
                        dve.wait_ge(dve_chain, own.n)
                        v.tensor_tensor(z[:, :, 0:8], rope_t[:, 0, :, 0:8], rope_t[:, 1, :, 8:16], ALU.subtract)
                        last = v.tensor_tensor(z[:, :, 8:16], rope_t[:, 0, :, 8:16], rope_t[:, 1, :, 0:8], ALU.add)
                    last.then_inc(qk_normed.sem, 1)

                head_sums(0)
                for i in range(1, 8):
                    head_sums(i)
                    head_norm(i - 1)
                head_norm(7)

                for i in range(2):
                    part = slice(3 * i, 3 * i + 3)
                    dve.wait_ge(logs_ready.sem, logs_ready.at(layer, i + 1))
                    own.one(v.tensor_scalar(ctmp[:], cz[:, part, :], 0.0, None, ALU.max).then_inc(dve_chain, 1))
                    dve.wait_ge(dve_chain, own.n)
                    flat = ce[:, part, :].rearrange("p a b -> p (a b)")
                    zflat = cz[:, part, :].rearrange("p a b -> p (a b)")
                    own.one(v.scalar_tensor_tensor(out=flat, in0=ctmp[:].rearrange("p a b -> p (a b)"), scalar=-1.0,
                                                     in1=flat, op0=ALU.mult, op1=ALU.subtract).then_inc(dve_chain, 1))
                    dve.wait_ge(dve_chain, own.n)
                    own.one(v.tensor_tensor(zflat, zflat, flat, ALU.add).then_inc(dve_chain, 1))
                    dve.wait_ge(dve_chain, own.n)
                    if i == 0:
                        blocks = ce[:, 0:2, :].rearrange("p a (h q) -> p (a h) q", q=P)
                        v.tensor_tensor(blocks, blocks, strict[:].unsqueeze(1).broadcast_to([P, 8, P]), ALU.mult)
                        blocks = ce[:, 2, :].rearrange("p (h q) -> p h q", q=T)[:, :, 0:P]
                        last = v.tensor_tensor(blocks, blocks, strict[:].unsqueeze(1).broadcast_to([P, 2, P]),
                                               ALU.mult)
                    else:
                        blocks = ce[:, 3:6, :].rearrange("p a (h q) -> p (a h) q", q=T)[:, :, 0:P]
                        last = v.tensor_tensor(blocks, blocks, strict[:].unsqueeze(1).broadcast_to([P, 6, P]),
                                               ALU.mult)
                    last.then_inc(keep_ready.sem, 1)
                dve.wait_ge(dve_chain, own.n)
                for c in range(6):
                    dve.wait_ge(later_mm.sem, later_mm.at(layer, c + 1))
                    v.tensor_tensor(cz[:, c, :], cz[:, c, :], ps[:, 4 + c % 2, :], ALU.add
                                    ).then_inc(loga_ready.sem, 1)
                for c in range(6):
                    dve.wait_ge(a_exp.sem, a_exp.at(layer, c + 1))
                    n = P if c < 2 else T
                    blocks = cz[:, c, :].rearrange("p (h q) -> p h q", q=n)[:, :, 0:P]
                    v.tensor_tensor(blocks, blocks, strict[:].unsqueeze(1).broadcast_to([P, 512 // n, P]), ALU.mult
                                    ).then_inc(a_ready.sem, 1)

                dve.wait_ge(bias_ready.sem, bias_ready.at(layer, 1))
                dve.sem_inc(seen_dve, 1)

                def score_max(i):
                    t, ch = by_head(i)
                    n, off = (t + 1) * P, (1 - t) * P
                    s = sring[:, i % 3, :, 0:n]
                    if i >= 3:
                        dve.wait_ge(probT_mm.sem, probT_mm.at(layer, i - 2))
                    dve.wait_ge(score_mm.sem, score_mm.at(layer, i + 1))
                    add = (blockmask[:, off:off + n].unsqueeze(1).broadcast_to([P, 2, n]) if i < 8
                           else bias[:, 2 * ch:2 * ch + 2, off:off + n])
                    own.one(v.scalar_tensor_tensor(out=s, in0=ps[:, SCORE_BANK[i % 2]:SCORE_BANK[i % 2] + 2, 0:n],
                                                     scalar=SCALE, in1=add, op0=ALU.mult, op1=ALU.add).then_inc(dve_chain, 1))
                    dve.wait_ge(dve_chain, own.n)
                    v.tensor_reduce(nmax[:, i, :], s, AX.X, ALU.max, negate=True).then_inc(smax_ready.sem, 1)

                def probabilities(i):
                    t, _ = by_head(i)
                    s = [sring[:, i % 3, c, 0:(t + 1) * P] for c in range(2)]
                    dve.wait_ge(exp_ready.sem, exp_ready.at(layer, i + 1))
                    own.one(v.reciprocal(rinv[:, i, :], rsum[:, i, :]).then_inc(dve_chain, 1))
                    dve.wait_ge(dve_chain, own.n)
                    if i < 8:
                        own.one(v.tensor_scalar(rinv[:, i, 1:2], rinv[:, i, 1:2], lam[:, 5:6], None, ALU.mult).then_inc(dve_chain, 1))
                        own.one(v.tensor_scalar(s[0], s[0], rinv[:, i, 0:1], None, ALU.mult).then_inc(dve_chain, 1))
                        dve.wait_ge(dve_chain, own.n)
                        last = v.scalar_tensor_tensor(out=s[0], in0=s[1], scalar=rinv[:, i, 1:2], in1=s[0],
                                                      op0=ALU.mult, op1=ALU.add)
                    else:
                        v.tensor_scalar(s[0], s[0], rinv[:, i, 0:1], None, ALU.mult)
                        last = v.tensor_scalar(s[1], s[1], rinv[:, i, 1:2], None, ALU.mult)
                    last.then_inc(prob_ready.sem, 1)

                def ya_sums(t):
                    dve.wait_ge(ya_sq.sem, ya_sq.at(layer, t + 1))
                    v.tensor_reduce(ya_ss[:, t, :], ysq[:, t, :].rearrange("p (h d) -> p h d", h=4), AX.X, ALU.add
                                    ).then_inc(ya_ssr.sem, 1)

                def ya_norm(t):
                    dve.wait_ge(ya_rsr.sem, ya_rsr.at(layer, t + 1))
                    v.tensor_tensor(yan[:, t, :].rearrange("p (h d) -> p h d", h=4),
                                    ps[:, t, :].rearrange("p (h d) -> p h d", h=4),
                                    ya_rs[:, t, :].unsqueeze(2).broadcast_to([P, 4, P]), ALU.mult
                                    ).then_inc(ya_normed.sem, 1)

                score_max(0)
                score_max(1)
                for i in range(16):
                    probabilities(i)
                    if i + 2 < 16:
                        score_max(i + 2)
                    if i in (5, 9):
                        ya_sums((i - 5) // 4)
                    if i in (6, 10):
                        ya_norm((i - 6) // 4)
                for t in range(TT):
                    dve.wait_ge(yaT_mm.sem, yaT_mm.at(layer, t + 1))
                    v.tensor_scalar(yT[:, 0, :, t * P:(t + 1) * P], ps[:, 4 + t, :].rearrange("p (a b) -> p a b", a=4),
                                    par[:, C_SUB:C_SUB + 1], par[:, C_OML:C_OML + 1], ALU.mult, ALU.mult
                                    ).then_inc(ya_ready.sem, 1)

                for u in range(12):
                    d0 = ((u // 2) % 2) * 4 + (u % 2) * 2
                    b = u // 4
                    if u % 4 == 0:
                        dve.wait_ge(gate_ready.sem, gate_ready.at(layer, b + 1))
                    dve.wait_ge(up_mm.sem, up_mm.at(layer, u + 1))
                    dst = merged[:, d0:d0 + 2, :] if b == 0 else upt[:, u % 2, :].rearrange("p (a b) -> p a b", a=2)
                    v.tensor_tensor(dst, ps[:, u % 4, :].rearrange("p (a b) -> p a b", a=2),
                                    gates[:, 8 * b + d0:8 * b + d0 + 2, :], ALU.mult).then_inc(up_taken.sem, 1)
                    if b:
                        dve.wait_ge(up_taken.sem, up_taken.at(layer, u + 1))
                        dve.wait_ge(dve_chain, own.n)
                        last = v.tensor_tensor(merged[:, d0:d0 + 2, :], merged[:, d0:d0 + 2, :], dst, ALU.add)
                        if u < 11:
                            own.one(last.then_inc(dve_chain, 1))
                last.then_inc(merged_ready.sem, 1)
                for n in range(4):
                    c, t = n // 2, n % 2
                    dve.wait_ge(wout_mm.sem, wout_mm.at(layer, n + 1))
                    v.tensor_tensor(x[:, t, c * 512:(c + 1) * 512], x[:, t, c * 512:(c + 1) * 512],
                                    ps[:, 4 + n, :], ALU.add).then_inc(x_mid.sem, 1)
                norm(1)

                def top(values, best, where_):
                    for r, vals_ in enumerate(values):
                        own.one(v.max(best[r][:, 0:8], vals_).then_inc(dve_chain, 1))
                    dve.wait_ge(dve_chain, own.n)
                    for r, vals_ in enumerate(values):
                        own.one(v.max_index(where_[r][:, 0:8], best[r][:, 0:8], vals_).then_inc(dve_chain, 1))
                    dve.wait_ge(dve_chain, own.n)
                    for r, vals_ in enumerate(values):
                        own.one(v.match_replace(vals_, best[r][:, 0:8], vals_, -3.0e38).then_inc(dve_chain, 1))
                    dve.wait_ge(dve_chain, own.n)
                    for r, vals_ in enumerate(values):
                        own.one(v.max(best[r][:, 8:16], vals_).then_inc(dve_chain, 1))
                    dve.wait_ge(dve_chain, own.n)
                    for r, vals_ in enumerate(values):
                        own.one(v.max_index(where_[r][:, 8:16], best[r][:, 8:16], vals_).then_inc(dve_chain, 1))
                    dve.wait_ge(dve_chain, own.n)

                for t in range(TT):
                    dve.wait_ge(s_ready.sem, s_ready.at(layer, 4 * (t + 1)))
                    dve.sem_inc(seen_dve, 1)
                    top([scores[:, t, ch, :] for ch in range(16)], [topv[:, t, ch, :] for ch in range(16)],
                        [topi[:, t, ch, :] for ch in range(16)])
                    halves = topv[:, t, :, :].rearrange("p (h s) k -> p h s k", s=2)
                    own.one(v.tensor_copy(topf[:, t, :, :], topi[:, t, :, :]).then_inc(dve_chain, 1))
                    own.one(v.tensor_tensor(cand[:], halves[:, :, 0, :].unsqueeze(3).broadcast_to([P, 8, 16, 16]),
                                              halves[:, :, 1, :].unsqueeze(2).broadcast_to([P, 8, 16, 16]), ALU.add).then_inc(dve_chain, 1))
                    dve.wait_ge(dve_chain, own.n)
                    top([cand[:, h, :, :].rearrange("p a b -> p (a b)") for h in range(8)],
                        [bestv[:, t, h, :] for h in range(8)], [bestp[:, t, h, :] for h in range(8)])
                    v.tensor_tensor(bd[:, t, :].rearrange("p (h k) -> p h k", h=8), bestv[:, t, :, :],
                                    bestv[:, t, :, 0:1].broadcast_to([P, 8, 16]), ALU.subtract
                                    ).then_inc(best_ready.sem, 1)
                    own.one(v.tensor_scalar(pab[:, 0, :, :], bestp[:, t, :, :], 4, None, ALU.logical_shift_right).then_inc(dve_chain, 1))
                    own.one(v.tensor_scalar(pab[:, 1, :, :], bestp[:, t, :, :], 15, None, ALU.bitwise_and).then_inc(dve_chain, 1))
                    dve.wait_ge(dve_chain, own.n)
                    own.one(v.tensor_copy(pabf[:], pab[:]).then_inc(dve_chain, 1))
                    dve.wait_ge(dve_chain, own.n)
                    keys = topf[:, t, :, :].rearrange("p (h s) k -> p h s k", s=2)
                    for s, e in ((0, eq), (1, eq2)):
                        own.one(v.tensor_tensor(e[:], pabf[:, s, :, :].unsqueeze(3).broadcast_to([P, 8, 16, 16]),
                                                  iota[:, 0:16].unsqueeze(1).unsqueeze(1).broadcast_to([P, 8, 16, 16]),
                                                  ALU.is_equal).then_inc(dve_chain, 1))
                    dve.wait_ge(dve_chain, own.n)
                    for s, e in ((0, eq), (1, eq2)):
                        own.one(v.tensor_tensor(e[:], e[:], keys[:, :, s, :].unsqueeze(2).broadcast_to([P, 8, 16, 16]),
                                                  ALU.mult).then_inc(dve_chain, 1))
                    dve.wait_ge(dve_chain, own.n)
                    for s, e in ((0, eq), (1, eq2)):
                        own.one(v.tensor_reduce(rt_tok[:, t, s, :].rearrange("p (h k) -> p h k", h=8), e[:], AX.X,
                                                  ALU.add).then_inc(dve_chain, 1))
                    dve.wait_ge(best_exp.sem, best_exp.at(layer, t + 1))
                    if t:
                        dve.wait_ge(rt_ready.sem, rt_ready.at(layer, t))
                    own.one(v.tensor_reduce(gsum[:], bd[:, t, :].rearrange("p (h k) -> p h k", h=8), AX.X, ALU.add).then_inc(dve_chain, 1))
                    dve.wait_ge(dve_chain, own.n)
                    own.one(v.reciprocal(ginv[:], gsum[:]).then_inc(dve_chain, 1))
                    dve.wait_ge(dve_chain, own.n)
                    v.tensor_tensor(rt_tok[:, t, 2, :].rearrange("p (h k) -> p h k", h=8),
                                    bd[:, t, :].rearrange("p (h k) -> p h k", h=8),
                                    ginv[:].unsqueeze(2).broadcast_to([P, 8, 16]), ALU.mult
                                    ).then_inc(rt_ready.sem, 1)

                dve.wait_ge(route_ready.sem, route_ready.at(layer, 2))
                dve.sem_inc(seen_dve, 1)
                with dve.Fori(0, T // 16) as it:
                    for b in range(4):
                        dve.wait_ge(g_mm.sem, g_mm.at(layer, it * 4 + (b - 1)))
                        dve.sem_inc(seen_dve, 1)
                        for q in range(4):
                            tk = bass.ds(it * 16 + (b * 4 + q), 1)
                            v.tensor_scalar(hot_i[:, b % 2, q, :], iota[:], route[:, 0, tk], route[:, 2, tk],
                                            ALU.is_equal, ALU.mult)
                            last = v.tensor_scalar(hot_j[:, b % 2, q, :], iota[:], route[:, 1, tk], None,
                                                   ALU.is_equal)
                        last.then_inc(hot_ready.sem, 1)

                dve.wait_ge(g_ready.sem, g_ready.at(layer, 64))
                dve.sem_inc(seen_dve, 1)
                with dve.Fori(0, PAIRS // 2) as it:
                    for k in range(2):
                        dve.wait_ge(gelu_ready.sem, gelu_ready.at(layer, it * 2 + (k + 1)))
                        dve.wait_ge(v_mm.sem, v_mm.at(layer, it * 2 + (k - 1)))
                        v.tensor_tensor(wgt[:, k, :].rearrange("p (a b) -> p a b", a=2),
                                        act_h[:, k, :].rearrange("p (a b) -> p a b", a=2),
                                        G[:, bass.ds(it * 4 + 2 * k, 2), :], ALU.mult).then_inc(wgt_ready.sem, 1)
                dve.wait_ge(v_mm.sem, v_mm.at(layer, PAIRS))
                for t in range(TT):
                    last = v.tensor_tensor(x[:, t, :].rearrange("p (a b) -> p a b", a=2),
                                           x[:, t, :].rearrange("p (a b) -> p a b", a=2),
                                           ps[:, 4 + 2 * t:6 + 2 * t, :], ALU.add)
                last.then_inc(layer_done.sem, 1)
                dve.wait_ge(dve_chain, own.n)
                dve.sem_clear(dve_chain)
                own.n = 0


def kernel(x, norm1_g, w_in, a_qnorm_g, a_knorm_g, lam_q1, lam_k1, lam_q2, lam_k2, a_subln_g, b_qnorm_g,
           b_knorm_g, b_rel_bias, w_branch, w_out, norm2_g, peer_wq, peer_subkeys, peer_u, peer_v):
    import concourse.bacc as bacc
    from concourse.bass_utils import run_bass_kernel_spmd

    L = LAYERS
    f32 = np.float32

    def arr(a):
        return np.asarray(a)

    def two_halves(w, blocks):
        return w.reshape(L, 2, 4, P, blocks, 512).transpose(0, 4, 1, 3, 2, 5).reshape(L, 2 * blocks, P, SLOT)

    def columns(w):
        n = w.shape[-1] // 256
        return w.reshape(L, KC, P, n, 256).transpose(0, 3, 2, 1, 4).reshape(L, n, P, SLOT)

    w_in, w_br = arr(w_in), arr(w_branch)
    stream = np.concatenate([
        two_halves(w_in[:, :, :9 * 512], 9),
        columns(w_in[:, :, 9 * 512:]),
        w_br.reshape(L, 3, 4, P, 2, 512).transpose(0, 1, 4, 3, 2, 5).reshape(L, N_BR, P, SLOT),
        two_halves(arr(w_out), 2),
        columns(arr(peer_wq)),
    ], axis=1).reshape(L * N_STREAM, P, SLOT)
    w_u = arr(peer_u).reshape(L, P, PAIRS, 2, KC, P).transpose(0, 2, 5, 3, 4, 1).reshape(L * PAIRS, P, SLOT)
    w_v = arr(peer_v).reshape(L, P, PAIRS, SLOT)
    subk = arr(peer_subkeys).transpose(0, 4, 2, 1, 3).reshape(L, P, 16 * P)

    def everywhere(a):
        return np.broadcast_to(a[:, None, :], (L, P, a.shape[-1]))

    lam_init = np.array([0.8 - 0.6 * math.exp(-0.3 * i) for i in range(L)])
    half = HD // 8
    inv = 1.0 / (f32(500000.0) ** (np.arange(0, 2 * half, 2, dtype=f32) / f32(2 * half)))
    ang = np.arange(T, dtype=f32)[:, None] * inv[None, :].astype(f32)

    def table(a):
        return np.broadcast_to(a.astype(f32).reshape(TT, P, 8).transpose(1, 0, 2).reshape(1, P, 16), (L, P, 16))

    params = np.concatenate([
        arr(norm1_g).reshape(L, KC, P).transpose(0, 2, 1),
        arr(norm2_g).reshape(L, KC, P).transpose(0, 2, 1),
        arr(a_subln_g).reshape(L, P, 1),
        np.broadcast_to(lam_init.astype(f32)[:, None, None], (L, P, 1)),
        np.broadcast_to((1.0 - lam_init).astype(f32)[:, None, None], (L, P, 1)),
        table(np.cos(ang)), table(np.sin(ang)),
        *[everywhere(arr(a)) for a in (a_qnorm_g, a_knorm_g, b_qnorm_g, b_knorm_g, lam_q1, lam_q2, lam_k1, lam_k2)],
    ], axis=2)
    distance = np.clip(np.arange(P)[:, None] - np.arange(2 * P)[None, :] + P, -REL, REL) + REL
    arrays = {
        "x": arr(x).reshape(TT, P, D).transpose(1, 0, 2), "stream": stream, "w_u": w_u, "w_v": w_v, "subk": subk,
        "params": params, "bias": arr(b_rel_bias)[:, :, distance].transpose(0, 2, 1, 3).reshape(L, P, B_HEADS * 2 * P),
    }
    arrays = {f"in_{k}": np.ascontiguousarray(a) for k, a in arrays.items()}

    nc = bacc.Bacc("TRN2", target_bir_lowering=False, num_devices=1)
    args = [nc.dram_tensor(k, a.shape, mybir.dt.from_np(a.dtype), kind="ExternalInput").ap()
            for k, a in arrays.items()]
    out = nc.dram_tensor("out_0", (P, TT, D), mybir.dt.float32, kind="ExternalOutput").ap()
    build(nc, *args, out)
    r = run_bass_kernel_spmd(nc, [arrays], core_ids=[0])
    return r.results[0]["out_0"].transpose(1, 0, 2).reshape(1, T, D)
```

```python
import math
from contextlib import ExitStack

import numpy as np
import concourse.bass as bass
from concourse import mybir

D, T, LAYERS = 1024, 256, 2
P = 128
TT = T // P
KC = D // P
HD = 64
A_HEADS, B_HEADS, C_HEADS = 4, 8, 8
PEER_HEADS, KEYS, TOPK = 8, 128, 16
REL = 128
SLOTS, SLOT = 4, 1024
N_QKV, N_GATE, N_BR, N_OUT, N_WQ = 36, 24, 12, 8, 16
N_STREAM = N_QKV + N_GATE + N_BR + N_OUT + N_WQ
PAIRS = KEYS // 2
EARLY = 20
LATE = PAIRS - EARLY
N_EARLY = 2 * EARLY
N_LAYER = N_STREAM + 4 * PAIRS
N_DVE = N_LAYER - N_EARLY
N_V = N_STREAM + 4 * LATE
ROUNDS = N_LAYER // SLOTS
N_USED = 27 + 12 + 6 + 8
UP_ORDER = (2, 1, 0)
EPS = 1e-6
SCALE = HD ** -0.5
NEG = -1e30

C_N1, C_N2, C_SUB, C_LAMI, C_OML, C_COS, C_SIN = 0, 8, 16, 17, 18, 19, 35
C_GAIN, C_LAM = 51, 307
N_PAR = 563

TOK, VV, QKT, GATE, YT, MRG, BIAS, SCR = 0, 6144, 9216, 15360, 21504, 24576, 26624, 28672
ROPE, LAMW, PAR, MASKS = MRG, MRG + 256, SCR + 3072, SCR + 3072 + 608
SRING, PTR, YSQ, YAN, UPT = 0, 1536, 2560, 3584, 4608
PQT, SSB, CAND, EQ, TOPV, TOPI, TOPF, BV, BP, PAB, PABF, BEST_D = (
    0, 4096, 9216, 11264, 13312, 13824, 14336, 14848, 15104, 15360, 15872, 16384)
EQ2 = 16896


class Signal:

    def __init__(self, sem, per_layer, start=0):
        self.sem, self.per_layer, self.start = sem, per_layer, start

    def at(self, layer, n):
        return layer * self.per_layer + (self.start + n)


class Count:

    def __init__(self):
        self.n = 0

    def one(self, ins):
        self.n += 1


def build(nc, x_in, stream, w_u, w_v, subk, params, bias_in, out):
    F = mybir.dt.float32
    FR = mybir.dt.float32r
    U32 = mybir.dt.uint32
    ALU = mybir.AluOpType
    ACT = mybir.ActivationFunctionType
    AX = mybir.AxisListType
    ctx = ExitStack()
    with ctx:
        def sb(name, shape, dt=F):
            return ctx.enter_context(nc.sbuf_tensor(name, shape, dt))

        def sem(name):
            return ctx.enter_context(nc.semaphore(name))

        def overlay(*tensors):
            with ExitStack() as region:
                return [region.enter_context(nc.sbuf_tensor(n, shape, dt)) for n, shape, dt in tensors]

        ident = sb("ident", [P, P])
        iota = sb("iota", [P, P])
        blockmask = sb("blockmask", [P, 2 * P])
        half_neg = sb("half_neg", [P, 8])
        ssq = sb("ssq", [P, 2])
        rstd = sb("rstd", [P, 2])
        qk_ss = sb("qk_ss", [P, 8, 8])
        qk_rs = sb("qk_rs", [P, 8, 8])
        ya_ss = sb("ya_ss", [P, 2, 4])
        ya_rs = sb("ya_rs", [P, 2, 4])
        lam = sb("lam", [P, 8])
        gsum = sb("gsum", [P, 8])
        ginv = sb("ginv", [P, 8])
        raw = sb("raw", [P, SLOTS, SLOT])
        w_hi = sb("w_hi", [P, SLOTS, SLOT], FR)
        w_lo = sb("w_lo", [P, SLOTS, SLOT], FR)
        hT_hi = sb("hT_hi", [P, KC, T], FR)
        hT_lo = sb("hT_lo", [P, KC, T], FR)
        g_part_b = sb("g_part_b", [P, 2 * EARLY, 4])
        hot_i, hot_j = overlay(("hot_i", [P, 2, 4, P], F), ("hot_j", [P, 2, 4, P], F))
        wgt_hi, wgt_lo = overlay(("wgt_hi", [P, 2, 512], FR), ("wgt_lo", [P, 2, 512], FR))
        x = sb("x", [P, TT, D])
        route, g_part_a = overlay(("route", [P, 3, T], F), ("g_part_a", [P, 2 * EARLY, 4], F))
        act_h = sb("act_h", [P, 2, 512])
        _, m_hi, m_lo = overlay(("at_tok", [P, TOK + 8], F), ("m_hi", [P, KC, T], FR), ("m_lo", [P, KC, T], FR))
        _, y_hi, y_lo = overlay(("at_qkt", [P, QKT], F), ("y_hi", [P, 3, 4, T], FR), ("y_lo", [P, 3, 4, T], FR))
        arena = sb("arena", [P, KEYS * T])
        ps = ctx.enter_context(nc.psum_tensor("ps", [P, 8, 512], F))

        def view(off, *shape):
            n = int(np.prod(shape))
            v = arena[:, off:off + n]
            names = "abcd"[:len(shape)]
            if len(shape) == 1:
                return v
            spec = f"p ({' '.join(names)}) -> p {' '.join(names)}"
            return v.rearrange(spec, **dict(zip(names, shape)))

        tok = view(TOK, 6, TT, 512)
        vals = view(VV, 3, TT, 512)
        qkT = view(QKT, 6, 4, T)
        gates = view(GATE, 24, T)
        yT = view(YT, 3, 4, T)
        merged = view(MRG, KC, T)
        xs = view(MRG, TT, D)
        bias = view(BIAS, B_HEADS, T)
        subT = view(BIAS, 16, P)
        sq = view(QKT, 8, 512)
        nsq = view(SCR, TT, D)
        cz = view(SCR, 6, 512)
        ctmp = view(TOK + 4096, 3, 512)
        ce = view(YT, 6, 512)
        sring = view(SRING, 3, 2, 256)
        ptr = view(PTR, 2, 512)
        ysq = view(YSQ, 2, 512)
        yan = view(YAN, 2, 512)
        upt = view(UPT, 2, 512)
        pqT = view(PQT, 16, T)
        scores = view(SSB, TT, 16, P)
        cand = view(CAND, 8, 16, 16)
        eq = view(EQ, 8, 16, 16)
        eq2 = view(EQ2, 8, 16, 16)
        topv = view(TOPV, TT, 16, 16)
        topi = view(TOPI, TT, 16, 16).bitcast(U32)
        topf = view(TOPF, TT, 16, 16)
        bestv = view(BV, TT, 8, 16)
        bestp = view(BP, TT, 8, 16).bitcast(U32)
        pab = view(PAB, 2, 8, 16).bitcast(U32)
        pabf = view(PABF, 2, 8, 16)
        bd = view(BEST_D, TT, 128)
        rt_tok = view(EQ2 + 2048, TT, 3, P)
        G = view(0, KEYS, T)
        htmp = view(TOK, 4, 512)
        par = view(PAR, N_PAR)
        strict, below, ones = (view(MASKS + P * k, P) for k in range(3))
        rope_t = view(ROPE, 2, 8, 16)
        lam_w = view(LAMW, 2, HD)
        nmax, rsum, rinv = (view(MRG + 384 + 32 * k, 16, 2) for k in range(3))

        x_loaded = sem("x_loaded")
        w_loaded = [Signal(sem(f"w_loaded{s}"), ROUNDS * 16) for s in range(SLOTS)]
        hi_ready = Signal(sem("hi_ready"), N_LAYER, SLOTS)
        w_ready = Signal(sem("w_ready"), N_DVE, SLOTS)
        early_ready = Signal(sem("early_ready"), N_EARLY)
        early_mm = Signal(sem("early_mm"), EARLY)
        early_gelu = Signal(sem("early_gelu"), EARLY, 2)
        part_ready = Signal(sem("part_ready"), 64)
        part_used = Signal(sem("part_used"), 64, 2)
        w_used = Signal(sem("w_used"), N_USED)
        masks_ready = Signal(sem("masks_ready"), 1)
        y_split = Signal(sem("y_split"), 3)
        x_parked = Signal(sem("x_parked"), 1)
        par_loaded = Signal(sem("par_loaded"), 16)
        bias_loaded = Signal(sem("bias_loaded"), 16)
        subk_loaded = Signal(sem("subk_loaded"), 16)
        constants = sem("constants")
        layer_done = Signal(sem("layer_done"), 1, 1)
        squared = Signal(sem("squared"), 4)
        rstd_ready = Signal(sem("rstd_ready"), 4)
        xs_ready = Signal(sem("xs_ready"), 4)
        normT_mm = Signal(sem("normT_mm"), 8)
        hT_ready = Signal(sem("hT_ready"), 8)
        proj_mm = Signal(sem("proj_mm"), 48)
        proj_ev = Signal(sem("proj_ev"), 48)
        sq_ready = Signal(sem("sq_ready"), 8)
        ss_ready = Signal(sem("ss_ready"), 8)
        qkrs_ready = Signal(sem("qkrs_ready"), 8)
        qk_normed = Signal(sem("qk_normed"), 8)
        logs_ready = Signal(sem("logs_ready"), 2)
        keep_ready = Signal(sem("keep_ready"), 2)
        later_mm = Signal(sem("later_mm"), 6)
        loga_ready = Signal(sem("loga_ready"), 6)
        a_exp = Signal(sem("a_exp"), 6)
        a_ready = Signal(sem("a_ready"), 6)
        cout_mm = Signal(sem("cout_mm"), 2)
        yc_ready = Signal(sem("yc_ready"), 2)
        score_mm = Signal(sem("score_mm"), 16)
        smax_ready = Signal(sem("smax_ready"), 16)
        exp_ready = Signal(sem("exp_ready"), 16)
        prob_ready = Signal(sem("prob_ready"), 16)
        probT_mm = Signal(sem("probT_mm"), 16)
        probT_ready = Signal(sem("probT_ready"), 16)
        mix_mm = Signal(sem("mix_mm"), 16)
        ya_sq = Signal(sem("ya_sq"), 2)
        ya_ssr = Signal(sem("ya_ssr"), 2)
        ya_rsr = Signal(sem("ya_rsr"), 2)
        ya_normed = Signal(sem("ya_normed"), 2)
        yaT_mm = Signal(sem("yaT_mm"), 2)
        ya_ready = Signal(sem("ya_ready"), 2)
        yb_ready = Signal(sem("yb_ready"), 2)
        lam_sum = Signal(sem("lam_sum"), 1)
        lam_exp = Signal(sem("lam_exp"), 1)
        bias_ready = Signal(sem("bias_ready"), 1)
        gate_ready = Signal(sem("gate_ready"), 3)
        up_mm = Signal(sem("up_mm"), 12)
        up_taken = Signal(sem("up_taken"), 12)
        merged_ready = Signal(sem("merged_ready"), 4)
        wout_mm = Signal(sem("wout_mm"), 4)
        x_mid = Signal(sem("x_mid"), 4)
        pq_mm = Signal(sem("pq_mm"), 8)
        pq_ready = Signal(sem("pq_ready"), 8)
        s_mm = Signal(sem("s_mm"), 8)
        s_ready = Signal(sem("s_ready"), 8)
        best_ready = Signal(sem("best_ready"), 2)
        best_exp = Signal(sem("best_exp"), 2)
        rt_ready = Signal(sem("rt_ready"), 2)
        rtT_mm = Signal(sem("rtT_mm"), 2)
        route_ready = Signal(sem("route_ready"), 2)
        hot_ready = Signal(sem("hot_ready"), 64)
        g_mm = Signal(sem("g_mm"), 64, 2)
        g_ready = Signal(sem("g_ready"), 64, 4)
        h_mm = Signal(sem("h_mm"), LATE, 2)
        gelu_ready = Signal(sem("gelu_ready"), LATE, 2)
        wgt_ready = Signal(sem("wgt_ready"), PAIRS, 2)
        v_mm = Signal(sem("v_mm"), PAIRS, 2)
        dve_chain, act_chain, pool_chain = sem("dve_chain"), sem("act_chain"), sem("pool_chain")
        dve_loop = sem("dve_loop")
        seen_sp, seen_dve, seen_pool, seen_pe = sem("seen_sp"), sem("seen_dve"), sem("seen_pool"), sem("seen_pe")
        stored = sem("stored")

        M_CT, M_G0, M_CZ, M_G4, M_G8, M_ABT = 18, 22, 26, 32, 36, 40

        def proj_bank(m):
            return m % 8 if m < 18 else (m - 18) % 4

        def gate_m(g):
            return (M_G0, M_G4, M_G8)[g // 4] + g % 4

        def used(n):
            if n < N_QKV:
                cb, k = n // 4, n % 4
                return (proj_mm, 2 * cb + 2) if k == 3 else (w_used, 3 * cb + k + 1)
            n -= N_QKV
            if n < N_GATE:
                return (proj_mm, gate_m(n // 2) + 1) if n % 2 else (w_used, 27 + n // 2 + 1)
            n -= N_GATE
            if n < N_BR:
                return up_mm, n + 1
            n -= N_BR
            if n < N_OUT:
                return (wout_mm, 2 * (n // 4) + 2) if n % 4 == 3 else (w_used, 39 + 3 * (n // 4) + n % 4 + 1)
            n -= N_OUT
            return (pq_mm, n // 2 + 1) if n % 2 else (w_used, 45 + n // 2 + 1)

        SCORE_BANK = (2, 6)

        def by_head(i):
            return (i % 8) // 4, i % 4

        def c_heads(c):
            if c < 2:
                return 1, c, [c + 2 * j for j in range(4)]
            par_, g = (c - 2) % 2, (c - 2) // 2
            return 0, par_, [par_ + 4 * g, par_ + 4 * g + 2]

        block = ctx.enter_context(nc.Block())

        @block.sync
        def _(sp):
            sp.dma_start(x[:], x_in).then_inc(x_loaded, 16)

            def load(layer, n, slot, source, early=False):
                if early:
                    sp.wait_ge(early_ready.sem, early_ready.at(layer, n))
                else:
                    sp.wait_ge(w_ready.sem, w_ready.at(layer, n))
                sp.sem_inc(seen_sp, 1)
                sp.dma_start(raw[:, slot, :], source).then_inc(w_loaded[slot].sem, 16)

            with sp.Fori(0, LAYERS) as layer:
                with sp.Fori(0, N_STREAM // SLOTS) as r:
                    for k in range(SLOTS):
                        load(layer, r * SLOTS + (k + 1 - SLOTS), k,
                             stream[bass.ds(layer * N_STREAM + (r * SLOTS + k), 1), :, :].rearrange(
                                 "a p n -> p (a n)"))

                def load_u(j, n, slot, early=False):
                    load(layer, n, slot, w_u[bass.ds(layer * KEYS + j, 1), :, :].rearrange("a p n -> p (a n)"), early)

                def load_v(j, n, slot):
                    load(layer, n, slot, w_v[bass.ds(layer, 1), :, bass.ds(j, 1), :].rearrange(
                        "a p b n -> p (a b n)"))

                for i in range(SLOTS):
                    load_u(2 * LATE + i, N_STREAM + i + 1 - SLOTS, i)
                with sp.Fori(1, N_EARLY // SLOTS) as r:
                    for i in range(SLOTS):
                        load_u(r * SLOTS + (2 * LATE + i), r * SLOTS + (i + 1 - SLOTS), i, early=True)
                for i in range(SLOTS):
                    load_u(i, N_EARLY + i + 1 - SLOTS, i, early=True)
                for e in range(2):
                    load_v(e, N_STREAM + 1 + e, e)
                with sp.Fori(1, LATE - 1) as p:
                    for e in range(2):
                        load_u(p * 2 + (2 + e), p * 4 + (N_STREAM - 1 + e), 2 + e)
                    for e in range(2):
                        load_v(p * 2 + e, p * 4 + (N_STREAM + 1 + e), e)
                for e in range(2):
                    load_v(2 * LATE - 2 + e, N_V - 5 + e, 2 + e)
                with sp.Fori(0, N_EARLY // SLOTS) as r:
                    for i in range(SLOTS):
                        load_v(r * SLOTS + (2 * LATE + i), r * SLOTS + (N_V + i + 1 - SLOTS), i)
            sp.wait_ge(layer_done.sem, layer_done.at(LAYERS, 0))
            sp.dma_start(out, x[:]).then_inc(stored, 16)
            sp.wait_ge(stored, 16)

        @block.gpsimd
        def _(pool):
            own = Count()

            def fill(t, value):
                own.one(nc.gpsimd.memset(t, value).then_inc(pool_chain, 1))

            fill(ident[:], 0.0)
            fill(blockmask[:], 0.0)
            fill(half_neg[:], -0.5)
            pool.wait_ge(pool_chain, own.n)
            own.one(nc.gpsimd.affine_select(out=ident[:], in_=ident[:], compare_op=ALU.not_equal, fill=1.0,
                                              base=0, pattern=[[-1, P]], channel_multiplier=1).then_inc(pool_chain, 1))
            own.one(nc.gpsimd.memset(blockmask[0:64, P + 64:2 * P], NEG).then_inc(pool_chain, 1))
            own.one(nc.gpsimd.iota(iota[:], pattern=[[1, P]], base=0, channel_multiplier=0,
                                     allow_small_or_imprecise_dtypes=True).then_inc(pool_chain, 1))
            pool.wait_ge(pool_chain, own.n)
            pool.sem_inc(constants, 1)
            pool.wait_ge(pool_chain, own.n)
            pool.sem_clear(pool_chain)
            own.n = 0

            pool.sem_inc(part_used.sem, part_used.start)
            with pool.Fori(0, LAYERS) as layer:
                pool.wait_ge(layer_done.sem, layer_done.at(layer, 0))
                pool.sem_inc(seen_pool, 1)
                for mask in (ones, strict, below):
                    own.one(nc.gpsimd.memset(mask, 1.0).then_inc(pool_chain, 1))
                pool.wait_ge(pool_chain, own.n)
                own.one(nc.gpsimd.affine_select(out=strict, in_=strict, compare_op=ALU.is_gt, fill=0.0, base=0,
                                                pattern=[[1, P]], channel_multiplier=-1).then_inc(pool_chain, 1))
                nc.gpsimd.affine_select(out=below, in_=below, compare_op=ALU.is_gt, fill=0.0, base=0,
                                        pattern=[[-1, P]], channel_multiplier=1).then_inc(masks_ready.sem, 1)

                def inverse_root(dst, src, count, wait_for, n, ready):
                    pool.wait_ge(wait_for.sem, wait_for.at(layer, n))
                    pool.sem_inc(seen_pool, 1)
                    own.one(nc.gpsimd.tensor_scalar(dst, src, 1.0 / count, EPS, ALU.mult, ALU.add).then_inc(pool_chain, 1))
                    pool.wait_ge(pool_chain, own.n)
                    nc.gpsimd.tensor_tensor(dst, dst, half_neg[:, 0:dst.shape[-1]], ALU.pow
                                            ).then_inc(ready.sem, 1)

                for t in range(TT):
                    inverse_root(rstd[:, t:t + 1], ssq[:, t:t + 1], D, squared, t + 1, rstd_ready)
                pool.wait_ge(bias_loaded.sem, bias_loaded.at(layer, 16))
                pool.sem_inc(seen_pool, 1)
                nc.gpsimd.tensor_tensor(bias[:], bias[:],
                                        blockmask[:].unsqueeze(1).broadcast_to([P, B_HEADS, 2 * P]),
                                        ALU.add).then_inc(bias_ready.sem, 1)
                for i in range(8):
                    inverse_root(qk_rs[:, i, :], qk_ss[:, i, :], HD, ss_ready, i + 1, qkrs_ready)
                for t in range(TT):
                    inverse_root(ya_rs[:, t, :], ya_ss[:, t, :], P, ya_ssr, t + 1, ya_rsr)
                for t in range(TT):
                    inverse_root(rstd[:, t:t + 1], ssq[:, t:t + 1], D, squared, TT + t + 1, rstd_ready)
                with pool.Fori(0, N_EARLY // SLOTS) as r:
                    for i in range(SLOTS):
                        pool.wait_ge(hi_ready.sem, hi_ready.at(layer, r * SLOTS + (N_STREAM + i + 1)))
                        pool.sem_inc(seen_pool, 1)
                        nc.gpsimd.tensor_tensor(w_lo[:, i, :], raw[:, i, :], w_hi[:, i, :].bitcast(F), ALU.subtract
                                                ).then_inc(early_ready.sem, 1)
                with pool.Fori(0, T // 16) as it:
                    for b in range(4):
                        pool.wait_ge(part_ready.sem, part_ready.at(layer, it * 4 + (b + 1)))
                        pool.sem_inc(seen_pool, 1)
                        early = G[:, 2 * LATE:KEYS, bass.ds(it * 16 + b * 4, 4)]
                        nc.gpsimd.tensor_tensor(early, early, (g_part_a, g_part_b)[b % 2][:], ALU.mult
                                                ).then_inc(part_used.sem, 1)
                pool.wait_ge(pool_chain, own.n)
                pool.sem_clear(pool_chain)
                own.n = 0

        @block.tensor
        def _(pe):
            mm = nc.tensor.matmul
            for s in (h_mm, v_mm, g_mm):
                pe.sem_inc(s.sem, s.start)

            def product(out_, left, right, start, stop, group=False):
                mm(out_, left[0], right[0], start=start, stop=False, skip_group_check=group)
                mm(out_, left[0], right[1], start=False, stop=False, skip_group_check=group)
                return mm(out_, left[1], right[0], start=False, stop=stop, skip_group_check=group)

            pe.wait_ge(constants, 1)

            def transposes(dst, src, count):
                for q in range(count):
                    last = nc.tensor.transpose(dst[:, q * P:(q + 1) * P], src[:, q * P:(q + 1) * P], ident[:])
                return last

            with pe.Fori(0, LAYERS) as layer:
                def norm_transposes(which):
                    for n in range(4):
                        t, half = n // 2, n % 2
                        if half == 0:
                            pe.wait_ge(xs_ready.sem, xs_ready.at(layer, 2 * which + t + 1))
                        transposes(ps[:, n, :], xs[:, t, half * 512:(half + 1) * 512], 4
                                   ).then_inc(normT_mm.sem, 1)

                def by_token(lhs, bank, n0, signal, first_wait, lhs_wait=lambda k: None):
                    for k in range(4):
                        pe.wait_ge(w_ready.sem, w_ready.at(layer, n0 + k + 1))
                        lhs_wait(k)
                        for t in range(TT):
                            if k == 0:
                                first_wait(t)
                            for kc in range(2):
                                last = product(ps[:, bank(t), :],
                                               [a[:, 2 * k + kc, t * P:(t + 1) * P] for a in lhs],
                                               [w[:, (n0 + k) % SLOTS, kc * 512:(kc + 1) * 512] for w in (w_hi, w_lo)],
                                               start=(k == 0 and kc == 0), stop=(k == 3 and kc == 1))
                            if k == 3:
                                last.then_inc(signal.sem, 1)
                        if k < 3:
                            last.then_inc(w_used.sem, 1)

                def by_feature(bank, n0, signal):
                    for c2 in range(2):
                        pe.wait_ge(w_ready.sem, w_ready.at(layer, n0 + c2 + 1))
                        for kc in range(KC):
                            last = product(ps[:, bank, c2 * T:(c2 + 1) * T],
                                           [w[:, (n0 + c2) % SLOTS, kc * P:(kc + 1) * P] for w in (w_hi, w_lo)],
                                           [h[:, kc, :] for h in (hT_hi, hT_lo)], start=(kc == 0), stop=(kc == KC - 1))
                        last.then_inc((w_used if c2 == 0 else signal).sem, 1)

                norm_transposes(0)
                pe.wait_ge(hT_ready.sem, hT_ready.at(layer, 4))
                for cb in range(9):
                    def bank_free(t):
                        if 2 * cb + t >= 8:
                            pe.wait_ge(proj_ev.sem, proj_ev.at(layer, 2 * cb + t - 7))
                    by_token((hT_hi, hT_lo), lambda t: proj_bank(2 * cb + t), 4 * cb, proj_mm, bank_free)

                def feature_tile(m, ten, t):
                    transposes(ps[:, proj_bank(m), :], tok[:, ten, t, :], 4).then_inc(proj_mm.sem, 1)

                for r in range(4):
                    pe.wait_ge(proj_ev.sem, proj_ev.at(layer, 18))
                    feature_tile(M_CT + r, 4 + r // 2, r % 2)

                def gate_tiles(g0):
                    for g in range(g0, g0 + 4):
                        pe.wait_ge(proj_ev.sem, proj_ev.at(layer, gate_m(g) - 3))
                        by_feature(proj_bank(gate_m(g)), N_QKV + 2 * g, proj_mm)

                gate_tiles(0)
                for c in range(6):
                    kt, par_, heads = c_heads(c)
                    pe.wait_ge(proj_ev.sem, proj_ev.at(layer, M_CZ + c - 3))
                    n = (2 - kt) * P
                    for j, h in enumerate(heads):
                        rows = slice(64 * par_, 64 * par_ + 64)
                        last = mm(ps[:, proj_bank(M_CZ + c), j * n:(j + 1) * n],
                                  qkT[rows, 5, h // 2, kt * P:(kt + 1) * P], qkT[rows, 4, h // 2, kt * P:T],
                                  start=True, stop=True)
                    last.then_inc(proj_mm.sem, 1)
                gate_tiles(4)
                pe.wait_ge(masks_ready.sem, masks_ready.at(layer, 1))
                for c in range(6):
                    kt, par_, heads = c_heads(c)
                    pe.wait_ge(keep_ready.sem, keep_ready.at(layer, 1 if c < 3 else 2))
                    if c >= 2:
                        pe.wait_ge(loga_ready.sem, loga_ready.at(layer, c - 1))
                    last = mm(ps[:, 4 + c % 2, :], below, ce[:, c, :], start=True, stop=(kt == 1))
                    if kt == 0:
                        g = (c - 2) // 2
                        last = mm(ps[:, 4 + c % 2, :].rearrange("p (h q) -> p h q", h=2)[:, :, P:T], ones,
                                  ce[:, par_, 2 * g * P:(2 * g + 2) * P].rearrange("p (h q) -> p h q", h=2),
                                  start=False, stop=True)
                    last.then_inc(later_mm.sem, 1)
                gate_tiles(8)
                for r in range(8):
                    pe.wait_ge(proj_ev.sem, proj_ev.at(layer, M_ABT + r - 3))
                    pe.wait_ge(qk_normed.sem, qk_normed.at(layer, r + 1))
                    feature_tile(M_ABT + r, r // 2, r % 2)
                pe.wait_ge(a_ready.sem, a_ready.at(layer, 6))
                for o in range(2):
                    for h in range(4 * o, 4 * o + 4):
                        par_, rows = h % 2, slice(64 * (h % 2), 64 * (h % 2) + 64)
                        at = ((h // 2) % 2) * T
                        mm(ps[rows, 4 + o, at:at + T], vals[:, 2, 0, h * HD:(h + 1) * HD],
                           cz[:, 2 + par_ + 2 * (h // 4), ((h // 2) % 2) * T:((h // 2) % 2 + 1) * T],
                           start=True, stop=False)
                        last = mm(ps[rows, 4 + o, at + P:at + T], vals[:, 2, 1, h * HD:(h + 1) * HD],
                                  cz[:, par_, (h // 2) * P:(h // 2 + 1) * P], start=False, stop=True)
                    last.then_inc(cout_mm.sem, 1)

                def score(i):
                    t, ch = by_head(i)
                    q_, k_ = (0, 1) if i < 8 else (2, 3)
                    for c in range(2):
                        rows = slice(64 * c, 64 * c + 64)
                        last = mm(ps[:, SCORE_BANK[i % 2] + c, 0:(t + 1) * P],
                                  qkT[rows, q_, ch, t * P:(t + 1) * P], qkT[rows, k_, ch, 0:(t + 1) * P],
                                  start=True, stop=True)
                    last.then_inc(score_mm.sem, 1)

                def prob_transposes(i):
                    t, _ = by_head(i)
                    pe.wait_ge(prob_ready.sem, prob_ready.at(layer, i + 1))
                    if i >= 2:
                        pe.wait_ge(probT_ready.sem, probT_ready.at(layer, i - 1))
                    elif i == 0:
                        pe.wait_ge(yc_ready.sem, yc_ready.at(layer, 2))
                    for c in range(1 if i < 8 else 2):
                        last = transposes(ps[:, 4 + i % 2, c * (t + 1) * P:(c + 1) * (t + 1) * P],
                                          sring[:, i % 3, c, :], t + 1)
                    last.then_inc(probT_mm.sem, 1)

                def mix(i):
                    t, ch = by_head(i)
                    pe.wait_ge(probT_ready.sem, probT_ready.at(layer, i + 1))
                    if i >= 8 and ch == 0:
                        pe.wait_ge(ya_normed.sem, ya_normed.at(layer, t + 1))
                    if i < 8:
                        for kt in range(t + 1):
                            last = mm(ps[:, t, ch * P:(ch + 1) * P], ptr[:, i % 2, kt * P:(kt + 1) * P],
                                      vals[:, 0, kt, ch * P:(ch + 1) * P], start=(kt == 0), stop=(kt == t))
                    else:
                        for c in range(2):
                            h = 2 * ch + c
                            for kt in range(t + 1):
                                at = (c * (t + 1) + kt) * P
                                last = mm(ps[64 * c:64 * c + 64, t, ch * P:(ch + 1) * P],
                                          vals[:, 1, kt, h * HD:(h + 1) * HD], ptr[:, i % 2, at:at + P],
                                          start=(kt == 0), stop=(kt == t))
                    last.then_inc(mix_mm.sem, 1)

                pe.wait_ge(proj_ev.sem, proj_ev.at(layer, 48))
                score(0)
                score(1)
                for i in range(16):
                    prob_transposes(i)
                    if i + 2 < 16:
                        score(i + 2)
                    if i:
                        mix(i - 1)
                mix(15)
                pe.wait_ge(probT_ready.sem, probT_ready.at(layer, 16))
                for t in range(TT):
                    pe.wait_ge(ya_normed.sem, ya_normed.at(layer, t + 1))
                    transposes(ps[:, 4 + t, :], yan[:, t, :], 4).then_inc(yaT_mm.sem, 1)

                pe.wait_ge(yb_ready.sem, yb_ready.at(layer, 2))
                for u in range(12):
                    n = N_QKV + N_GATE + u
                    if u % 4 == 0:
                        pe.wait_ge(y_split.sem, y_split.at(layer, u // 4 + 1))
                    if u >= 4:
                        pe.wait_ge(up_taken.sem, up_taken.at(layer, u - 3))
                    pe.wait_ge(w_ready.sem, w_ready.at(layer, n + 1))
                    for c2 in range(2):
                        for wc in range(4):
                            at = wc * 256 + c2 * P
                            last = product(ps[:, u % 4, c2 * T:(c2 + 1) * T],
                                           [w[:, n % SLOTS, at:at + P] for w in (w_hi, w_lo)],
                                           [y[:, UP_ORDER[u // 4], wc, :] for y in (y_hi, y_lo)],
                                           start=(wc == 0), stop=(wc == 3))
                    last.then_inc(up_mm.sem, 1)
                for c in range(2):
                    by_token((m_hi, m_lo), lambda t: 4 + 2 * c + t, N_STREAM - N_WQ - N_OUT + 4 * c, wout_mm,
                             lambda t: None,
                             lambda k: pe.wait_ge(merged_ready.sem, merged_ready.at(layer, k + 1)) if c == 0 else None)

                norm_transposes(1)
                pe.wait_ge(hT_ready.sem, hT_ready.at(layer, 8))
                for n in range(N_WQ // 2):
                    if n >= 4:
                        pe.wait_ge(pq_ready.sem, pq_ready.at(layer, n - 3))
                    by_feature(4 + n % 4, N_STREAM - N_WQ + 2 * n, pq_mm)
                pe.wait_ge(subk_loaded.sem, subk_loaded.at(layer, 16))
                pe.wait_ge(pq_ready.sem, pq_ready.at(layer, 8))
                for n in range(8):
                    for q in range(4):
                        ch = (n % 4) * 4 + q
                        last = mm(ps[:, n, q * P:(q + 1) * P], pqT[:, ch, (n // 4) * P:(n // 4 + 1) * P],
                                  subT[:, ch, :], start=True, stop=True)
                    last.then_inc(s_mm.sem, 1)
                pe.wait_ge(s_ready.sem, s_ready.at(layer, 8))
                for n in range(4):
                    last = mm(ps[:, 4 + n, :], ident[:], x[:, n // 2, (n % 2) * 512:(n % 2 + 1) * 512],
                              start=True, stop=False, skip_group_check=True)
                last.then_inc(x_parked.sem, 1)
                with pe.Fori(0, EARLY // 2) as r:
                    for k in range(2):
                        pe.wait_ge(early_gelu.sem, early_gelu.at(layer, r * 2 + (k - 1)))
                        for e in range(2):
                            pe.wait_ge(early_ready.sem, early_ready.at(layer, r * SLOTS + (2 * k + e + 1)))
                            for kc in range(KC):
                                last = product(ps[:, 2 + k, e * T:(e + 1) * T],
                                               [w[:, 2 * k + e, kc * P:(kc + 1) * P] for w in (w_hi, w_lo)],
                                               [h[:, kc, :] for h in (hT_hi, hT_lo)], start=(kc == 0),
                                               stop=(kc == KC - 1))
                        last.then_inc(early_mm.sem, 1)
                for t in range(TT):
                    pe.wait_ge(rt_ready.sem, rt_ready.at(layer, t + 1))
                    transposes(ps[:, t, :], rt_tok[:, t, :, :].rearrange("p a b -> p (a b)"), 3
                               ).then_inc(rtT_mm.sem, 1)

                pe.wait_ge(early_gelu.sem, early_gelu.at(layer, EARLY))
                pe.wait_ge(route_ready.sem, route_ready.at(layer, 2))
                pe.sem_inc(seen_pe, 1)
                with pe.Fori(0, T // 16) as it:
                    for b in range(4):
                        pe.wait_ge(hot_ready.sem, hot_ready.at(layer, it * 4 + (b + 1)))
                        pe.wait_ge(g_ready.sem, g_ready.at(layer, it * 4 + (b - 3)))
                        for q in range(4):
                            last = mm(ps[:, b, q * P:(q + 1) * P], hot_i[:, b % 2, q, :],
                                      hot_j[:, b % 2, q, :], start=True, stop=True)
                        last.then_inc(g_mm.sem, 1)

                def hidden(p, k, slot, n):
                    pe.wait_ge(gelu_ready.sem, gelu_ready.at(layer, p - 1))
                    for e in range(2):
                        pe.wait_ge(w_ready.sem, w_ready.at(layer, n + (e + 1)))
                        for kc in range(KC):
                            last = product(ps[:, k, e * T:(e + 1) * T],
                                           [w[:, slot + e, kc * P:(kc + 1) * P] for w in (w_hi, w_lo)],
                                           [h[:, kc, :] for h in (hT_hi, hT_lo)], start=(kc == 0), stop=(kc == KC - 1))
                    last.then_inc(h_mm.sem, 1)

                def expert_out(p, k, slot, n, final=False):
                    pe.wait_ge(wgt_ready.sem, wgt_ready.at(layer, p + 1))
                    for e in range(2):
                        pe.wait_ge(w_ready.sem, w_ready.at(layer, n + (e + 1)))
                        for t in range(TT):
                            for half in range(2):
                                last = product(ps[:, 4 + 2 * t + half, :],
                                               [w[:, k, e * T + t * P:e * T + (t + 1) * P] for w in (wgt_hi, wgt_lo)],
                                               [w[:, slot + e, half * 512:(half + 1) * 512] for w in (w_hi, w_lo)],
                                               start=False, stop=(final and e == 1), group=True)
                    last.then_inc(v_mm.sem, 1)

                def u_and_v(p, k):
                    hidden(p + 1, 1 - k, 2, p * 4 + (N_STREAM + 2))
                    expert_out(p, k, 0, p * 4 + (N_STREAM + 4))

                pe.wait_ge(g_ready.sem, g_ready.at(layer, 64))
                hidden(0, 0, 0, N_STREAM)
                u_and_v(0, 0)
                with pe.Fori(0, LATE // 2 - 1) as it:
                    u_and_v(it * 2 + 1, 1)
                    u_and_v(it * 2 + 2, 0)
                expert_out(LATE - 1, 1, 2, N_V - 2)
                with pe.Fori(0, EARLY // 2 - 1) as it:
                    for k in range(2):
                        expert_out(it * 2 + (LATE + k), k, 2 * k, it * SLOTS + (N_V + 2 * k))
                expert_out(PAIRS - 2, 0, 0, N_DVE - 4)
                expert_out(PAIRS - 1, 1, 2, N_DVE - 2, final=True)

        @block.scalar
        def _(act):
            f = nc.scalar.activation
            own = Count()
            for s in (g_ready, gelu_ready, hi_ready, early_gelu):
                act.sem_inc(s.sem, s.start)
            act.wait_ge(x_loaded, 16)
            act.wait_ge(constants, 1)

            with act.Fori(0, LAYERS) as layer:
                act.wait_ge(layer_done.sem, layer_done.at(layer, 0))
                act.dma_start(par[:], params[bass.ds(layer, 1), :, :].rearrange("a p n -> p (a n)")
                              ).then_inc(par_loaded.sem, 16)
                act.dma_start(bias[:].rearrange("p a b -> p (a b)"),
                              bias_in[bass.ds(layer, 1), :, :].rearrange("a p n -> p (a n)")).then_inc(bias_loaded.sem, 16)

                def split(n):
                    if n < SLOTS:
                        act.wait_ge(v_mm.sem, v_mm.at(layer, n // 2 - 1))
                    else:
                        sig, count = used(n - SLOTS)
                        act.wait_ge(sig.sem, sig.at(layer, count))
                    w = w_loaded[n % SLOTS]
                    act.wait_ge(w.sem, w.at(layer, 16 * (n // SLOTS + 1)))
                    f(w_hi[:, n % SLOTS, :], raw[:, n % SLOTS, :], ACT.Copy).then_inc(hi_ready.sem, 1)

                def square_sums():
                    for t in range(TT):
                        f(nsq[:, t, :], x[:, t, :], ACT.Square, accum_out=ssq[:, t:t + 1]
                          ).then_inc(squared.sem, 1)

                square_sums()
                for n in range(SLOTS):
                    split(n)
                act.wait_ge(lam_sum.sem, lam_sum.at(layer, 1))
                f(lam[:, 2:4], lam[:, 0:2], ACT.Exp).then_inc(lam_exp.sem, 1)
                normed = {0: 0, 1: 1, 3: 2, 4: 3}
                where = {0: tok[:, 0], 1: tok[:, 1], 2: vals[:, 0], 3: tok[:, 2], 4: tok[:, 3],
                         5: vals[:, 1], 6: tok[:, 4], 7: tok[:, 5], 8: vals[:, 2]}
                for m in range(18):
                    cb, t = m // 2, m % 2
                    if t == 0:
                        for k in range(4):
                            split(4 * cb + k + SLOTS)
                    act.wait_ge(proj_mm.sem, proj_mm.at(layer, m + 1))
                    if cb in normed:
                        f(sq[:, 2 * normed[cb] + t, :], ps[:, proj_bank(m), :], ACT.Square
                          ).then_inc(sq_ready.sem, 1)
                    f(where[cb][:, t, :], ps[:, proj_bank(m), :], ACT.Copy).then_inc(proj_ev.sem, 1)

                def take_feature_tile(m, ten, t):
                    act.wait_ge(proj_mm.sem, proj_mm.at(layer, m + 1))
                    f(qkT[:, ten, :, t * P:(t + 1) * P], ps[:, proj_bank(m), :].rearrange("p (a b) -> p a b", a=4),
                      ACT.Copy).then_inc(proj_ev.sem, 1)

                def take_gates(g0):
                    for g in range(g0, g0 + 4):
                        for k in range(2):
                            split(N_QKV + 2 * g + k + SLOTS)
                        act.wait_ge(proj_mm.sem, proj_mm.at(layer, gate_m(g) + 1))
                        f(gates[:, 2 * g:2 * g + 2, :], ps[:, proj_bank(gate_m(g)), :].rearrange(
                            "p (a b) -> p a b", a=2), ACT.Copy).then_inc(proj_ev.sem, 1)

                for r in range(4):
                    take_feature_tile(M_CT + r, 4 + r // 2, r % 2)
                take_gates(0)
                for c in range(6):
                    act.wait_ge(proj_mm.sem, proj_mm.at(layer, M_CZ + c + 1))
                    own.one(f(ce[:, c, :], ps[:, proj_bank(M_CZ + c), :], ACT.Abs, scale=SCALE).then_inc(act_chain, 1))
                    f(cz[:, c, :], ps[:, proj_bank(M_CZ + c), :], ACT.Copy, scale=SCALE
                      ).then_inc(proj_ev.sem, 1)
                act.wait_ge(act_chain, own.n)
                for i in range(2):
                    own.one(f(ce[:, 3 * i:3 * i + 3, :], ce[:, 3 * i:3 * i + 3, :], ACT.Exp, scale=-1.0).then_inc(act_chain, 1))
                act.wait_ge(act_chain, own.n)
                for i in range(2):
                    f(ce[:, 3 * i:3 * i + 3, :], ce[:, 3 * i:3 * i + 3, :], ACT.Ln, bias=1.0
                      ).then_inc(logs_ready.sem, 1)
                take_gates(4)
                for c in range(6):
                    act.wait_ge(loga_ready.sem, loga_ready.at(layer, c + 1))
                    f(cz[:, c, :], cz[:, c, :], ACT.Exp).then_inc(a_exp.sem, 1)
                take_gates(8)
                act.wait_ge(ss_ready.sem, ss_ready.at(layer, 8))
                for r in range(8):
                    take_feature_tile(M_ABT + r, r // 2, r % 2)
                for o in range(2):
                    act.wait_ge(cout_mm.sem, cout_mm.at(layer, o + 1))
                    f(yT[:, 2, 2 * o:2 * o + 2, :], ps[:, 4 + o, :].rearrange("p (a b) -> p a b", a=2),
                      ACT.Copy).then_inc(yc_ready.sem, 1)

                def take_probT(i):
                    t, _ = by_head(i)
                    n = (1 if i < 8 else 2) * (t + 1) * P
                    act.wait_ge(probT_mm.sem, probT_mm.at(layer, i + 1))
                    if i >= 2:
                        act.wait_ge(mix_mm.sem, mix_mm.at(layer, i - 1))
                    f(ptr[:, i % 2, 0:n], ps[:, 4 + i % 2, 0:n], ACT.Copy).then_inc(probT_ready.sem, 1)

                def take_yb(t):
                    act.wait_ge(mix_mm.sem, mix_mm.at(layer, 12 + 4 * t))
                    f(yT[:, 1, :, t * P:(t + 1) * P], ps[:, t, :].rearrange("p (a b) -> p a b", a=4), ACT.Copy
                      ).then_inc(yb_ready.sem, 1)

                for i in range(16):
                    t, _ = by_head(i)
                    act.wait_ge(smax_ready.sem, smax_ready.at(layer, i + 1))
                    for c in range(2):
                        s = sring[:, i % 3, c, 0:(t + 1) * P]
                        last = f(s, s, ACT.Exp, bias=nmax[:, i, c:c + 1], accum_out=rsum[:, i, c:c + 1])
                    last.then_inc(exp_ready.sem, 1)
                    if i:
                        take_probT(i - 1)
                    if i in (5, 9):
                        t = (i - 5) // 4
                        act.wait_ge(mix_mm.sem, mix_mm.at(layer, 4 * (t + 1)))
                        f(ysq[:, t, :], ps[:, t, :], ACT.Square).then_inc(ya_sq.sem, 1)
                    if i == 14:
                        take_yb(0)
                act.dma_start(subT[:].rearrange("p a b -> p (a b)"),
                              subk[bass.ds(layer, 1), :, :].rearrange("a p n -> p (a n)")
                              ).then_inc(subk_loaded.sem, 16)
                take_probT(15)
                take_yb(1)
                act.wait_ge(proj_ev.sem, proj_ev.at(layer, 48))
                for b in UP_ORDER:
                    f(gates[:, 8 * b:8 * b + 8, :], gates[:, 8 * b:8 * b + 8, :], ACT.Sigmoid
                      ).then_inc(gate_ready.sem, 1)
                for n in range(N_STREAM - N_WQ - N_OUT - N_BR, N_STREAM - N_WQ):
                    split(n + SLOTS)
                act.wait_ge(x_mid.sem, x_mid.at(layer, 4))
                square_sums()
                def split_e(slot, rnd, sig, count):
                    act.wait_ge(sig.sem, sig.at(layer, count))
                    act.wait_ge(w_loaded[slot].sem, w_loaded[slot].at(layer, rnd * 16 + 16))
                    f(w_hi[:, slot, :], raw[:, slot, :], ACT.Copy).then_inc(hi_ready.sem, 1)

                for n in range(N_WQ // 2):
                    if n < 6:
                        for k in range(2):
                            split(N_STREAM - N_WQ + 2 * n + k + SLOTS)
                    if n == 7:
                        for e in range(2):
                            split_e(e, N_STREAM // SLOTS, *used(N_STREAM - SLOTS + e))
                    act.wait_ge(pq_mm.sem, pq_mm.at(layer, n + 1))
                    f(pqT[:, 2 * n:2 * n + 2, :], ps[:, 4 + n % 4, :].rearrange("p (a b) -> p a b", a=2),
                      ACT.Copy).then_inc(pq_ready.sem, 1)
                for n in range(8):
                    act.wait_ge(s_mm.sem, s_mm.at(layer, n + 1))
                    f(scores[:, n // 4, (n % 4) * 4:(n % 4) * 4 + 4, :],
                      ps[:, n, :].rearrange("p (a b) -> p a b", a=4), ACT.Copy).then_inc(s_ready.sem, 1)
                def early_pair(q, k, rnd, first=False):
                    for e in range(2):
                        sig, count = used(N_STREAM - 2 + e) if first else (early_mm, q)
                        split_e(2 * (1 - k) + e, rnd, sig, count)
                    act.wait_ge(early_mm.sem, early_mm.at(layer, q + 1))
                    f(G[:, bass.ds(q * 2 + 2 * LATE, 2), :] if not first else G[:, 2 * LATE:2 * LATE + 2, :],
                      ps[:, 2 + k, :].rearrange("p (a b) -> p a b", a=2), ACT.Gelu).then_inc(early_gelu.sem, 1)

                def early_pairs(q0, count):
                    with act.Fori(0, count // 2) as r:
                        for k in range(2):
                            early_pair(r * 2 + (q0 + k), 1 - k, r + (N_STREAM // SLOTS + (q0 + k + 1) // 2))

                def exponents(t):
                    act.wait_ge(best_ready.sem, best_ready.at(layer, t + 1))
                    f(bd[:, t, :], bd[:, t, :], ACT.Exp).then_inc(best_exp.sem, 1)

                early_pair(0, 0, N_STREAM // SLOTS, first=True)
                early_pairs(1, EARLY // 2)
                exponents(0)
                early_pairs(EARLY // 2 + 1, EARLY // 2 - 2)
                exponents(1)
                for e in range(2):
                    split_e(e, (N_STREAM + N_EARLY) // SLOTS, early_mm, EARLY - 1)
                act.wait_ge(early_mm.sem, early_mm.at(layer, EARLY))
                f(G[:, KEYS - 2:KEYS, :], ps[:, 3, :].rearrange("p (a b) -> p a b", a=2), ACT.Gelu
                  ).then_inc(early_gelu.sem, 1)
                for t in range(TT):
                    act.wait_ge(rtT_mm.sem, rtT_mm.at(layer, t + 1))
                    f(route[:, :, t * P:(t + 1) * P], ps[:, t, 0:3 * P].rearrange("p (a b) -> p a b", a=3),
                      ACT.Copy).then_inc(route_ready.sem, 1)
                with act.Fori(0, T // 16) as it:
                    for b in range(4):
                        act.wait_ge(g_mm.sem, g_mm.at(layer, it * 4 + (b + 1)))
                        act.wait_ge(part_used.sem, part_used.at(layer, it * 4 + (b - 1)))
                        tokens = ps[:, b, :].rearrange("p (t j) -> p j t", t=4)
                        f((g_part_a, g_part_b)[b % 2][:], tokens[:, 2 * LATE:KEYS, :], ACT.Copy
                          ).then_inc(part_ready.sem, 1)
                        f(G[:, 0:2 * LATE, bass.ds(it * 16 + b * 4, 4)], tokens[:, 0:2 * LATE, :], ACT.Copy
                          ).then_inc(g_ready.sem, 1)

                FIRST = (N_STREAM + N_EARLY) // SLOTS

                def experts(p, k, first=False):
                    rnd = p + FIRST
                    for e in range(2):
                        sig, count = (early_mm, EARLY) if first else (h_mm, p + 1)
                        split_e(2 + e, rnd, sig, count)
                    act.wait_ge(h_mm.sem, h_mm.at(layer, p + 1))
                    act.wait_ge(wgt_ready.sem, wgt_ready.at(layer, p - 1))
                    f(act_h[:, k, :], ps[:, k, :], ACT.Gelu).then_inc(gelu_ready.sem, 1)
                    for e in range(2):
                        sig, count = (h_mm, 1) if first else (v_mm, p)
                        split_e(e, rnd + 1, sig, count)

                act.wait_ge(part_used.sem, part_used.at(layer, 64))
                experts(0, 0, first=True)
                with act.Fori(0, LATE // 2 - 1) as it:
                    for k in range(2):
                        experts(it * 2 + (k + 1), 1 - k)
                for e in range(2):
                    split_e(2 + e, FIRST + LATE - 1, h_mm, LATE)
                act.wait_ge(h_mm.sem, h_mm.at(layer, LATE))
                f(act_h[:, 1, :], ps[:, 1, :], ACT.Gelu).then_inc(gelu_ready.sem, 1)
                with act.Fori(0, EARLY // 2) as it:
                    for k in range(2):
                        for e in range(2):
                            split_e(2 * k + e, it + (FIRST + LATE), v_mm, it * 2 + (LATE - 1 + k))
                act.wait_ge(act_chain, own.n)
                act.sem_clear(act_chain)
                own.n = 0

        @block.vector
        def _(dve):
            v = nc.vector
            own = Count()
            for s in (wgt_ready, layer_done, w_ready):
                dve.sem_inc(s.sem, s.start)
            dve.wait_ge(x_loaded, 16)
            dve.wait_ge(constants, 1)

            with dve.Fori(0, LAYERS) as layer:
                def split(n):
                    for i in n:
                        dve.wait_ge(hi_ready.sem, hi_ready.at(layer, i + 1))
                        v.tensor_tensor(w_lo[:, i % SLOTS, :], raw[:, i % SLOTS, :],
                                        w_hi[:, i % SLOTS, :].bitcast(F), ALU.subtract).then_inc(w_ready.sem, 1)

                def norm(which):
                    for t in range(TT):
                        dve.wait_ge(rstd_ready.sem, rstd_ready.at(layer, 2 * which + t + 1))
                        v.tensor_scalar(xs[:, t, :], x[:, t, :], rstd[:, t:t + 1], None, ALU.mult
                                        ).then_inc(xs_ready.sem, 1)
                    tiles = []
                    for n in range(4):
                        t, half = n // 2, n % 2
                        dve.wait_ge(normT_mm.sem, normT_mm.at(layer, 4 * which + n + 1))
                        gain = par[:, (C_N1, C_N2)[which] + 4 * half:(C_N1, C_N2)[which] + 4 * half + 4]
                        own.one(v.tensor_tensor(htmp[:, n, :].rearrange("p (a b) -> p a b", a=4),
                                                ps[:, n, :].rearrange("p (a b) -> p a b", a=4),
                                                gain.unsqueeze(2).broadcast_to([P, 4, P]), ALU.mult
                                                ).then_inc(dve_chain, 1))
                        tiles.append((htmp[:, n, :].rearrange("p (a b) -> p a b", a=4),
                                      [h[:, 4 * half:4 * half + 4, t * P:(t + 1) * P] for h in (hT_hi, hT_lo)]))
                    dve.wait_ge(dve_chain, own.n)
                    for src, (hi, lo) in tiles:
                        own.one(v.tensor_copy(hi, src).then_inc(dve_chain, 1))
                    dve.wait_ge(dve_chain, own.n)
                    for src, (hi, lo) in tiles:
                        v.tensor_tensor(lo, src, hi.bitcast(F), ALU.subtract).then_inc(hT_ready.sem, 1)

                dve.wait_ge(par_loaded.sem, par_loaded.at(layer, 16))
                dve.sem_inc(seen_dve, 1)
                norm(0)
                split(range(SLOTS))
                dve.wait_ge(normT_mm.sem, normT_mm.at(layer, 4))
                own.one(v.tensor_tensor(lam_w[:], par[:, C_LAM:C_LAM + 128].rearrange("p (a b) -> p a b", a=2),
                                        par[:, C_LAM + 128:C_LAM + 256].rearrange("p (a b) -> p a b", a=2),
                                        ALU.mult).then_inc(dve_chain, 1))
                dve.wait_ge(dve_chain, own.n)
                v.tensor_reduce(lam[:, 0:2], lam_w[:], AX.X, ALU.add).then_inc(lam_sum.sem, 1)
                dve.wait_ge(lam_exp.sem, lam_exp.at(layer, 1))
                own.one(v.tensor_tensor(lam[:, 4:5], lam[:, 2:3], lam[:, 3:4], ALU.subtract).then_inc(dve_chain, 1))
                dve.wait_ge(dve_chain, own.n)
                own.one(v.tensor_scalar(lam[:, 5:6], lam[:, 4:5], par[:, C_LAMI:C_LAMI + 1], -1.0,
                                        ALU.add, ALU.mult).then_inc(dve_chain, 1))

                def head_sums(i):
                    dve.wait_ge(sq_ready.sem, sq_ready.at(layer, i + 1))
                    v.tensor_reduce(qk_ss[:, i, :], sq[:, i, :].rearrange("p (h d) -> p h d", h=8), AX.X, ALU.add
                                    ).then_inc(ss_ready.sem, 1)

                evacuated = [1, 2, 3, 4, 7, 8, 9, 10]

                def head_norm(i):
                    ten, t = i // 2, i % 2
                    z = tok[:, ten, t, :].rearrange("p (h d) -> p h d", h=8)
                    dve.wait_ge(qkrs_ready.sem, qkrs_ready.at(layer, i + 1))
                    dve.wait_ge(proj_ev.sem, proj_ev.at(layer, evacuated[i]))
                    own.one(v.tensor_tensor(z, z, qk_rs[:, i, :].unsqueeze(2).broadcast_to([P, 8, HD]), ALU.mult).then_inc(dve_chain, 1))
                    dve.wait_ge(dve_chain, own.n)
                    gain = par[:, C_GAIN + HD * ten:C_GAIN + HD * (ten + 1)]
                    last = v.tensor_tensor(z, z, gain.unsqueeze(1).broadcast_to([P, 8, HD]), ALU.mult)
                    if ten < 2:
                        own.one(last.then_inc(dve_chain, 1))
                        dve.wait_ge(dve_chain, own.n)
                        pair = tok[:, ten, t, :].rearrange("p (h d) -> p h d", h=8)[:, :, 0:16].rearrange(
                            "p h (a d) -> p h a d", a=2)
                        if i:
                            dve.wait_ge(qk_normed.sem, qk_normed.at(layer, i))
                        for j, col in enumerate((C_COS, C_SIN)):
                            tab = par[:, col + 8 * t:col + 8 * t + 8]
                            own.one(v.tensor_tensor(rope_t[:, j, :, :].rearrange("p h (a d) -> p h a d", a=2), pair,
                                                      tab.unsqueeze(1).unsqueeze(1).broadcast_to([P, 8, 2, 8]),
                                                      ALU.mult).then_inc(dve_chain, 1))
                        dve.wait_ge(dve_chain, own.n)
                        v.tensor_tensor(z[:, :, 0:8], rope_t[:, 0, :, 0:8], rope_t[:, 1, :, 8:16], ALU.subtract)
                        last = v.tensor_tensor(z[:, :, 8:16], rope_t[:, 0, :, 8:16], rope_t[:, 1, :, 0:8], ALU.add)
                    last.then_inc(qk_normed.sem, 1)

                summed = 0
                for cb in range(9):
                    split(range(4 * cb + SLOTS, 4 * cb + 2 * SLOTS))
                    if cb in (1, 2, 4, 5):
                        for t in range(TT):
                            head_sums(summed)
                            if summed:
                                head_norm(summed - 1)
                            summed += 1
                    if cb == 6:
                        head_norm(7)
                for n in range(N_QKV, N_QKV + 8, 2):
                    split((n + SLOTS, n + 1 + SLOTS))

                for i in range(2):
                    part = slice(3 * i, 3 * i + 3)
                    dve.wait_ge(logs_ready.sem, logs_ready.at(layer, i + 1))
                    if i == 0:
                        dve.wait_ge(masks_ready.sem, masks_ready.at(layer, 1))
                        dve.sem_inc(seen_dve, 1)
                    own.one(v.tensor_scalar(ctmp[:], cz[:, part, :], 0.0, None, ALU.max).then_inc(dve_chain, 1))
                    dve.wait_ge(dve_chain, own.n)
                    flat = ce[:, part, :].rearrange("p a b -> p (a b)")
                    zflat = cz[:, part, :].rearrange("p a b -> p (a b)")
                    own.one(v.scalar_tensor_tensor(out=flat, in0=ctmp[:].rearrange("p a b -> p (a b)"), scalar=-1.0,
                                                     in1=flat, op0=ALU.mult, op1=ALU.subtract).then_inc(dve_chain, 1))
                    dve.wait_ge(dve_chain, own.n)
                    own.one(v.tensor_tensor(zflat, zflat, flat, ALU.add).then_inc(dve_chain, 1))
                    dve.wait_ge(dve_chain, own.n)
                    if i == 0:
                        blocks = ce[:, 0:2, :].rearrange("p a (h q) -> p (a h) q", q=P)
                        v.tensor_tensor(blocks, blocks, strict.unsqueeze(1).broadcast_to([P, 8, P]), ALU.mult)
                        blocks = ce[:, 2, :].rearrange("p (h q) -> p h q", q=T)[:, :, 0:P]
                        last = v.tensor_tensor(blocks, blocks, strict.unsqueeze(1).broadcast_to([P, 2, P]),
                                               ALU.mult)
                    else:
                        blocks = ce[:, 3:6, :].rearrange("p a (h q) -> p (a h) q", q=T)[:, :, 0:P]
                        last = v.tensor_tensor(blocks, blocks, strict.unsqueeze(1).broadcast_to([P, 6, P]),
                                               ALU.mult)
                    last.then_inc(keep_ready.sem, 1)
                dve.wait_ge(dve_chain, own.n)
                split(range(N_QKV + 8 + SLOTS, N_QKV + 16 + SLOTS))
                for c in range(6):
                    dve.wait_ge(later_mm.sem, later_mm.at(layer, c + 1))
                    v.tensor_tensor(cz[:, c, :], cz[:, c, :], ps[:, 4 + c % 2, :], ALU.add
                                    ).then_inc(loga_ready.sem, 1)
                for c in range(6):
                    dve.wait_ge(a_exp.sem, a_exp.at(layer, c + 1))
                    n = P if c < 2 else T
                    blocks = cz[:, c, :].rearrange("p (h q) -> p h q", q=n)[:, :, 0:P]
                    v.tensor_tensor(blocks, blocks, strict.unsqueeze(1).broadcast_to([P, 512 // n, P]), ALU.mult
                                    ).then_inc(a_ready.sem, 1)

                split(range(N_QKV + 16 + SLOTS, N_QKV + 24 + SLOTS))
                dve.wait_ge(bias_ready.sem, bias_ready.at(layer, 1))
                dve.sem_inc(seen_dve, 1)

                def score_max(i):
                    t, ch = by_head(i)
                    n, off = (t + 1) * P, (1 - t) * P
                    s = sring[:, i % 3, :, 0:n]
                    if i >= 3:
                        dve.wait_ge(probT_mm.sem, probT_mm.at(layer, i - 2))
                    dve.wait_ge(score_mm.sem, score_mm.at(layer, i + 1))
                    add = (blockmask[:, off:off + n].unsqueeze(1).broadcast_to([P, 2, n]) if i < 8
                           else bias[:, 2 * ch:2 * ch + 2, off:off + n])
                    own.one(v.scalar_tensor_tensor(out=s, in0=ps[:, SCORE_BANK[i % 2]:SCORE_BANK[i % 2] + 2, 0:n],
                                                     scalar=SCALE, in1=add, op0=ALU.mult, op1=ALU.add).then_inc(dve_chain, 1))
                    dve.wait_ge(dve_chain, own.n)
                    v.tensor_reduce(nmax[:, i, :], s, AX.X, ALU.max, negate=True).then_inc(smax_ready.sem, 1)

                def probabilities(i):
                    t, _ = by_head(i)
                    s = [sring[:, i % 3, c, 0:(t + 1) * P] for c in range(2)]
                    dve.wait_ge(exp_ready.sem, exp_ready.at(layer, i + 1))
                    own.one(v.reciprocal(rinv[:, i, :], rsum[:, i, :]).then_inc(dve_chain, 1))
                    dve.wait_ge(dve_chain, own.n)
                    if i < 8:
                        own.one(v.tensor_scalar(rinv[:, i, 1:2], rinv[:, i, 1:2], lam[:, 5:6], None, ALU.mult).then_inc(dve_chain, 1))
                        own.one(v.tensor_scalar(s[0], s[0], rinv[:, i, 0:1], None, ALU.mult).then_inc(dve_chain, 1))
                        dve.wait_ge(dve_chain, own.n)
                        last = v.scalar_tensor_tensor(out=s[0], in0=s[1], scalar=rinv[:, i, 1:2], in1=s[0],
                                                      op0=ALU.mult, op1=ALU.add)
                    else:
                        v.tensor_scalar(s[0], s[0], rinv[:, i, 0:1], None, ALU.mult)
                        last = v.tensor_scalar(s[1], s[1], rinv[:, i, 1:2], None, ALU.mult)
                    last.then_inc(prob_ready.sem, 1)

                def ya_sums(t):
                    dve.wait_ge(ya_sq.sem, ya_sq.at(layer, t + 1))
                    v.tensor_reduce(ya_ss[:, t, :], ysq[:, t, :].rearrange("p (h d) -> p h d", h=4), AX.X, ALU.add
                                    ).then_inc(ya_ssr.sem, 1)

                def ya_norm(t):
                    dve.wait_ge(ya_rsr.sem, ya_rsr.at(layer, t + 1))
                    v.tensor_tensor(yan[:, t, :].rearrange("p (h d) -> p h d", h=4),
                                    ps[:, t, :].rearrange("p (h d) -> p h d", h=4),
                                    ya_rs[:, t, :].unsqueeze(2).broadcast_to([P, 4, P]), ALU.mult
                                    ).then_inc(ya_normed.sem, 1)

                score_max(0)
                score_max(1)
                for i in range(16):
                    probabilities(i)
                    if i + 2 < 16:
                        score_max(i + 2)
                    if i in (5, 9):
                        ya_sums((i - 5) // 4)
                    if i in (6, 10):
                        ya_norm((i - 6) // 4)
                for t in range(TT):
                    dve.wait_ge(yaT_mm.sem, yaT_mm.at(layer, t + 1))
                    v.tensor_scalar(yT[:, 0, :, t * P:(t + 1) * P], ps[:, 4 + t, :].rearrange("p (a b) -> p a b", a=4),
                                    par[:, C_SUB:C_SUB + 1], par[:, C_OML:C_OML + 1], ALU.mult, ALU.mult
                                    ).then_inc(ya_ready.sem, 1)

                for b, done in ((2, yc_ready), (1, yb_ready), (0, ya_ready)):
                    dve.wait_ge(done.sem, done.at(layer, 2))
                    own.one(v.tensor_copy(y_hi[:, b, :, :], yT[:, b, :, :]).then_inc(dve_chain, 1))
                    dve.wait_ge(dve_chain, own.n)
                    v.tensor_tensor(y_lo[:, b, :, :], yT[:, b, :, :], y_hi[:, b, :, :].bitcast(F), ALU.subtract
                                    ).then_inc(y_split.sem, 1)

                for u in range(12):
                    split((N_STREAM - N_WQ - N_OUT - N_BR + u + SLOTS,))
                    d0 = (u % 4) * 2
                    b = UP_ORDER[u // 4]
                    if u % 4 == 0:
                        dve.wait_ge(gate_ready.sem, gate_ready.at(layer, u // 4 + 1))
                    dve.wait_ge(up_mm.sem, up_mm.at(layer, u + 1))
                    part = merged[:, d0:d0 + 2, :]
                    dst = part if u < 4 else upt[:, u % 2, :].rearrange("p (a b) -> p a b", a=2)
                    v.tensor_tensor(dst, ps[:, u % 4, :].rearrange("p (a b) -> p a b", a=2),
                                    gates[:, 8 * b + d0:8 * b + d0 + 2, :], ALU.mult).then_inc(up_taken.sem, 1)
                    if u >= 4:
                        dve.wait_ge(up_taken.sem, up_taken.at(layer, u + 1))
                        dve.wait_ge(dve_chain, own.n)
                        own.one(v.tensor_tensor(part, part, dst, ALU.add).then_inc(dve_chain, 1))
                    if u >= 8:
                        hi, lo = m_hi[:, d0:d0 + 2, :], m_lo[:, d0:d0 + 2, :]
                        dve.wait_ge(dve_chain, own.n)
                        own.one(v.tensor_copy(hi, part).then_inc(dve_chain, 1))
                        dve.wait_ge(dve_chain, own.n)
                        v.tensor_tensor(lo, part, hi.bitcast(F), ALU.subtract).then_inc(merged_ready.sem, 1)
                for n in range(N_OUT):
                    split((N_STREAM - N_WQ - N_OUT + n + SLOTS,))
                for n in range(4):
                    c, t = n // 2, n % 2
                    dve.wait_ge(wout_mm.sem, wout_mm.at(layer, n + 1))
                    v.tensor_tensor(x[:, t, c * 512:(c + 1) * 512], x[:, t, c * 512:(c + 1) * 512],
                                    ps[:, 4 + n, :], ALU.add).then_inc(x_mid.sem, 1)
                norm(1)
                for n in range(12):
                    split((N_STREAM - N_WQ + n + SLOTS,))

                def top(values, best, where_):
                    for r, vals_ in enumerate(values):
                        own.one(v.max(best[r][:, 0:8], vals_).then_inc(dve_chain, 1))
                    dve.wait_ge(dve_chain, own.n)
                    for r, vals_ in enumerate(values):
                        own.one(v.max_index(where_[r][:, 0:8], best[r][:, 0:8], vals_).then_inc(dve_chain, 1))
                    dve.wait_ge(dve_chain, own.n)
                    for r, vals_ in enumerate(values):
                        own.one(v.match_replace(vals_, best[r][:, 0:8], vals_, -3.0e38).then_inc(dve_chain, 1))
                    dve.wait_ge(dve_chain, own.n)
                    for r, vals_ in enumerate(values):
                        own.one(v.max(best[r][:, 8:16], vals_).then_inc(dve_chain, 1))
                    dve.wait_ge(dve_chain, own.n)
                    for r, vals_ in enumerate(values):
                        own.one(v.max_index(where_[r][:, 8:16], best[r][:, 8:16], vals_).then_inc(dve_chain, 1))
                    dve.wait_ge(dve_chain, own.n)

                def choose(t):
                    dve.wait_ge(s_ready.sem, s_ready.at(layer, 4 * (t + 1)))
                    dve.sem_inc(seen_dve, 1)
                    top([scores[:, t, ch, :] for ch in range(16)], [topv[:, t, ch, :] for ch in range(16)],
                        [topi[:, t, ch, :] for ch in range(16)])
                    halves = topv[:, t, :, :].rearrange("p (h s) k -> p h s k", s=2)
                    own.one(v.tensor_copy(topf[:, t, :, :], topi[:, t, :, :]).then_inc(dve_chain, 1))
                    own.one(v.tensor_tensor(cand[:], halves[:, :, 0, :].unsqueeze(3).broadcast_to([P, 8, 16, 16]),
                                              halves[:, :, 1, :].unsqueeze(2).broadcast_to([P, 8, 16, 16]), ALU.add).then_inc(dve_chain, 1))
                    dve.wait_ge(dve_chain, own.n)
                    top([cand[:, h, :, :].rearrange("p a b -> p (a b)") for h in range(8)],
                        [bestv[:, t, h, :] for h in range(8)], [bestp[:, t, h, :] for h in range(8)])
                    v.tensor_tensor(bd[:, t, :].rearrange("p (h k) -> p h k", h=8), bestv[:, t, :, :],
                                    bestv[:, t, :, 0:1].broadcast_to([P, 8, 16]), ALU.subtract
                                    ).then_inc(best_ready.sem, 1)

                def places(t):
                    own.one(v.tensor_scalar(pab[:, 0, :, :], bestp[:, t, :, :], 4, None, ALU.logical_shift_right).then_inc(dve_chain, 1))
                    own.one(v.tensor_scalar(pab[:, 1, :, :], bestp[:, t, :, :], 15, None, ALU.bitwise_and).then_inc(dve_chain, 1))
                    dve.wait_ge(dve_chain, own.n)
                    own.one(v.tensor_copy(pabf[:], pab[:]).then_inc(dve_chain, 1))
                    dve.wait_ge(dve_chain, own.n)
                    keys = topf[:, t, :, :].rearrange("p (h s) k -> p h s k", s=2)
                    for s, e in ((0, eq), (1, eq2)):
                        own.one(v.tensor_tensor(e[:], pabf[:, s, :, :].unsqueeze(3).broadcast_to([P, 8, 16, 16]),
                                                  iota[:, 0:16].unsqueeze(1).unsqueeze(1).broadcast_to([P, 8, 16, 16]),
                                                  ALU.is_equal).then_inc(dve_chain, 1))
                    dve.wait_ge(dve_chain, own.n)
                    for s, e in ((0, eq), (1, eq2)):
                        own.one(v.tensor_tensor(e[:], e[:], keys[:, :, s, :].unsqueeze(2).broadcast_to([P, 8, 16, 16]),
                                                  ALU.mult).then_inc(dve_chain, 1))
                    dve.wait_ge(dve_chain, own.n)
                    for s, e in ((0, eq), (1, eq2)):
                        own.one(v.tensor_reduce(rt_tok[:, t, s, :].rearrange("p (h k) -> p h k", h=8), e[:], AX.X,
                                                  ALU.add).then_inc(dve_chain, 1))

                def weights(t):
                    dve.wait_ge(best_exp.sem, best_exp.at(layer, t + 1))
                    if t:
                        dve.wait_ge(rt_ready.sem, rt_ready.at(layer, t))
                    own.one(v.tensor_reduce(gsum[:], bd[:, t, :].rearrange("p (h k) -> p h k", h=8), AX.X, ALU.add).then_inc(dve_chain, 1))
                    dve.wait_ge(dve_chain, own.n)
                    own.one(v.reciprocal(ginv[:], gsum[:]).then_inc(dve_chain, 1))
                    dve.wait_ge(dve_chain, own.n)
                    v.tensor_tensor(rt_tok[:, t, 2, :].rearrange("p (h k) -> p h k", h=8),
                                    bd[:, t, :].rearrange("p (h k) -> p h k", h=8),
                                    ginv[:].unsqueeze(2).broadcast_to([P, 8, 16]), ALU.mult
                                    ).then_inc(rt_ready.sem, 1)

                choose(0)
                places(0)
                choose(1)
                weights(0)
                places(1)
                weights(1)

                dve.wait_ge(x_parked.sem, x_parked.at(layer, 1))
                dve.sem_inc(seen_dve, 1)
                dve.wait_ge(route_ready.sem, route_ready.at(layer, 2))
                dve.sem_inc(seen_dve, 1)
                with dve.Fori(0, T // 16) as it:
                    for b in range(4):
                        dve.wait_ge(g_mm.sem, g_mm.at(layer, it * 4 + (b - 1)))
                        dve.sem_inc(seen_dve, 1)
                        for q in range(4):
                            tk = bass.ds(it * 16 + (b * 4 + q), 1)
                            v.tensor_scalar(hot_i[:, b % 2, q, :], iota[:], route[:, 0, tk], route[:, 2, tk],
                                            ALU.is_equal, ALU.mult)
                            last = v.tensor_scalar(hot_j[:, b % 2, q, :], iota[:], route[:, 1, tk], None,
                                                   ALU.is_equal)
                        last.then_inc(hot_ready.sem, 1)

                def split_e(n, slot):
                    dve.wait_ge(hi_ready.sem, hi_ready.at(layer, n + (N_EARLY + 1)))
                    v.tensor_tensor(w_lo[:, slot, :], raw[:, slot, :], w_hi[:, slot, :].bitcast(F), ALU.subtract
                                    ).then_inc(w_ready.sem, 1)

                def weigh(p, k, at):
                    dve.wait_ge(gelu_ready.sem, gelu_ready.at(layer, p + 1))
                    a = act_h[:, k, :].rearrange("p (a b) -> p a b", a=2)
                    v.tensor_tensor(a, a, G[:, at, :], ALU.mult).then_inc(dve_loop, 1)
                    dve.wait_ge(dve_loop, 1)
                    dve.sem_inc(seen_dve, 1)
                    dve.wait_ge(v_mm.sem, v_mm.at(layer, p - 1))
                    v.tensor_copy(wgt_hi[:, k, :], act_h[:, k, :]).then_inc(dve_loop, 1)
                    dve.wait_ge(dve_loop, 2)
                    dve.sem_clear(dve_loop)
                    v.tensor_tensor(wgt_lo[:, k, :], act_h[:, k, :], wgt_hi[:, k, :].bitcast(F), ALU.subtract
                                    ).then_inc(wgt_ready.sem, 1)

                def experts(p, k, at):
                    for e in range(2):
                        split_e(p * 4 + (N_STREAM + 2 + e), 2 + e)
                    weigh(p, k, at)
                    for e in range(2):
                        split_e(p * 4 + (N_STREAM + 4 + e), e)

                dve.wait_ge(g_ready.sem, g_ready.at(layer, 64))
                dve.sem_inc(seen_dve, 1)
                for e in range(2):
                    split_e(N_STREAM + e, e)
                experts(0, 0, slice(0, 2))
                with dve.Fori(0, LATE // 2 - 1) as it:
                    for k in range(2):
                        experts(it * 2 + (k + 1), 1 - k, bass.ds(it * 4 + 2 * (k + 1), 2))
                for e in range(2):
                    split_e(N_V - 2 + e, 2 + e)
                weigh(LATE - 1, 1, slice(2 * LATE - 2, 2 * LATE))
                dve.wait_ge(part_used.sem, part_used.at(layer, 64))
                dve.sem_inc(seen_dve, 1)
                with dve.Fori(0, EARLY // 2) as it:
                    for k in range(2):
                        at = bass.ds(it * 4 + (2 * LATE + 2 * k), 2)
                        dve.wait_ge(v_mm.sem, v_mm.at(layer, it * 2 + (LATE + k - 1)))
                        v.tensor_copy(wgt_hi[:, k, :].rearrange("p (a b) -> p a b", a=2), G[:, at, :]
                                      ).then_inc(dve_loop, 1)
                        dve.wait_ge(dve_loop, 1)
                        dve.sem_clear(dve_loop)
                        v.tensor_tensor(wgt_lo[:, k, :].rearrange("p (a b) -> p a b", a=2), G[:, at, :],
                                        wgt_hi[:, k, :].bitcast(F).rearrange("p (a b) -> p a b", a=2), ALU.subtract
                                        ).then_inc(wgt_ready.sem, 1)
                        for e in range(2):
                            split_e(it * SLOTS + (N_V + 2 * k + e), 2 * k + e)
                dve.wait_ge(v_mm.sem, v_mm.at(layer, PAIRS))
                v.tensor_copy(x[:].rearrange("p t (a b) -> p (t a) b", a=2), ps[:, 4:8, :]
                              ).then_inc(layer_done.sem, 1)
                dve.wait_ge(dve_chain, own.n)
                dve.sem_clear(dve_chain)
                own.n = 0


def kernel(x, norm1_g, w_in, a_qnorm_g, a_knorm_g, lam_q1, lam_k1, lam_q2, lam_k2, a_subln_g, b_qnorm_g,
           b_knorm_g, b_rel_bias, w_branch, w_out, norm2_g, peer_wq, peer_subkeys, peer_u, peer_v):
    import concourse.bacc as bacc
    from concourse.bass_utils import run_bass_kernel_spmd

    L = LAYERS
    f32 = np.float32

    def arr(a):
        return np.asarray(a)

    def chunk_pairs(w, blocks):
        return w.reshape(L, 4, 2, P, blocks, 512).transpose(0, 4, 1, 3, 2, 5).reshape(L, 4 * blocks, P, SLOT)

    def columns(w):
        n = w.shape[-1] // P
        return w.reshape(L, KC, P, n, P).transpose(0, 3, 2, 1, 4).reshape(L, n, P, SLOT)

    w_in, w_br = arr(w_in), arr(w_branch)
    stream = np.concatenate([
        chunk_pairs(w_in[:, :, :9 * 512], 9),
        columns(w_in[:, :, 9 * 512:]),
        w_br[:, UP_ORDER, :, :].reshape(L, 3, 4, P, 4, 256).transpose(0, 1, 4, 3, 2, 5).reshape(L, N_BR, P, SLOT),
        chunk_pairs(arr(w_out), 2),
        columns(arr(peer_wq)),
    ], axis=1).reshape(L * N_STREAM, P, SLOT)
    w_u = arr(peer_u).reshape(L, P, KEYS, KC, P).transpose(0, 2, 4, 3, 1).reshape(L * KEYS, P, SLOT)
    w_v = arr(peer_v).reshape(L, P, KEYS, SLOT)
    subk = arr(peer_subkeys).transpose(0, 4, 2, 1, 3).reshape(L, P, 16 * P)

    def everywhere(a):
        return np.broadcast_to(a[:, None, :], (L, P, a.shape[-1]))

    lam_init = np.array([0.8 - 0.6 * math.exp(-0.3 * i) for i in range(L)])
    half = HD // 8
    inv = 1.0 / (f32(500000.0) ** (np.arange(0, 2 * half, 2, dtype=f32) / f32(2 * half)))
    ang = np.arange(T, dtype=f32)[:, None] * inv[None, :].astype(f32)

    def table(a):
        return np.broadcast_to(a.astype(f32).reshape(TT, P, 8).transpose(1, 0, 2).reshape(1, P, 16), (L, P, 16))

    params = np.concatenate([
        arr(norm1_g).reshape(L, KC, P).transpose(0, 2, 1),
        arr(norm2_g).reshape(L, KC, P).transpose(0, 2, 1),
        arr(a_subln_g).reshape(L, P, 1),
        np.broadcast_to(lam_init.astype(f32)[:, None, None], (L, P, 1)),
        np.broadcast_to((1.0 - lam_init).astype(f32)[:, None, None], (L, P, 1)),
        table(np.cos(ang)), table(np.sin(ang)),
        *[everywhere(arr(a)) for a in (a_qnorm_g, a_knorm_g, b_qnorm_g, b_knorm_g, lam_q1, lam_q2, lam_k1, lam_k2)],
    ], axis=2)
    distance = np.clip(np.arange(P)[:, None] - np.arange(2 * P)[None, :] + P, -REL, REL) + REL
    arrays = {
        "x": arr(x).reshape(TT, P, D).transpose(1, 0, 2), "stream": stream, "w_u": w_u, "w_v": w_v, "subk": subk,
        "params": params, "bias": arr(b_rel_bias)[:, :, distance].transpose(0, 2, 1, 3).reshape(L, P, B_HEADS * 2 * P),
    }
    arrays = {f"in_{k}": np.ascontiguousarray(a) for k, a in arrays.items()}

    nc = bacc.Bacc("TRN2", target_bir_lowering=False, num_devices=1)
    args = [nc.dram_tensor(k, a.shape, mybir.dt.from_np(a.dtype), kind="ExternalInput").ap()
            for k, a in arrays.items()]
    out = nc.dram_tensor("out_0", (P, TT, D), mybir.dt.float32, kind="ExternalOutput").ap()
    build(nc, *args, out)
    r = run_bass_kernel_spmd(nc, [arrays], core_ids=[0])
    return r.results[0]["out_0"].transpose(1, 0, 2).reshape(1, T, D)
```

```python
import math
from contextlib import ExitStack

import numpy as np
import concourse.bass as bass
from concourse import mybir

D, T, LAYERS = 1024, 256, 2
P = 128
TT = T // P
KC = D // P
HD = 64
A_HEADS, B_HEADS, C_HEADS = 4, 8, 8
PEER_HEADS, KEYS, TOPK = 8, 128, 16
REL = 128
SLOTS, SLOT = 4, 1024
N_QKV, N_GATE, N_BR, N_OUT, N_WQ = 36, 24, 12, 8, 16
N_STREAM = N_QKV + N_GATE + N_BR + N_OUT + N_WQ
PAIRS = KEYS // 2
EARLY = 18
FILL = 8
KEPT = FILL + EARLY
LATE = PAIRS - KEPT
N_EARLY = 2 * EARLY
N_LAYER = N_STREAM + 4 * PAIRS
N_HI = N_LAYER - 2 * FILL
N_DVE = N_HI - N_EARLY
N_V = N_STREAM + 4 * LATE
ROUNDS = N_LAYER // SLOTS
N_USED = 27 + 12 + 6 + 8
UP_ORDER = (2, 1, 0)
GROUP = 8
FILL_AT, FILL_TAKEN = (3, 7), 7
EPS = 1e-6
SCALE = HD ** -0.5
NEG = -1e30

C_N1, C_N2, C_SUB, C_LAMI, C_OML, C_COS, C_SIN = 0, 8, 16, 17, 18, 19, 35
C_GAIN, C_LAM = 51, 307
N_PAR = 563

TOK, VV, QKT, GATE, YT, MRG, BIAS, SCR = 0, 6144, 9216, 15360, 21504, 24576, 26624, 28672
ROPE, LAMW, PAR, MASKS = MRG, MRG + 256, SCR + 3072, SCR + 3072 + 608
SRING, PTR, YSQ, YAN, UPT = 0, 1536, 2560, 3584, 4608
PQT, SSB, CAND, EQ, TOPV, TOPI, TOPF, BV, BP, PAB, PABF, BEST_D = (
    0, 4096, 9216, 11264, 13312, 13824, 14336, 14848, 15104, 15360, 15872, 16384)
EQ2 = 16896


class Signal:

    def __init__(self, sem, per_layer, start=0):
        self.sem, self.per_layer, self.start = sem, per_layer, start

    def at(self, layer, n):
        return layer * self.per_layer + (self.start + n)


class Count:

    def __init__(self):
        self.n = 0

    def one(self, ins):
        self.n += 1


def build(nc, x_in, stream, w_u, w_v, subk, params, bias_in, out):
    F = mybir.dt.float32
    FR = mybir.dt.float32r
    U32 = mybir.dt.uint32
    BF = mybir.dt.bfloat16
    ALU = mybir.AluOpType
    ACT = mybir.ActivationFunctionType
    AX = mybir.AxisListType
    ctx = ExitStack()
    with ctx:
        def sb(name, shape, dt=F):
            return ctx.enter_context(nc.sbuf_tensor(name, shape, dt))

        def sem(name):
            return ctx.enter_context(nc.semaphore(name))

        def overlay(*tensors):
            with ExitStack() as region:
                return [region.enter_context(nc.sbuf_tensor(n, shape, dt)) for n, shape, dt in tensors]

        ident = sb("ident", [P, P])
        iota = sb("iota", [P, P])
        blockmask = sb("blockmask", [P, 2 * P])
        half_neg = sb("half_neg", [P, 8])
        keys_b, = overlay(("keys_b", [P, 2, T], BF))
        ssq = sb("ssq", [P, 2])
        rstd = sb("rstd", [P, 2])
        qk_ss = sb("qk_ss", [P, 8, 8])
        qk_rs = sb("qk_rs", [P, 8, 8])
        ya_ss = sb("ya_ss", [P, 2, 4])
        ya_rs = sb("ya_rs", [P, 2, 4])
        lam = sb("lam", [P, 8])
        gsum = sb("gsum", [P, 8])
        ginv = sb("ginv", [P, 8])
        sb("rest_of_keys_b", [P, 72])
        raw = sb("raw", [P, SLOTS, SLOT])
        _, *hot = overlay(("at_w_hi", [P, SLOTS // 2, SLOT], F), ("hot_0", [P, 2, KEYS, GROUP], BF),
                          ("hot_1", [P, 2, KEYS, GROUP], BF))
        hT_full, = overlay(("hT_full", [P, KC, T], F))
        w_hi = sb("w_hi", [P, SLOTS, SLOT], FR)
        _, hot_w_1, weight_parts = overlay(("at_w_lo", [P, SLOTS // 2, SLOT], F),
                                           ("hot_w_1", [P, 3, KEYS, GROUP], BF), ("weight_parts", [P, 3, T], BF))
        fill_h, = overlay(("fill_h", [P, 2, 512], F))
        w_lo = sb("w_lo", [P, SLOTS, SLOT], FR)
        hT_hi = sb("hT_hi", [P, KC, T], FR)
        hT_lo = sb("hT_lo", [P, KC, T], FR)
        g_part_b = sb("g_part_b", [P, 2 * KEPT, 4])
        hot_w_0, key_of = overlay(("hot_w_0", [P, 3, KEYS, GROUP], BF), ("key_of", [P, KEYS, GROUP], BF))
        hot_w = (hot_w_0, hot_w_1)
        wgt_hi, wgt_lo = overlay(("wgt_hi", [P, 2, 512], FR), ("wgt_lo", [P, 2, 512], FR))
        x = sb("x", [P, TT, D])
        route, g_part_a = overlay(("route", [P, 3, T], F), ("g_part_a", [P, 2 * KEPT, 4], F))
        act_h = sb("act_h", [P, 2, 512])
        _, m_hi, m_lo = overlay(("at_tok", [P, TOK + 8], F), ("m_hi", [P, KC, T], FR), ("m_lo", [P, KC, T], FR))
        _, y_hi, y_lo = overlay(("at_qkt", [P, QKT], F), ("y_hi", [P, 3, 4, T], FR), ("y_lo", [P, 3, 4, T], FR))
        arena = sb("arena", [P, KEYS * T])
        ps = ctx.enter_context(nc.psum_tensor("ps", [P, 8, 512], F))

        def view(off, *shape):
            n = int(np.prod(shape))
            v = arena[:, off:off + n]
            names = "abcd"[:len(shape)]
            if len(shape) == 1:
                return v
            spec = f"p ({' '.join(names)}) -> p {' '.join(names)}"
            return v.rearrange(spec, **dict(zip(names, shape)))

        tok = view(TOK, 6, TT, 512)
        vals = view(VV, 3, TT, 512)
        qkT = view(QKT, 6, 4, T)
        gates = view(GATE, 24, T)
        yT = view(YT, 3, 4, T)
        merged = view(MRG, KC, T)
        xs = view(MRG, TT, D)
        bias = view(BIAS, B_HEADS, T)
        subT = view(BIAS, 16, P)
        sq = view(QKT, 8, 512)
        nsq = view(SCR, TT, D)
        cz = view(SCR, 6, 512)
        positive = [view(at, 3, 512) for at in (TOK + 4096, MRG + 512)]
        ce = view(YT, 6, 512)
        sring = view(SRING, 3, 2, 256)
        ptr = view(PTR, 2, 512)
        ysq = view(YSQ, 2, 512)
        yan = view(YAN, 2, 512)
        upt = view(UPT, 2, 512)
        pqT = view(PQT, 16, T)
        scores = view(SSB, TT, 16, P)
        cand = view(CAND, 8, 16, 16)
        eq = view(EQ, 8, 16, 16)
        eq2 = view(EQ2, 8, 16, 16)
        topv = view(TOPV, TT, 16, 16)
        topi = view(TOPI, TT, 16, 16).bitcast(U32)
        topf = view(TOPF, TT, 16, 16)
        bestv = view(BV, TT, 8, 16)
        bestp = view(BP, TT, 8, 16).bitcast(U32)
        pab = view(PAB, 2, 8, 16).bitcast(U32)
        pabf = view(PABF, 2, 8, 16)
        bd = view(BEST_D, TT, 128)
        rt_tok = view(0, TT, 3, P)
        G = view(0, KEYS, T)
        htmp = view(TOK, 4, 512)
        par = view(PAR, N_PAR)
        strict, below, ones = (view(MASKS + P * k, P) for k in range(3))
        rope_t = view(ROPE, 2, 8, 16)
        lam_w = view(LAMW, 2, HD)
        nmax, rsum, rinv = (view(MRG + 384 + 32 * k, 16, 2) for k in range(3))

        x_loaded = sem("x_loaded")
        w_loaded = [Signal(sem(f"w_loaded{s}"), ROUNDS * 16) for s in range(SLOTS)]
        hi_ready = Signal(sem("hi_ready"), N_HI, SLOTS)
        w_ready = Signal(sem("w_ready"), N_DVE, SLOTS)
        early_ready = Signal(sem("early_ready"), N_EARLY)
        early_mm = Signal(sem("early_mm"), EARLY)
        early_gelu = Signal(sem("early_gelu"), EARLY, 2)
        full_ready = Signal(sem("full_ready"), 1)
        fill_mm = Signal(sem("fill_mm"), FILL)
        fill_gelu = Signal(sem("fill_gelu"), FILL, 2)
        fill_used = Signal(sem("fill_used"), FILL, 2)
        part_ready = Signal(sem("part_ready"), 64)
        part_used = Signal(sem("part_used"), 64, 2)
        w_used = Signal(sem("w_used"), N_USED)
        masks_ready = Signal(sem("masks_ready"), 1)
        y_split = Signal(sem("y_split"), 3)
        x_parked = Signal(sem("x_parked"), 1)
        par_loaded = Signal(sem("par_loaded"), 16)
        bias_loaded = Signal(sem("bias_loaded"), 16)
        subk_loaded = Signal(sem("subk_loaded"), 16)
        constants = sem("constants")
        layer_done = Signal(sem("layer_done"), 2, 2)
        squared = Signal(sem("squared"), 4)
        rstd_ready = Signal(sem("rstd_ready"), 4)
        xs_ready = Signal(sem("xs_ready"), 4)
        normT_mm = Signal(sem("normT_mm"), 8)
        gained = Signal(sem("gained"), 8)
        hT_hi_ready = Signal(sem("hT_hi_ready"), 8)
        hT_ready = Signal(sem("hT_ready"), 8)
        proj_mm = Signal(sem("proj_mm"), 48)
        proj_ev = Signal(sem("proj_ev"), 48)
        sq_ready = Signal(sem("sq_ready"), 8)
        ss_ready = Signal(sem("ss_ready"), 8)
        qkrs_ready = Signal(sem("qkrs_ready"), 8)
        qk_normed = Signal(sem("qk_normed"), 8)
        logs_ready = Signal(sem("logs_ready"), 2)
        logs_summed = Signal(sem("logs_summed"), 2)
        keep_ready = Signal(sem("keep_ready"), 2)
        later_mm = Signal(sem("later_mm"), 6)
        loga_ready = Signal(sem("loga_ready"), 6)
        a_exp = Signal(sem("a_exp"), 6)
        a_ready = Signal(sem("a_ready"), 6)
        cout_mm = Signal(sem("cout_mm"), 2)
        yc_ready = Signal(sem("yc_ready"), 2)
        score_mm = Signal(sem("score_mm"), 16)
        smax_ready = Signal(sem("smax_ready"), 16)
        exp_ready = Signal(sem("exp_ready"), 16)
        prob_ready = Signal(sem("prob_ready"), 16)
        probT_mm = Signal(sem("probT_mm"), 16)
        probT_ready = Signal(sem("probT_ready"), 16)
        mix_mm = Signal(sem("mix_mm"), 16)
        ya_sq = Signal(sem("ya_sq"), 2)
        ya_ssr = Signal(sem("ya_ssr"), 2)
        ya_rsr = Signal(sem("ya_rsr"), 2)
        ya_normed = Signal(sem("ya_normed"), 2)
        yaT_mm = Signal(sem("yaT_mm"), 2)
        ya_ready = Signal(sem("ya_ready"), 2)
        yb_ready = Signal(sem("yb_ready"), 2)
        lam_sum = Signal(sem("lam_sum"), 1)
        lam_exp = Signal(sem("lam_exp"), 1)
        bias_ready = Signal(sem("bias_ready"), 1)
        gate_ready = Signal(sem("gate_ready"), 3)
        up_mm = Signal(sem("up_mm"), 12)
        up_taken = Signal(sem("up_taken"), 12)
        merged_ready = Signal(sem("merged_ready"), 4)
        wout_mm = Signal(sem("wout_mm"), 4)
        x_mid = Signal(sem("x_mid"), 4)
        pq_mm = Signal(sem("pq_mm"), 8)
        pq_ready = Signal(sem("pq_ready"), 8)
        s_mm = Signal(sem("s_mm"), 8)
        s_ready = Signal(sem("s_ready"), 8)
        best_ready = Signal(sem("best_ready"), 2)
        best_exp = Signal(sem("best_exp"), 2)
        rt_ready = Signal(sem("rt_ready"), 2)
        rtT_mm = Signal(sem("rtT_mm"), 2)
        route_ready = Signal(sem("route_ready"), 2)
        hot_ready = Signal(sem("hot_ready"), 32)
        g_mm = Signal(sem("g_mm"), 64, 4)
        g_ready = Signal(sem("g_ready"), 64, 4)
        h_mm = Signal(sem("h_mm"), LATE, 2)
        gelu_ready = Signal(sem("gelu_ready"), LATE, 2)
        wgt_ready = Signal(sem("wgt_ready"), PAIRS, 2)
        v_mm = Signal(sem("v_mm"), PAIRS, 2)
        dve_chain, act_chain, pool_chain = sem("dve_chain"), sem("act_chain"), sem("pool_chain")
        dve_loop = sem("dve_loop")
        seen_sp, seen_dve, seen_pool, seen_pe = sem("seen_sp"), sem("seen_dve"), sem("seen_pool"), sem("seen_pe")
        stored = sem("stored")

        M_CT, M_G0, M_CZ, M_G4, M_ABT, M_G8 = 18, 22, 26, 32, 36, 44

        def proj_bank(m):
            if m >= M_G8:
                return (1, 1, 0, 1)[m - M_G8]
            return m % 8 if m < 18 else (m - 18) % 4

        def gate_m(g):
            return (M_G0, M_G4, M_G8)[g // 4] + g % 4

        def used(n):
            if n < N_QKV:
                cb, k = n // 4, n % 4
                return (proj_mm, 2 * cb + 2) if k == 3 else (w_used, 3 * cb + k + 1)
            n -= N_QKV
            if n < N_GATE:
                return (proj_mm, gate_m(n // 2) + 1) if n % 2 else (w_used, 27 + n // 2 + 1)
            n -= N_GATE
            if n < N_BR:
                return up_mm, n + 1
            n -= N_BR
            if n < N_OUT:
                return (wout_mm, 2 * (n // 4) + 2) if n % 4 == 3 else (w_used, 39 + 3 * (n // 4) + n % 4 + 1)
            n -= N_OUT
            return (pq_mm, n // 2 + 1) if n % 2 else (w_used, 45 + n // 2 + 1)

        SCORE_BANK = (2, 6)
        GATE_STEPS = (0, 1, 2, 3, 7, 8, 11, 12)

        def by_head(i):
            return (i % 8) // 4, i % 4

        def c_heads(c):
            if c < 2:
                return 1, c, [c + 2 * j for j in range(4)]
            par_, g = (c - 2) % 2, (c - 2) // 2
            return 0, par_, [par_ + 4 * g, par_ + 4 * g + 2]

        block = ctx.enter_context(nc.Block())

        @block.sync
        def _(sp):
            sp.dma_start(x[:], x_in).then_inc(x_loaded, 16)

            def load(layer, n, slot, source, signal=w_ready):
                sp.wait_ge(signal.sem, signal.at(layer, n))
                sp.sem_inc(seen_sp, 1)
                sp.dma_start(raw[:, slot, :], source).then_inc(w_loaded[slot].sem, 16)

            with sp.Fori(0, LAYERS) as layer:
                with sp.Fori(0, N_STREAM // SLOTS) as r:
                    for k in range(SLOTS):
                        load(layer, r * SLOTS + (k + 1 - SLOTS), k,
                             stream[bass.ds(layer * N_STREAM + (r * SLOTS + k), 1), :, :].rearrange(
                                 "a p n -> p (a n)"))

                def load_u(j, n, slot, signal=w_ready):
                    load(layer, n, slot, w_u[bass.ds(layer * KEYS + j, 1), :, :].rearrange("a p n -> p (a n)"), signal)

                def load_v(j, n, slot):
                    load(layer, n, slot, w_v[bass.ds(layer, 1), :, bass.ds(j, 1), :].rearrange(
                        "a p b n -> p (a b n)"))

                for i in range(SLOTS):
                    load_u(KEYS - N_EARLY + i, N_STREAM + i + 1 - SLOTS, i)
                with sp.Fori(1, N_EARLY // SLOTS) as r:
                    for i in range(SLOTS):
                        load_u(r * SLOTS + (KEYS - N_EARLY + i), r * SLOTS + (i + 1 - SLOTS), i, early_ready)
                for i in range(SLOTS):
                    load_u(2 * LATE + i, N_EARLY + i + 1 - SLOTS, i, early_ready)
                with sp.Fori(1, 2 * FILL // SLOTS) as r:
                    for i in range(SLOTS):
                        load_u(r * SLOTS + (2 * LATE + i), r * 2 + (i // 2 - 1), i, fill_mm)
                for i in range(SLOTS):
                    load_u(i, FILL - 1 + i // 2, i, fill_mm)
                for e in range(2):
                    load_v(e, N_STREAM + 1 + e, e)
                with sp.Fori(1, LATE - 1) as p:
                    for e in range(2):
                        load_u(p * 2 + (2 + e), p * 4 + (N_STREAM - 1 + e), 2 + e)
                    for e in range(2):
                        load_v(p * 2 + e, p * 4 + (N_STREAM + 1 + e), e)
                for e in range(2):
                    load_v(2 * LATE - 2 + e, N_V - 5 + e, 2 + e)
                with sp.Fori(0, KEPT // 2) as r:
                    for i in range(SLOTS):
                        load_v(r * SLOTS + (2 * LATE + i), r * SLOTS + (N_V + i + 1 - SLOTS), i)
            sp.wait_ge(layer_done.sem, layer_done.at(LAYERS, 0))
            sp.dma_start(out, x[:]).then_inc(stored, 16)
            sp.wait_ge(stored, 16)

        @block.gpsimd
        def _(pool):
            own = Count()

            def fill(t, value):
                own.one(nc.gpsimd.memset(t, value).then_inc(pool_chain, 1))

            fill(ident[:], 0.0)
            fill(blockmask[:], 0.0)
            fill(half_neg[:], -0.5)
            pool.wait_ge(pool_chain, own.n)
            own.one(nc.gpsimd.affine_select(out=ident[:], in_=ident[:], compare_op=ALU.not_equal, fill=1.0,
                                              base=0, pattern=[[-1, P]], channel_multiplier=1).then_inc(pool_chain, 1))
            own.one(nc.gpsimd.memset(blockmask[0:64, P + 64:2 * P], NEG).then_inc(pool_chain, 1))
            own.one(nc.gpsimd.iota(iota[:], pattern=[[1, P]], base=0, channel_multiplier=0,
                                     allow_small_or_imprecise_dtypes=True).then_inc(pool_chain, 1))
            pool.wait_ge(pool_chain, own.n)
            pool.sem_inc(constants, 1)
            pool.wait_ge(pool_chain, own.n)
            pool.sem_clear(pool_chain)
            own.n = 0

            for s in (part_used, fill_used):
                pool.sem_inc(s.sem, s.start)
            with pool.Fori(0, LAYERS) as layer:
                pool.wait_ge(layer_done.sem, layer_done.at(layer, 0))
                pool.sem_inc(seen_pool, 1)
                def inverse_root(dst, src, count, wait_for, n, ready):
                    pool.wait_ge(wait_for.sem, wait_for.at(layer, n))
                    pool.sem_inc(seen_pool, 1)
                    own.one(nc.gpsimd.tensor_scalar(dst, src, 1.0 / count, EPS, ALU.mult, ALU.add).then_inc(pool_chain, 1))
                    pool.wait_ge(pool_chain, own.n)
                    nc.gpsimd.tensor_tensor(dst, dst, half_neg[:, 0:dst.shape[-1]], ALU.pow
                                            ).then_inc(ready.sem, 1)

                for t in range(TT):
                    inverse_root(rstd[:, t:t + 1], ssq[:, t:t + 1], D, squared, t + 1, rstd_ready)
                for mask in (ones, strict, below):
                    own.one(nc.gpsimd.memset(mask, 1.0).then_inc(pool_chain, 1))
                pool.wait_ge(pool_chain, own.n)
                own.one(nc.gpsimd.affine_select(out=strict, in_=strict, compare_op=ALU.is_gt, fill=0.0, base=0,
                                                pattern=[[1, P]], channel_multiplier=-1).then_inc(pool_chain, 1))
                nc.gpsimd.affine_select(out=below, in_=below, compare_op=ALU.is_gt, fill=0.0, base=0,
                                        pattern=[[-1, P]], channel_multiplier=1).then_inc(masks_ready.sem, 1)
                pool.wait_ge(bias_loaded.sem, bias_loaded.at(layer, 16))
                pool.sem_inc(seen_pool, 1)
                nc.gpsimd.tensor_tensor(bias[:], bias[:],
                                        blockmask[:].unsqueeze(1).broadcast_to([P, B_HEADS, 2 * P]),
                                        ALU.add).then_inc(bias_ready.sem, 1)
                def mask_keeps():
                    for i in range(2):
                        pool.wait_ge(logs_summed.sem, logs_summed.at(layer, i + 1))
                        pool.sem_inc(seen_pool, 1)
                        if i == 0:
                            pool.wait_ge(masks_ready.sem, masks_ready.at(layer, 1))
                            pool.sem_inc(seen_pool, 1)
                            blocks = ce[:, 0:2, :].rearrange("p a (h q) -> p (a h) q", q=P)
                            nc.gpsimd.tensor_tensor(blocks, blocks, strict.unsqueeze(1).broadcast_to([P, 8, P]),
                                                    ALU.mult)
                            blocks = ce[:, 2, :].rearrange("p (h q) -> p h q", q=T)[:, :, 0:P]
                        else:
                            blocks = ce[:, 3:6, :].rearrange("p a (h q) -> p (a h) q", q=T)[:, :, 0:P]
                        nc.gpsimd.tensor_tensor(blocks, blocks,
                                                strict.unsqueeze(1).broadcast_to([P, blocks.shape[1], P]), ALU.mult
                                                ).then_inc(keep_ready.sem, 1)

                for i in range(8):
                    inverse_root(qk_rs[:, i, :], qk_ss[:, i, :], HD, ss_ready, i + 1, qkrs_ready)
                mask_keeps()
                for t in range(TT):
                    inverse_root(ya_rs[:, t, :], ya_ss[:, t, :], P, ya_ssr, t + 1, ya_rsr)
                for t in range(TT):
                    inverse_root(rstd[:, t:t + 1], ssq[:, t:t + 1], D, squared, TT + t + 1, rstd_ready)
                own.one(nc.gpsimd.memset(G[:, 2 * LATE:2 * (LATE + FILL), :], 1.0).then_inc(pool_chain, 1))
                with pool.Fori(0, N_EARLY // SLOTS) as r:
                    for i in range(SLOTS):
                        pool.wait_ge(hi_ready.sem, hi_ready.at(layer, r * SLOTS + (N_STREAM + i + 1)))
                        pool.sem_inc(seen_pool, 1)
                        nc.gpsimd.tensor_tensor(w_lo[:, i, :], raw[:, i, :], w_hi[:, i, :].bitcast(F), ALU.subtract
                                                ).then_inc(early_ready.sem, 1)
                pool.wait_ge(early_mm.sem, early_mm.at(layer, EARLY - 1))
                pool.sem_inc(seen_pool, 1)
                nc.gpsimd.tensor_tensor(hT_full[:], hT_hi[:].bitcast(F), hT_lo[:].bitcast(F), ALU.add
                                        ).then_inc(full_ready.sem, 1)
                pool.wait_ge(pool_chain, own.n)
                with pool.Fori(0, FILL // 2) as it:
                    for k in range(2):
                        for b in range(8):
                            pool.wait_ge(part_ready.sem, part_ready.at(layer, it * 16 + (8 * k + b + 1)))
                            pool.sem_inc(seen_pool, 1)
                            kept = G[:, 2 * LATE:KEYS, bass.ds(it * 64 + (32 * k + 4 * b), 4)]
                            nc.gpsimd.tensor_tensor(kept, kept, (g_part_a, g_part_b)[b % 2][:], ALU.mult
                                                    ).then_inc(part_used.sem, 1)
                            if b == FILL_TAKEN:
                                pool.wait_ge(fill_gelu.sem, fill_gelu.at(layer, it * 2 + (k + 1)))
                                pool.sem_inc(seen_pool, 1)
                                pool.wait_ge(part_used.sem, part_used.at(layer, it * 16 + (8 * k + b + 1)))
                                pool.sem_inc(seen_pool, 1)
                                pair = G[:, bass.ds(it * 4 + (2 * LATE + 2 * k), 2), :]
                                nc.gpsimd.tensor_tensor(pair, pair, fill_h[:, k, :].rearrange("p (a b) -> p a b", a=2),
                                                        ALU.mult).then_inc(fill_used.sem, 1)
                                pool.wait_ge(fill_used.sem, fill_used.at(layer, it * 2 + (k + 1)))
                                pool.sem_inc(seen_pool, 1)
                pool.wait_ge(pool_chain, own.n)
                pool.sem_clear(pool_chain)
                own.n = 0

        @block.tensor
        def _(pe):
            mm = nc.tensor.matmul
            for s in (h_mm, v_mm, g_mm):
                pe.sem_inc(s.sem, s.start)

            def product(out_, left, right, start, stop, group=False):
                mm(out_, left[0], right[0], start=start, stop=False, skip_group_check=group)
                mm(out_, left[0], right[1], start=False, stop=False, skip_group_check=group)
                return mm(out_, left[1], right[0], start=False, stop=stop, skip_group_check=group)

            pe.wait_ge(constants, 1)

            def transposes(dst, src, count):
                for q in range(count):
                    last = nc.tensor.transpose(dst[:, q * P:(q + 1) * P], src[:, q * P:(q + 1) * P], ident[:])
                return last

            with pe.Fori(0, LAYERS) as layer:
                def norm_transposes(which):
                    for n in range(4):
                        t, half = n // 2, n % 2
                        if half == 0:
                            pe.wait_ge(xs_ready.sem, xs_ready.at(layer, 2 * which + t + 1))
                        transposes(ps[:, n, :], xs[:, t, half * 512:(half + 1) * 512], 4
                                   ).then_inc(normT_mm.sem, 1)

                def by_token(lhs, bank, n0, signal, first_wait, lhs_wait=lambda k: None):
                    for k in range(4):
                        pe.wait_ge(w_ready.sem, w_ready.at(layer, n0 + k + 1))
                        lhs_wait(k)
                        for t in range(TT):
                            if k == 0:
                                first_wait(t)
                            for kc in range(2):
                                last = product(ps[:, bank(t), :],
                                               [a[:, 2 * k + kc, t * P:(t + 1) * P] for a in lhs],
                                               [w[:, (n0 + k) % SLOTS, kc * 512:(kc + 1) * 512] for w in (w_hi, w_lo)],
                                               start=(k == 0 and kc == 0), stop=(k == 3 and kc == 1))
                            if k == 3:
                                last.then_inc(signal.sem, 1)
                        if k < 3:
                            last.then_inc(w_used.sem, 1)

                def by_feature(bank, n0, signal, parts=(0, 1)):
                    for c2 in parts:
                        pe.wait_ge(w_ready.sem, w_ready.at(layer, n0 + c2 + 1))
                        for kc in range(KC):
                            last = product(ps[:, bank, c2 * T:(c2 + 1) * T],
                                           [w[:, (n0 + c2) % SLOTS, kc * P:(kc + 1) * P] for w in (w_hi, w_lo)],
                                           [h[:, kc, :] for h in (hT_hi, hT_lo)], start=(kc == 0), stop=(kc == KC - 1))
                        last.then_inc((w_used if c2 == 0 else signal).sem, 1)

                norm_transposes(0)
                pe.wait_ge(hT_ready.sem, hT_ready.at(layer, 4))
                for cb in range(9):
                    def bank_free(t):
                        if 2 * cb + t >= 8:
                            pe.wait_ge(proj_ev.sem, proj_ev.at(layer, 2 * cb + t - 7))
                    by_token((hT_hi, hT_lo), lambda t: proj_bank(2 * cb + t), 4 * cb, proj_mm, bank_free)

                def feature_tile(m, ten, t):
                    transposes(ps[:, proj_bank(m), :], tok[:, ten, t, :], 4).then_inc(proj_mm.sem, 1)

                for r in range(4):
                    pe.wait_ge(proj_ev.sem, proj_ev.at(layer, 18))
                    feature_tile(M_CT + r, 4 + r // 2, r % 2)

                def gate_tiles(g0):
                    for g in range(g0, g0 + 4):
                        pe.wait_ge(proj_ev.sem, proj_ev.at(layer, gate_m(g) - 3))
                        by_feature(proj_bank(gate_m(g)), N_QKV + 2 * g, proj_mm)

                gate_tiles(0)
                for c in range(6):
                    kt, par_, heads = c_heads(c)
                    pe.wait_ge(proj_ev.sem, proj_ev.at(layer, M_CZ + c - 3))
                    n = (2 - kt) * P
                    for j, h in enumerate(heads):
                        rows = slice(64 * par_, 64 * par_ + 64)
                        last = mm(ps[:, proj_bank(M_CZ + c), j * n:(j + 1) * n],
                                  qkT[rows, 5, h // 2, kt * P:(kt + 1) * P], qkT[rows, 4, h // 2, kt * P:T],
                                  start=True, stop=True)
                    last.then_inc(proj_mm.sem, 1)
                gate_tiles(4)
                pe.wait_ge(masks_ready.sem, masks_ready.at(layer, 1))
                for c in range(6):
                    kt, par_, heads = c_heads(c)
                    pe.wait_ge(keep_ready.sem, keep_ready.at(layer, 1 if c < 3 else 2))
                    if c >= 2:
                        pe.wait_ge(loga_ready.sem, loga_ready.at(layer, c - 1))
                    last = mm(ps[:, 4 + c % 2, :], below, ce[:, c, :], start=True, stop=(kt == 1))
                    if kt == 0:
                        g = (c - 2) // 2
                        last = mm(ps[:, 4 + c % 2, :].rearrange("p (h q) -> p h q", h=2)[:, :, P:T], ones,
                                  ce[:, par_, 2 * g * P:(2 * g + 2) * P].rearrange("p (h q) -> p h q", h=2),
                                  start=False, stop=True)
                    last.then_inc(later_mm.sem, 1)
                for r in range(8):
                    pe.wait_ge(proj_ev.sem, proj_ev.at(layer, M_ABT + r - 3))
                    pe.wait_ge(qk_normed.sem, qk_normed.at(layer, r + 1))
                    feature_tile(M_ABT + r, r // 2, r % 2)
                pe.wait_ge(a_ready.sem, a_ready.at(layer, 6))
                for o in range(2):
                    for h in range(4 * o, 4 * o + 4):
                        par_, rows = h % 2, slice(64 * (h % 2), 64 * (h % 2) + 64)
                        at = ((h // 2) % 2) * T
                        mm(ps[rows, 4 + o, at:at + T], vals[:, 2, 0, h * HD:(h + 1) * HD],
                           cz[:, 2 + par_ + 2 * (h // 4), ((h // 2) % 2) * T:((h // 2) % 2 + 1) * T],
                           start=True, stop=False)
                        last = mm(ps[rows, 4 + o, at + P:at + T], vals[:, 2, 1, h * HD:(h + 1) * HD],
                                  cz[:, par_, (h // 2) * P:(h // 2 + 1) * P], start=False, stop=True)
                    last.then_inc(cout_mm.sem, 1)

                def score(i):
                    t, ch = by_head(i)
                    q_, k_ = (0, 1) if i < 8 else (2, 3)
                    for c in range(2):
                        rows = slice(64 * c, 64 * c + 64)
                        last = mm(ps[:, SCORE_BANK[i % 2] + c, 0:(t + 1) * P],
                                  qkT[rows, q_, ch, t * P:(t + 1) * P], qkT[rows, k_, ch, 0:(t + 1) * P],
                                  start=True, stop=True)
                    last.then_inc(score_mm.sem, 1)

                def prob_transposes(i):
                    t, _ = by_head(i)
                    pe.wait_ge(prob_ready.sem, prob_ready.at(layer, i + 1))
                    if i >= 2:
                        pe.wait_ge(probT_ready.sem, probT_ready.at(layer, i - 1))
                    elif i == 0:
                        pe.wait_ge(yc_ready.sem, yc_ready.at(layer, 2))
                    for c in range(1 if i < 8 else 2):
                        last = transposes(ps[:, 4 + i % 2, c * (t + 1) * P:(c + 1) * (t + 1) * P],
                                          sring[:, i % 3, c, :], t + 1)
                    last.then_inc(probT_mm.sem, 1)

                def mix(i):
                    t, ch = by_head(i)
                    pe.wait_ge(probT_ready.sem, probT_ready.at(layer, i + 1))
                    if i >= 8 and ch == 0:
                        pe.wait_ge(ya_normed.sem, ya_normed.at(layer, t + 1))
                    if i < 8:
                        for kt in range(t + 1):
                            last = mm(ps[:, t, ch * P:(ch + 1) * P], ptr[:, i % 2, kt * P:(kt + 1) * P],
                                      vals[:, 0, kt, ch * P:(ch + 1) * P], start=(kt == 0), stop=(kt == t))
                    else:
                        for c in range(2):
                            h = 2 * ch + c
                            for kt in range(t + 1):
                                at = (c * (t + 1) + kt) * P
                                last = mm(ps[64 * c:64 * c + 64, t, ch * P:(ch + 1) * P],
                                          vals[:, 1, kt, h * HD:(h + 1) * HD], ptr[:, i % 2, at:at + P],
                                          start=(kt == 0), stop=(kt == t))
                    last.then_inc(mix_mm.sem, 1)

                pe.wait_ge(proj_ev.sem, proj_ev.at(layer, 44))
                score(0)
                score(1)
                for i in range(16):
                    if i + 2 < 16:
                        pe.wait_ge(smax_ready.sem, smax_ready.at(layer, i + 1))
                        score(i + 2)
                    prob_transposes(i)
                    if i:
                        mix(i - 1)
                    if i in GATE_STEPS:
                        g, c2 = 8 + GATE_STEPS.index(i) // 2, GATE_STEPS.index(i) % 2
                        if c2 == 0:
                            pe.wait_ge(proj_ev.sem, proj_ev.at(layer, gate_m(g)))
                            if g >= 10:
                                pe.wait_ge(ya_normed.sem, ya_normed.at(layer, g - 9))
                        by_feature(proj_bank(gate_m(g)), N_QKV + 2 * g, proj_mm, (c2,))
                mix(15)
                pe.wait_ge(probT_ready.sem, probT_ready.at(layer, 16))
                for t in range(TT):
                    pe.wait_ge(ya_normed.sem, ya_normed.at(layer, t + 1))
                    transposes(ps[:, 4 + t, :], yan[:, t, :], 4).then_inc(yaT_mm.sem, 1)

                pe.wait_ge(yb_ready.sem, yb_ready.at(layer, 2))
                for u in range(12):
                    n = N_QKV + N_GATE + u
                    if u % 4 == 0:
                        pe.wait_ge(y_split.sem, y_split.at(layer, u // 4 + 1))
                    if u >= 4:
                        pe.wait_ge(up_taken.sem, up_taken.at(layer, u - 3))
                    pe.wait_ge(w_ready.sem, w_ready.at(layer, n + 1))
                    for c2 in range(2):
                        for wc in range(4):
                            at = wc * 256 + c2 * P
                            last = product(ps[:, u % 4, c2 * T:(c2 + 1) * T],
                                           [w[:, n % SLOTS, at:at + P] for w in (w_hi, w_lo)],
                                           [y[:, UP_ORDER[u // 4], wc, :] for y in (y_hi, y_lo)],
                                           start=(wc == 0), stop=(wc == 3))
                    last.then_inc(up_mm.sem, 1)
                for c in range(2):
                    by_token((m_hi, m_lo), lambda t: 4 + 2 * c + t, N_STREAM - N_WQ - N_OUT + 4 * c, wout_mm,
                             lambda t: None,
                             lambda k: pe.wait_ge(merged_ready.sem, merged_ready.at(layer, k + 1)) if c == 0 else None)

                norm_transposes(1)
                pe.wait_ge(hT_ready.sem, hT_ready.at(layer, 8))
                for n in range(N_WQ // 2):
                    if n >= 4:
                        pe.wait_ge(pq_ready.sem, pq_ready.at(layer, n - 3))
                    by_feature(4 + n % 4, N_STREAM - N_WQ + 2 * n, pq_mm)
                pe.wait_ge(subk_loaded.sem, subk_loaded.at(layer, 16))
                pe.wait_ge(pq_ready.sem, pq_ready.at(layer, 8))
                for n in range(8):
                    for q in range(4):
                        ch = (n % 4) * 4 + q
                        last = mm(ps[:, n, q * P:(q + 1) * P], pqT[:, ch, (n // 4) * P:(n // 4 + 1) * P],
                                  subT[:, ch, :], start=True, stop=True)
                    last.then_inc(s_mm.sem, 1)
                pe.wait_ge(s_ready.sem, s_ready.at(layer, 8))
                for n in range(4):
                    last = mm(ps[:, 4 + n, :], ident[:], x[:, n // 2, (n % 2) * 512:(n % 2 + 1) * 512],
                              start=True, stop=False, skip_group_check=True)
                last.then_inc(x_parked.sem, 1)
                with pe.Fori(0, EARLY // 2) as r:
                    for k in range(2):
                        pe.wait_ge(early_gelu.sem, early_gelu.at(layer, r * 2 + (k - 1)))
                        for e in range(2):
                            pe.wait_ge(early_ready.sem, early_ready.at(layer, r * SLOTS + (2 * k + e + 1)))
                            for kc in range(KC):
                                last = product(ps[:, 2 + k, e * T:(e + 1) * T],
                                               [w[:, 2 * k + e, kc * P:(kc + 1) * P] for w in (w_hi, w_lo)],
                                               [h[:, kc, :] for h in (hT_hi, hT_lo)], start=(kc == 0),
                                               stop=(kc == KC - 1))
                        last.then_inc(early_mm.sem, 1)
                for t in range(TT):
                    pe.wait_ge(rt_ready.sem, rt_ready.at(layer, t + 1))
                    transposes(ps[:, t, :], rt_tok[:, t, :, :].rearrange("p a b -> p (a b)"), 3
                               ).then_inc(rtT_mm.sem, 1)

                pe.wait_ge(early_gelu.sem, early_gelu.at(layer, EARLY))
                pe.wait_ge(route_ready.sem, route_ready.at(layer, 2))
                pe.wait_ge(full_ready.sem, full_ready.at(layer, 1))
                pe.sem_inc(seen_pe, 1)
                with pe.Fori(0, FILL // 2) as it:
                    for k in range(2):
                        for b in range(8):
                            group = (b // 2) % 2
                            if b % 2 == 0:
                                pe.wait_ge(hot_ready.sem, hot_ready.at(layer, it * 8 + (4 * k + b // 2 + 1)))
                            pe.wait_ge(g_ready.sem, g_ready.at(layer, it * 16 + (8 * k + b - 1)))
                            for q in range(4):
                                for part in range(3):
                                    last = mm(ps[:, b % 2, q * P:(q + 1) * P],
                                              hot_w[group][:, part, :, (b % 2) * 4 + q],
                                              hot[group][:, 1, :, (b % 2) * 4 + q], start=(part == 0), stop=(part == 2))
                            last.then_inc(g_mm.sem, 1)
                            if b in FILL_AT:
                                e = FILL_AT.index(b)
                                w = w_loaded[2 * k + e]
                                pe.wait_ge(fill_gelu.sem, fill_gelu.at(layer, it * 2 + (k - 1)))
                                pe.wait_ge(w.sem, w.at(layer, it * 16 + 16 * ((N_STREAM + N_EARLY) // SLOTS + 1)))
                                for kc in range(KC):
                                    last = mm(ps[:, 2 + k, e * T:(e + 1) * T],
                                              raw[:, 2 * k + e, kc * P:(kc + 1) * P], hT_full[:, kc, :],
                                              start=(kc == 0), stop=(kc == KC - 1))
                                if e == 1:
                                    last.then_inc(fill_mm.sem, 1)

                def hidden(p, k, slot, n):
                    pe.wait_ge(gelu_ready.sem, gelu_ready.at(layer, p - 1))
                    for e in range(2):
                        pe.wait_ge(w_ready.sem, w_ready.at(layer, n + (e + 1)))
                        for kc in range(KC):
                            last = product(ps[:, k, e * T:(e + 1) * T],
                                           [w[:, slot + e, kc * P:(kc + 1) * P] for w in (w_hi, w_lo)],
                                           [h[:, kc, :] for h in (hT_hi, hT_lo)], start=(kc == 0), stop=(kc == KC - 1))
                    last.then_inc(h_mm.sem, 1)

                def expert_out(p, k, slot, n, final=False):
                    pe.wait_ge(wgt_ready.sem, wgt_ready.at(layer, p + 1))
                    for e in range(2):
                        pe.wait_ge(w_ready.sem, w_ready.at(layer, n + (e + 1)))
                        for t in range(TT):
                            for half in range(2):
                                last = product(ps[:, 4 + 2 * t + half, :],
                                               [w[:, k, e * T + t * P:e * T + (t + 1) * P] for w in (wgt_hi, wgt_lo)],
                                               [w[:, slot + e, half * 512:(half + 1) * 512] for w in (w_hi, w_lo)],
                                               start=False, stop=(final and e == 1), group=True)
                    last.then_inc(v_mm.sem, 1)

                def u_and_v(p, k):
                    hidden(p + 1, 1 - k, 2, p * 4 + (N_STREAM + 2))
                    expert_out(p, k, 0, p * 4 + (N_STREAM + 4))

                pe.wait_ge(g_ready.sem, g_ready.at(layer, 64))
                hidden(0, 0, 0, N_STREAM)
                u_and_v(0, 0)
                with pe.Fori(0, LATE // 2 - 1) as it:
                    u_and_v(it * 2 + 1, 1)
                    u_and_v(it * 2 + 2, 0)
                expert_out(LATE - 1, 1, 2, N_V - 2)
                with pe.Fori(0, KEPT // 2 - 1) as it:
                    for k in range(2):
                        expert_out(it * 2 + (LATE + k), k, 2 * k, it * SLOTS + (N_V + 2 * k))
                expert_out(PAIRS - 2, 0, 0, N_DVE - 4)
                expert_out(PAIRS - 1, 1, 2, N_DVE - 2, final=True)

        @block.scalar
        def _(act):
            f = nc.scalar.activation
            own = Count()
            for s in (g_ready, gelu_ready, hi_ready, early_gelu, fill_gelu):
                act.sem_inc(s.sem, s.start)
            act.wait_ge(x_loaded, 16)
            act.wait_ge(constants, 1)

            with act.Fori(0, LAYERS) as layer:
                def load_small():
                    act.wait_ge(wgt_ready.sem, wgt_ready.at(layer, 0))
                    act.dma_start(par[:], params[bass.ds(layer, 1), :, :].rearrange("a p n -> p (a n)")
                                  ).then_inc(par_loaded.sem, 16)
                    act.dma_start(bias[:].rearrange("p a b -> p (a b)"),
                                  bias_in[bass.ds(layer, 1), :, :].rearrange("a p n -> p (a n)")
                                  ).then_inc(bias_loaded.sem, 16)

                def split(n):
                    if n < SLOTS:
                        act.wait_ge(v_mm.sem, v_mm.at(layer, n // 2 - 1))
                    else:
                        sig, count = used(n - SLOTS)
                        act.wait_ge(sig.sem, sig.at(layer, count))
                    w = w_loaded[n % SLOTS]
                    act.wait_ge(w.sem, w.at(layer, 16 * (n // SLOTS + 1)))
                    f(w_hi[:, n % SLOTS, :], raw[:, n % SLOTS, :], ACT.Copy).then_inc(hi_ready.sem, 1)

                def square_sums(done, n):
                    for t in range(TT):
                        act.wait_ge(done.sem, done.at(layer, n + t))
                        f(nsq[:, t, :], x[:, t, :], ACT.Square, accum_out=ssq[:, t:t + 1]
                          ).then_inc(squared.sem, 1)

                def norm_rows(which):
                    for t in range(TT):
                        act.wait_ge(rstd_ready.sem, rstd_ready.at(layer, 2 * which + t + 1))
                        f(xs[:, t, :], x[:, t, :], ACT.Copy, scale=rstd[:, t:t + 1]).then_inc(xs_ready.sem, 1)
                    for n in range(4):
                        t, half = n // 2, n % 2
                        act.wait_ge(gained.sem, gained.at(layer, 4 * which + n + 1))
                        f(hT_hi[:, 4 * half:4 * half + 4, t * P:(t + 1) * P],
                          htmp[:, n, :].rearrange("p (a b) -> p a b", a=4), ACT.Copy).then_inc(hT_hi_ready.sem, 1)

                load_small()
                for n in range(SLOTS):
                    split(n)
                square_sums(layer_done, -1)
                norm_rows(0)
                act.wait_ge(lam_sum.sem, lam_sum.at(layer, 1))
                f(lam[:, 2:4], lam[:, 0:2], ACT.Exp).then_inc(lam_exp.sem, 1)
                normed = {0: 0, 1: 1, 3: 2, 4: 3}
                where = {0: tok[:, 0], 1: tok[:, 1], 2: vals[:, 0], 3: tok[:, 2], 4: tok[:, 3],
                         5: vals[:, 1], 6: tok[:, 4], 7: tok[:, 5], 8: vals[:, 2]}
                for m in range(18):
                    cb, t = m // 2, m % 2
                    if t == 0:
                        for k in range(4):
                            split(4 * cb + k + SLOTS)
                    act.wait_ge(proj_mm.sem, proj_mm.at(layer, m + 1))
                    if cb in normed:
                        f(sq[:, 2 * normed[cb] + t, :], ps[:, proj_bank(m), :], ACT.Square
                          ).then_inc(sq_ready.sem, 1)
                    f(where[cb][:, t, :], ps[:, proj_bank(m), :], ACT.Copy).then_inc(proj_ev.sem, 1)

                def take_feature_tile(m, ten, t):
                    act.wait_ge(proj_mm.sem, proj_mm.at(layer, m + 1))
                    f(qkT[:, ten, :, t * P:(t + 1) * P], ps[:, proj_bank(m), :].rearrange("p (a b) -> p a b", a=4),
                      ACT.Copy).then_inc(proj_ev.sem, 1)

                def take_gate(g):
                    act.wait_ge(proj_mm.sem, proj_mm.at(layer, gate_m(g) + 1))
                    f(gates[:, 2 * g:2 * g + 2, :], ps[:, proj_bank(gate_m(g)), :].rearrange(
                        "p (a b) -> p a b", a=2), ACT.Copy).then_inc(proj_ev.sem, 1)

                def take_gates(g0):
                    for g in range(g0, g0 + 4):
                        for k in range(2):
                            split(N_QKV + 2 * g + k + SLOTS)
                        take_gate(g)

                for r in range(4):
                    take_feature_tile(M_CT + r, 4 + r // 2, r % 2)
                take_gates(0)
                for c in range(6):
                    act.wait_ge(proj_mm.sem, proj_mm.at(layer, M_CZ + c + 1))
                    own.one(f(ce[:, c, :], ps[:, proj_bank(M_CZ + c), :], ACT.Abs, scale=SCALE).then_inc(act_chain, 1))
                    f(cz[:, c, :], ps[:, proj_bank(M_CZ + c), :], ACT.Copy, scale=SCALE
                      ).then_inc(proj_ev.sem, 1)
                following = iter(range(N_QKV + 8 + SLOTS, N_QKV + 16 + SLOTS))
                act.wait_ge(act_chain, own.n)
                for i in range(2):
                    own.one(f(ce[:, 3 * i:3 * i + 3, :], ce[:, 3 * i:3 * i + 3, :], ACT.Exp, scale=-1.0).then_inc(act_chain, 1))
                    split(next(following))
                for i in range(2):
                    f(positive[i][:], cz[:, 3 * i:3 * i + 3, :], ACT.Relu)
                    act.wait_ge(act_chain, own.n)
                    f(ce[:, 3 * i:3 * i + 3, :], ce[:, 3 * i:3 * i + 3, :], ACT.Ln, bias=1.0
                      ).then_inc(logs_ready.sem, 1)
                    split(next(following))
                for n in following:
                    split(n)
                for g in range(4, 8):
                    take_gate(g)
                for c in range(6):
                    act.wait_ge(loga_ready.sem, loga_ready.at(layer, c + 1))
                    f(cz[:, c, :], cz[:, c, :], ACT.Exp).then_inc(a_exp.sem, 1)
                act.wait_ge(ss_ready.sem, ss_ready.at(layer, 8))
                for r in range(8):
                    take_feature_tile(M_ABT + r, r // 2, r % 2)
                for o in range(2):
                    act.wait_ge(cout_mm.sem, cout_mm.at(layer, o + 1))
                    f(yT[:, 2, 2 * o:2 * o + 2, :], ps[:, 4 + o, :].rearrange("p (a b) -> p a b", a=2),
                      ACT.Copy).then_inc(yc_ready.sem, 1)

                def take_probT(i):
                    t, _ = by_head(i)
                    n = (1 if i < 8 else 2) * (t + 1) * P
                    act.wait_ge(probT_mm.sem, probT_mm.at(layer, i + 1))
                    if i >= 2:
                        act.wait_ge(mix_mm.sem, mix_mm.at(layer, i - 1))
                    f(ptr[:, i % 2, 0:n], ps[:, 4 + i % 2, 0:n], ACT.Copy).then_inc(probT_ready.sem, 1)

                def take_yb(t):
                    act.wait_ge(mix_mm.sem, mix_mm.at(layer, 12 + 4 * t))
                    f(yT[:, 1, :, t * P:(t + 1) * P], ps[:, t, :].rearrange("p (a b) -> p a b", a=4), ACT.Copy
                      ).then_inc(yb_ready.sem, 1)

                for i in range(16):
                    t, _ = by_head(i)
                    act.wait_ge(smax_ready.sem, smax_ready.at(layer, i + 1))
                    for c in range(2):
                        s = sring[:, i % 3, c, 0:(t + 1) * P]
                        last = f(s, s, ACT.Exp, bias=nmax[:, i, c:c + 1], accum_out=rsum[:, i, c:c + 1])
                    last.then_inc(exp_ready.sem, 1)
                    if i - 1 in GATE_STEPS[1::2]:
                        take_gate(8 + GATE_STEPS.index(i - 1) // 2)
                    if i:
                        take_probT(i - 1)
                    if i - 1 in GATE_STEPS:
                        split(N_QKV + 16 + GATE_STEPS.index(i - 1) + SLOTS)
                    if i in (5, 9):
                        t = (i - 5) // 4
                        act.wait_ge(mix_mm.sem, mix_mm.at(layer, 4 * (t + 1)))
                        f(ysq[:, t, :], ps[:, t, :], ACT.Square).then_inc(ya_sq.sem, 1)
                    if i == 14:
                        take_yb(0)
                act.dma_start(subT[:].rearrange("p a b -> p (a b)"),
                              subk[bass.ds(layer, 1), :, :].rearrange("a p n -> p (a n)")
                              ).then_inc(subk_loaded.sem, 16)
                take_probT(15)
                take_yb(1)
                act.wait_ge(proj_ev.sem, proj_ev.at(layer, 48))
                for b in UP_ORDER:
                    f(gates[:, 8 * b:8 * b + 8, :], gates[:, 8 * b:8 * b + 8, :], ACT.Sigmoid
                      ).then_inc(gate_ready.sem, 1)
                for n in range(N_STREAM - N_WQ - N_OUT - N_BR, N_STREAM - N_WQ):
                    split(n + SLOTS)
                square_sums(x_mid, 3)
                norm_rows(1)
                def split_e(slot, rnd, sig, count):
                    act.wait_ge(sig.sem, sig.at(layer, count))
                    act.wait_ge(w_loaded[slot].sem, w_loaded[slot].at(layer, rnd * 16 + 16))
                    f(w_hi[:, slot, :], raw[:, slot, :], ACT.Copy).then_inc(hi_ready.sem, 1)

                for n in range(N_WQ // 2):
                    if n < 6:
                        for k in range(2):
                            split(N_STREAM - N_WQ + 2 * n + k + SLOTS)
                    if n == 7:
                        for e in range(2):
                            split_e(e, N_STREAM // SLOTS, *used(N_STREAM - SLOTS + e))
                    act.wait_ge(pq_mm.sem, pq_mm.at(layer, n + 1))
                    f(pqT[:, 2 * n:2 * n + 2, :], ps[:, 4 + n % 4, :].rearrange("p (a b) -> p a b", a=2),
                      ACT.Copy).then_inc(pq_ready.sem, 1)
                for n in range(8):
                    act.wait_ge(s_mm.sem, s_mm.at(layer, n + 1))
                    f(scores[:, n // 4, (n % 4) * 4:(n % 4) * 4 + 4, :],
                      ps[:, n, :].rearrange("p (a b) -> p a b", a=4), ACT.Copy).then_inc(s_ready.sem, 1)
                def early_pair(q, k, rnd, first=False):
                    for e in range(2):
                        sig, count = used(N_STREAM - 2 + e) if first else (early_mm, q)
                        split_e(2 * (1 - k) + e, rnd, sig, count)
                    act.wait_ge(early_mm.sem, early_mm.at(layer, q + 1))
                    at = KEYS - N_EARLY
                    f(G[:, at:at + 2, :] if first else G[:, bass.ds(q * 2 + at, 2), :],
                      ps[:, 2 + k, :].rearrange("p (a b) -> p a b", a=2), ACT.Gelu).then_inc(early_gelu.sem, 1)

                def early_pairs(q0, count):
                    with act.Fori(0, count // 2) as r:
                        for k in range(2):
                            early_pair(r * 2 + (q0 + k), 1 - k, r + (N_STREAM // SLOTS + (q0 + k + 1) // 2))

                def exponents(t):
                    act.wait_ge(best_ready.sem, best_ready.at(layer, t + 1))
                    f(bd[:, t, :], bd[:, t, :], ACT.Exp).then_inc(best_exp.sem, 1)

                early_pair(0, 0, N_STREAM // SLOTS, first=True)
                early_pairs(1, 10)
                exponents(0)
                early_pairs(11, EARLY - 12)
                exponents(1)
                act.wait_ge(early_mm.sem, early_mm.at(layer, EARLY))
                f(G[:, KEYS - 2:KEYS, :], ps[:, 3, :].rearrange("p (a b) -> p a b", a=2), ACT.Gelu
                  ).then_inc(early_gelu.sem, 1)
                for t in range(TT):
                    act.wait_ge(rtT_mm.sem, rtT_mm.at(layer, t + 1))
                    f(route[:, :, t * P:(t + 1) * P], ps[:, t, 0:3 * P].rearrange("p (a b) -> p a b", a=3),
                      ACT.Copy).then_inc(route_ready.sem, 1)
                with act.Fori(0, FILL // 2) as it:
                    for k in range(2):
                        for b in range(8):
                            act.wait_ge(g_mm.sem, g_mm.at(layer, it * 16 + (8 * k + b + 1)))
                            act.wait_ge(part_used.sem, part_used.at(layer, it * 16 + (8 * k + b - 1)))
                            tokens = ps[:, b % 2, :].rearrange("p (t j) -> p j t", t=4)
                            f((g_part_a, g_part_b)[b % 2][:], tokens[:, 2 * LATE:KEYS, :], ACT.Copy
                              ).then_inc(part_ready.sem, 1)
                            f(G[:, 0:2 * LATE, bass.ds(it * 64 + (32 * k + 4 * b), 4)], tokens[:, 0:2 * LATE, :],
                              ACT.Copy).then_inc(g_ready.sem, 1)
                            if b == FILL_TAKEN:
                                act.wait_ge(fill_mm.sem, fill_mm.at(layer, it * 2 + (k + 1)))
                                act.wait_ge(fill_used.sem, fill_used.at(layer, it * 2 + (k - 1)))
                                f(fill_h[:, k, :], ps[:, 2 + k, :], ACT.Gelu).then_inc(fill_gelu.sem, 1)

                FIRST = (N_STREAM + N_EARLY + 2 * FILL) // SLOTS

                def experts(p, k, first=False):
                    rnd = p + FIRST
                    for e in range(2):
                        sig, count = (fill_mm, FILL) if first else (h_mm, p + 1)
                        split_e(2 + e, rnd, sig, count)
                    act.wait_ge(h_mm.sem, h_mm.at(layer, p + 1))
                    act.wait_ge(wgt_ready.sem, wgt_ready.at(layer, p - 1))
                    f(act_h[:, k, :], ps[:, k, :], ACT.Gelu).then_inc(gelu_ready.sem, 1)
                    for e in range(2):
                        sig, count = (h_mm, 1) if first else (v_mm, p)
                        split_e(e, rnd + 1, sig, count)

                for e in range(2):
                    split_e(e, FIRST, fill_mm, FILL)
                act.wait_ge(part_used.sem, part_used.at(layer, 64))
                experts(0, 0, first=True)
                with act.Fori(0, LATE // 2 - 1) as it:
                    for k in range(2):
                        experts(it * 2 + (k + 1), 1 - k)
                for e in range(2):
                    split_e(2 + e, FIRST + LATE - 1, h_mm, LATE)
                act.wait_ge(h_mm.sem, h_mm.at(layer, LATE))
                f(act_h[:, 1, :], ps[:, 1, :], ACT.Gelu).then_inc(gelu_ready.sem, 1)
                with act.Fori(0, KEPT // 2) as it:
                    for k in range(2):
                        for e in range(2):
                            split_e(2 * k + e, it + (FIRST + LATE), v_mm, it * 2 + (LATE - 1 + k))
                act.wait_ge(act_chain, own.n)
                act.sem_clear(act_chain)
                own.n = 0

        @block.vector
        def _(dve):
            v = nc.vector
            own = Count()
            for s in (wgt_ready, layer_done, w_ready):
                dve.sem_inc(s.sem, s.start)
            dve.wait_ge(x_loaded, 16)
            dve.wait_ge(constants, 1)

            with dve.Fori(0, LAYERS) as layer:
                def split(n):
                    for i in n:
                        dve.wait_ge(hi_ready.sem, hi_ready.at(layer, i + 1))
                        v.tensor_tensor(w_lo[:, i % SLOTS, :], raw[:, i % SLOTS, :],
                                        w_hi[:, i % SLOTS, :].bitcast(F), ALU.subtract).then_inc(w_ready.sem, 1)

                def norm(which):
                    if which == 0:
                        split((2, 3))
                    for n in range(4):
                        t, half = n // 2, n % 2
                        dve.wait_ge(normT_mm.sem, normT_mm.at(layer, 4 * which + n + 1))
                        gain = par[:, (C_N1, C_N2)[which] + 4 * half:(C_N1, C_N2)[which] + 4 * half + 4]
                        v.tensor_tensor(htmp[:, n, :].rearrange("p (a b) -> p a b", a=4),
                                        ps[:, n, :].rearrange("p (a b) -> p a b", a=4),
                                        gain.unsqueeze(2).broadcast_to([P, 4, P]), ALU.mult).then_inc(gained.sem, 1)
                    for n in range(4):
                        t, half = n // 2, n % 2
                        hi, lo = (h[:, 4 * half:4 * half + 4, t * P:(t + 1) * P] for h in (hT_hi, hT_lo))
                        dve.wait_ge(gained.sem, gained.at(layer, 4 * which + n + 1))
                        dve.wait_ge(hT_hi_ready.sem, hT_hi_ready.at(layer, 4 * which + n + 1))
                        v.tensor_tensor(lo, htmp[:, n, :].rearrange("p (a b) -> p a b", a=4), hi.bitcast(F),
                                        ALU.subtract).then_inc(hT_ready.sem, 1)

                split((0, 1))
                dve.wait_ge(par_loaded.sem, par_loaded.at(layer, 16))
                dve.sem_inc(seen_dve, 1)
                norm(0)
                dve.wait_ge(normT_mm.sem, normT_mm.at(layer, 4))
                own.one(v.tensor_tensor(lam_w[:], par[:, C_LAM:C_LAM + 128].rearrange("p (a b) -> p a b", a=2),
                                        par[:, C_LAM + 128:C_LAM + 256].rearrange("p (a b) -> p a b", a=2),
                                        ALU.mult).then_inc(dve_chain, 1))
                dve.wait_ge(dve_chain, own.n)
                v.tensor_reduce(lam[:, 0:2], lam_w[:], AX.X, ALU.add).then_inc(lam_sum.sem, 1)
                dve.wait_ge(lam_exp.sem, lam_exp.at(layer, 1))
                own.one(v.tensor_tensor(lam[:, 4:5], lam[:, 2:3], lam[:, 3:4], ALU.subtract).then_inc(dve_chain, 1))
                dve.wait_ge(dve_chain, own.n)
                own.one(v.tensor_scalar(lam[:, 5:6], lam[:, 4:5], par[:, C_LAMI:C_LAMI + 1], -1.0,
                                        ALU.add, ALU.mult).then_inc(dve_chain, 1))

                def head_sums(i):
                    dve.wait_ge(sq_ready.sem, sq_ready.at(layer, i + 1))
                    v.tensor_reduce(qk_ss[:, i, :], sq[:, i, :].rearrange("p (h d) -> p h d", h=8), AX.X, ALU.add
                                    ).then_inc(ss_ready.sem, 1)

                evacuated = [1, 2, 3, 4, 7, 8, 9, 10]

                def head_norm(i):
                    ten, t = i // 2, i % 2
                    z = tok[:, ten, t, :].rearrange("p (h d) -> p h d", h=8)
                    dve.wait_ge(qkrs_ready.sem, qkrs_ready.at(layer, i + 1))
                    dve.wait_ge(proj_ev.sem, proj_ev.at(layer, evacuated[i]))
                    own.one(v.tensor_tensor(z, z, qk_rs[:, i, :].unsqueeze(2).broadcast_to([P, 8, HD]), ALU.mult).then_inc(dve_chain, 1))
                    dve.wait_ge(dve_chain, own.n)
                    gain = par[:, C_GAIN + HD * ten:C_GAIN + HD * (ten + 1)]
                    last = v.tensor_tensor(z, z, gain.unsqueeze(1).broadcast_to([P, 8, HD]), ALU.mult)
                    if ten < 2:
                        own.one(last.then_inc(dve_chain, 1))
                        dve.wait_ge(dve_chain, own.n)
                        pair = tok[:, ten, t, :].rearrange("p (h d) -> p h d", h=8)[:, :, 0:16].rearrange(
                            "p h (a d) -> p h a d", a=2)
                        if i:
                            dve.wait_ge(qk_normed.sem, qk_normed.at(layer, i))
                        for j, col in enumerate((C_COS, C_SIN)):
                            tab = par[:, col + 8 * t:col + 8 * t + 8]
                            own.one(v.tensor_tensor(rope_t[:, j, :, :].rearrange("p h (a d) -> p h a d", a=2), pair,
                                                      tab.unsqueeze(1).unsqueeze(1).broadcast_to([P, 8, 2, 8]),
                                                      ALU.mult).then_inc(dve_chain, 1))
                        dve.wait_ge(dve_chain, own.n)
                        v.tensor_tensor(z[:, :, 0:8], rope_t[:, 0, :, 0:8], rope_t[:, 1, :, 8:16], ALU.subtract)
                        last = v.tensor_tensor(z[:, :, 8:16], rope_t[:, 0, :, 8:16], rope_t[:, 1, :, 0:8], ALU.add)
                    last.then_inc(qk_normed.sem, 1)

                summed = 0
                for cb in range(9):
                    split(range(4 * cb + SLOTS, 4 * cb + 2 * SLOTS))
                    if cb in (1, 2, 4, 5):
                        for t in range(TT):
                            head_sums(summed)
                            if summed:
                                head_norm(summed - 1)
                            summed += 1
                    if cb == 6:
                        head_norm(7)
                for n in range(N_QKV, N_QKV + 8, 2):
                    split((n + SLOTS, n + 1 + SLOTS))

                following = iter(range(N_QKV + 8 + SLOTS, N_QKV + 16 + SLOTS))
                for _ in range(2):
                    split((next(following),))

                for i in range(2):
                    part = slice(3 * i, 3 * i + 3)
                    dve.wait_ge(logs_ready.sem, logs_ready.at(layer, i + 1))
                    if i == 0:
                        dve.sem_inc(seen_dve, 1)
                    flat = ce[:, part, :].rearrange("p a b -> p (a b)")
                    zflat = cz[:, part, :].rearrange("p a b -> p (a b)")
                    own.one(v.scalar_tensor_tensor(out=flat, in0=positive[i][:].rearrange("p a b -> p (a b)"), scalar=-1.0,
                                                     in1=flat, op0=ALU.mult, op1=ALU.subtract).then_inc(dve_chain, 1))
                    split((next(following),))
                    dve.wait_ge(dve_chain, own.n)
                    v.tensor_tensor(zflat, zflat, flat, ALU.add).then_inc(logs_summed.sem, 1)
                split(following)
                for c in range(6):
                    dve.wait_ge(later_mm.sem, later_mm.at(layer, c + 1))
                    v.tensor_tensor(cz[:, c, :], cz[:, c, :], ps[:, 4 + c % 2, :], ALU.add
                                    ).then_inc(loga_ready.sem, 1)
                dve.wait_ge(masks_ready.sem, masks_ready.at(layer, 1))
                for c in range(6):
                    dve.wait_ge(a_exp.sem, a_exp.at(layer, c + 1))
                    n = P if c < 2 else T
                    blocks = cz[:, c, :].rearrange("p (h q) -> p h q", q=n)[:, :, 0:P]
                    v.tensor_tensor(blocks, blocks, strict.unsqueeze(1).broadcast_to([P, 512 // n, P]), ALU.mult
                                    ).then_inc(a_ready.sem, 1)

                dve.wait_ge(bias_ready.sem, bias_ready.at(layer, 1))
                dve.sem_inc(seen_dve, 1)

                def score_max(i):
                    t, ch = by_head(i)
                    n, off = (t + 1) * P, (1 - t) * P
                    s = sring[:, i % 3, :, 0:n]
                    if i >= 3:
                        dve.wait_ge(probT_mm.sem, probT_mm.at(layer, i - 2))
                    dve.wait_ge(score_mm.sem, score_mm.at(layer, i + 1))
                    add = (blockmask[:, off:off + n].unsqueeze(1).broadcast_to([P, 2, n]) if i < 8
                           else bias[:, 2 * ch:2 * ch + 2, off:off + n])
                    own.one(v.scalar_tensor_tensor(out=s, in0=ps[:, SCORE_BANK[i % 2]:SCORE_BANK[i % 2] + 2, 0:n],
                                                     scalar=SCALE, in1=add, op0=ALU.mult, op1=ALU.add).then_inc(dve_chain, 1))
                    dve.wait_ge(dve_chain, own.n)
                    v.tensor_reduce(nmax[:, i, :], s, AX.X, ALU.max, negate=True).then_inc(smax_ready.sem, 1)

                def probabilities(i):
                    t, _ = by_head(i)
                    s = [sring[:, i % 3, c, 0:(t + 1) * P] for c in range(2)]
                    dve.wait_ge(exp_ready.sem, exp_ready.at(layer, i + 1))
                    own.one(v.reciprocal(rinv[:, i, :], rsum[:, i, :]).then_inc(dve_chain, 1))
                    dve.wait_ge(dve_chain, own.n)
                    if i < 8:
                        own.one(v.tensor_scalar(rinv[:, i, 1:2], rinv[:, i, 1:2], lam[:, 5:6], None, ALU.mult).then_inc(dve_chain, 1))
                        own.one(v.tensor_scalar(s[0], s[0], rinv[:, i, 0:1], None, ALU.mult).then_inc(dve_chain, 1))
                        dve.wait_ge(dve_chain, own.n)
                        last = v.scalar_tensor_tensor(out=s[0], in0=s[1], scalar=rinv[:, i, 1:2], in1=s[0],
                                                      op0=ALU.mult, op1=ALU.add)
                    else:
                        v.tensor_scalar(s[0], s[0], rinv[:, i, 0:1], None, ALU.mult)
                        last = v.tensor_scalar(s[1], s[1], rinv[:, i, 1:2], None, ALU.mult)
                    last.then_inc(prob_ready.sem, 1)

                def ya_sums(t):
                    dve.wait_ge(ya_sq.sem, ya_sq.at(layer, t + 1))
                    v.tensor_reduce(ya_ss[:, t, :], ysq[:, t, :].rearrange("p (h d) -> p h d", h=4), AX.X, ALU.add
                                    ).then_inc(ya_ssr.sem, 1)

                def ya_norm(t):
                    dve.wait_ge(ya_rsr.sem, ya_rsr.at(layer, t + 1))
                    v.tensor_tensor(yan[:, t, :].rearrange("p (h d) -> p h d", h=4),
                                    ps[:, t, :].rearrange("p (h d) -> p h d", h=4),
                                    ya_rs[:, t, :].unsqueeze(2).broadcast_to([P, 4, P]), ALU.mult
                                    ).then_inc(ya_normed.sem, 1)

                score_max(0)
                score_max(1)
                for i in range(16):
                    probabilities(i)
                    if i + 2 < 16:
                        score_max(i + 2)
                    if i - 2 in GATE_STEPS:
                        split((N_QKV + 16 + GATE_STEPS.index(i - 2) + SLOTS,))
                    if i in (5, 9):
                        ya_sums((i - 5) // 4)
                    if i in (6, 10):
                        ya_norm((i - 6) // 4)
                def split_outputs(b, done):
                    dve.wait_ge(done.sem, done.at(layer, 2))
                    own.one(v.tensor_copy(y_hi[:, b, :, :], yT[:, b, :, :]).then_inc(dve_chain, 1))
                    dve.wait_ge(dve_chain, own.n)
                    v.tensor_tensor(y_lo[:, b, :, :], yT[:, b, :, :], y_hi[:, b, :, :].bitcast(F), ALU.subtract
                                    ).then_inc(y_split.sem, 1)

                split_outputs(2, yc_ready)
                for t in range(TT):
                    dve.wait_ge(yaT_mm.sem, yaT_mm.at(layer, t + 1))
                    v.tensor_scalar(yT[:, 0, :, t * P:(t + 1) * P], ps[:, 4 + t, :].rearrange("p (a b) -> p a b", a=4),
                                    par[:, C_SUB:C_SUB + 1], par[:, C_OML:C_OML + 1], ALU.mult, ALU.mult
                                    ).then_inc(ya_ready.sem, 1)

                split_outputs(1, yb_ready)
                split_outputs(0, ya_ready)

                for u in range(12):
                    split((N_STREAM - N_WQ - N_OUT - N_BR + u + SLOTS,))
                    d0 = (u % 4) * 2
                    b = UP_ORDER[u // 4]
                    if u % 4 == 0:
                        dve.wait_ge(gate_ready.sem, gate_ready.at(layer, u // 4 + 1))
                    dve.wait_ge(up_mm.sem, up_mm.at(layer, u + 1))
                    part = merged[:, d0:d0 + 2, :]
                    dst = part if u < 4 else upt[:, u % 2, :].rearrange("p (a b) -> p a b", a=2)
                    v.tensor_tensor(dst, ps[:, u % 4, :].rearrange("p (a b) -> p a b", a=2),
                                    gates[:, 8 * b + d0:8 * b + d0 + 2, :], ALU.mult).then_inc(up_taken.sem, 1)
                    if u >= 4:
                        dve.wait_ge(up_taken.sem, up_taken.at(layer, u + 1))
                        dve.wait_ge(dve_chain, own.n)
                        own.one(v.tensor_tensor(part, part, dst, ALU.add).then_inc(dve_chain, 1))
                    if u >= 8:
                        hi, lo = m_hi[:, d0:d0 + 2, :], m_lo[:, d0:d0 + 2, :]
                        dve.wait_ge(dve_chain, own.n)
                        own.one(v.tensor_copy(hi, part).then_inc(dve_chain, 1))
                        dve.wait_ge(dve_chain, own.n)
                        v.tensor_tensor(lo, part, hi.bitcast(F), ALU.subtract).then_inc(merged_ready.sem, 1)
                def add_out(n):
                    c, t = n // 2, n % 2
                    dve.wait_ge(wout_mm.sem, wout_mm.at(layer, n + 1))
                    v.tensor_tensor(x[:, t, c * 512:(c + 1) * 512], x[:, t, c * 512:(c + 1) * 512],
                                    ps[:, 4 + n, :], ALU.add).then_inc(x_mid.sem, 1)

                for n in range(N_OUT):
                    split((N_STREAM - N_WQ - N_OUT + n + SLOTS,))
                    if n in (5, 6):
                        add_out(n - 5)
                add_out(2)
                add_out(3)
                norm(1)
                for n in range(12):
                    split((N_STREAM - N_WQ + n + SLOTS,))

                def top(values, best, where_):
                    for r, vals_ in enumerate(values):
                        own.one(v.max(best[r][:, 0:8], vals_).then_inc(dve_chain, 1))
                    dve.wait_ge(dve_chain, own.n)
                    for r, vals_ in enumerate(values):
                        own.one(v.max_index(where_[r][:, 0:8], best[r][:, 0:8], vals_).then_inc(dve_chain, 1))
                    dve.wait_ge(dve_chain, own.n)
                    for r, vals_ in enumerate(values):
                        own.one(v.match_replace(vals_, best[r][:, 0:8], vals_, -3.0e38).then_inc(dve_chain, 1))
                    dve.wait_ge(dve_chain, own.n)
                    for r, vals_ in enumerate(values):
                        own.one(v.max(best[r][:, 8:16], vals_).then_inc(dve_chain, 1))
                    dve.wait_ge(dve_chain, own.n)
                    for r, vals_ in enumerate(values):
                        own.one(v.max_index(where_[r][:, 8:16], best[r][:, 8:16], vals_).then_inc(dve_chain, 1))
                    dve.wait_ge(dve_chain, own.n)

                def choose(t):
                    dve.wait_ge(s_ready.sem, s_ready.at(layer, 4 * (t + 1)))
                    dve.sem_inc(seen_dve, 1)
                    top([scores[:, t, ch, :] for ch in range(16)], [topv[:, t, ch, :] for ch in range(16)],
                        [topi[:, t, ch, :] for ch in range(16)])
                    halves = topv[:, t, :, :].rearrange("p (h s) k -> p h s k", s=2)
                    own.one(v.tensor_copy(topf[:, t, :, :], topi[:, t, :, :]).then_inc(dve_chain, 1))
                    own.one(v.tensor_tensor(cand[:], halves[:, :, 0, :].unsqueeze(3).broadcast_to([P, 8, 16, 16]),
                                              halves[:, :, 1, :].unsqueeze(2).broadcast_to([P, 8, 16, 16]), ALU.add).then_inc(dve_chain, 1))
                    dve.wait_ge(dve_chain, own.n)
                    top([cand[:, h, :, :].rearrange("p a b -> p (a b)") for h in range(8)],
                        [bestv[:, t, h, :] for h in range(8)], [bestp[:, t, h, :] for h in range(8)])
                    v.tensor_tensor(bd[:, t, :].rearrange("p (h k) -> p h k", h=8), bestv[:, t, :, :],
                                    bestv[:, t, :, 0:1].broadcast_to([P, 8, 16]), ALU.subtract
                                    ).then_inc(best_ready.sem, 1)

                def places(t):
                    if t == 0:
                        dve.wait_ge(s_ready.sem, s_ready.at(layer, 8))
                        dve.sem_inc(seen_dve, 1)
                    own.one(v.tensor_scalar(pab[:, 0, :, :], bestp[:, t, :, :], 4, None, ALU.logical_shift_right).then_inc(dve_chain, 1))
                    own.one(v.tensor_scalar(pab[:, 1, :, :], bestp[:, t, :, :], 15, None, ALU.bitwise_and).then_inc(dve_chain, 1))
                    dve.wait_ge(dve_chain, own.n)
                    own.one(v.tensor_copy(pabf[:], pab[:]).then_inc(dve_chain, 1))
                    dve.wait_ge(dve_chain, own.n)
                    keys = topf[:, t, :, :].rearrange("p (h s) k -> p h s k", s=2)
                    for s, e in ((0, eq), (1, eq2)):
                        own.one(v.tensor_tensor(e[:], pabf[:, s, :, :].unsqueeze(3).broadcast_to([P, 8, 16, 16]),
                                                  iota[:, 0:16].unsqueeze(1).unsqueeze(1).broadcast_to([P, 8, 16, 16]),
                                                  ALU.is_equal).then_inc(dve_chain, 1))
                    dve.wait_ge(dve_chain, own.n)
                    for s, e in ((0, eq), (1, eq2)):
                        own.one(v.tensor_tensor(e[:], e[:], keys[:, :, s, :].unsqueeze(2).broadcast_to([P, 8, 16, 16]),
                                                  ALU.mult).then_inc(dve_chain, 1))
                    dve.wait_ge(dve_chain, own.n)
                    for s, e in ((0, eq), (1, eq2)):
                        own.one(v.tensor_reduce(rt_tok[:, t, s, :].rearrange("p (h k) -> p h k", h=8), e[:], AX.X,
                                                  ALU.add).then_inc(dve_chain, 1))

                def weights(t):
                    dve.wait_ge(best_exp.sem, best_exp.at(layer, t + 1))
                    if t:
                        dve.wait_ge(rt_ready.sem, rt_ready.at(layer, t))
                    own.one(v.tensor_reduce(gsum[:], bd[:, t, :].rearrange("p (h k) -> p h k", h=8), AX.X, ALU.add).then_inc(dve_chain, 1))
                    dve.wait_ge(dve_chain, own.n)
                    own.one(v.reciprocal(ginv[:], gsum[:]).then_inc(dve_chain, 1))
                    dve.wait_ge(dve_chain, own.n)
                    v.tensor_tensor(rt_tok[:, t, 2, :].rearrange("p (h k) -> p h k", h=8),
                                    bd[:, t, :].rearrange("p (h k) -> p h k", h=8),
                                    ginv[:].unsqueeze(2).broadcast_to([P, 8, 16]), ALU.mult
                                    ).then_inc(rt_ready.sem, 1)

                choose(0)
                places(0)
                choose(1)
                weights(0)
                places(1)
                weights(1)

                dve.wait_ge(x_parked.sem, x_parked.at(layer, 1))
                dve.sem_inc(seen_dve, 1)
                own.one(v.tensor_copy(key_of[:], iota[:].unsqueeze(2).broadcast_to([P, KEYS, GROUP])
                                      ).then_inc(dve_chain, 1))
                dve.wait_ge(early_mm.sem, early_mm.at(layer, EARLY))
                dve.sem_inc(seen_dve, 1)
                dve.wait_ge(route_ready.sem, route_ready.at(layer, 2))
                dve.sem_inc(seen_dve, 1)
                own.one(v.tensor_copy(keys_b[:], route[:, 0:2, :]).then_inc(dve_chain, 1))
                for part in range(3):
                    dve.wait_ge(dve_chain, own.n)
                    own.one(v.tensor_copy(weight_parts[:, part, :], route[:, 2, :]).then_inc(dve_chain, 1))
                    if part < 2:
                        dve.wait_ge(dve_chain, own.n)
                        own.one(v.tensor_tensor(route[:, 2, :], route[:, 2, :], weight_parts[:, part, :],
                                                ALU.subtract).then_inc(dve_chain, 1))
                dve.wait_ge(dve_chain, own.n)
                with dve.Fori(0, T // 16) as it:
                    for k in range(2):
                        tokens = bass.ds(it * 16 + k * GROUP, GROUP)
                        dve.wait_ge(g_mm.sem, g_mm.at(layer, it * 4 + (2 * k - 2)))
                        dve.sem_inc(seen_dve, 1)
                        v.tensor_tensor(hot[k][:], key_of[:].unsqueeze(1).broadcast_to([P, 2, KEYS, GROUP]),
                                        keys_b[:, :, tokens].unsqueeze(2).broadcast_to([P, 2, KEYS, GROUP]),
                                        ALU.is_equal).then_inc(dve_loop, 1)
                        dve.wait_ge(dve_loop, 1)
                        dve.sem_clear(dve_loop)
                        v.tensor_tensor(hot_w[k][:], hot[k][:, 0:1, :, :].broadcast_to([P, 3, KEYS, GROUP]),
                                        weight_parts[:, :, tokens].unsqueeze(2).broadcast_to([P, 3, KEYS, GROUP]),
                                        ALU.mult).then_inc(hot_ready.sem, 1)

                def split_e(n, slot):
                    dve.wait_ge(hi_ready.sem, hi_ready.at(layer, n + (N_EARLY + 1)))
                    v.tensor_tensor(w_lo[:, slot, :], raw[:, slot, :], w_hi[:, slot, :].bitcast(F), ALU.subtract
                                    ).then_inc(w_ready.sem, 1)

                def weigh(p, k, at):
                    dve.wait_ge(gelu_ready.sem, gelu_ready.at(layer, p + 1))
                    a = act_h[:, k, :].rearrange("p (a b) -> p a b", a=2)
                    v.tensor_tensor(a, a, G[:, at, :], ALU.mult).then_inc(dve_loop, 1)
                    dve.wait_ge(dve_loop, 1)
                    dve.sem_inc(seen_dve, 1)
                    dve.wait_ge(v_mm.sem, v_mm.at(layer, p - 1))
                    v.tensor_copy(wgt_hi[:, k, :], act_h[:, k, :]).then_inc(dve_loop, 1)
                    dve.wait_ge(dve_loop, 2)
                    dve.sem_clear(dve_loop)
                    v.tensor_tensor(wgt_lo[:, k, :], act_h[:, k, :], wgt_hi[:, k, :].bitcast(F), ALU.subtract
                                    ).then_inc(wgt_ready.sem, 1)

                def experts(p, k, at):
                    for e in range(2):
                        split_e(p * 4 + (N_STREAM + 2 + e), 2 + e)
                    weigh(p, k, at)
                    for e in range(2):
                        split_e(p * 4 + (N_STREAM + 4 + e), e)

                dve.wait_ge(g_ready.sem, g_ready.at(layer, 64))
                dve.sem_inc(seen_dve, 1)
                dve.wait_ge(fill_used.sem, fill_used.at(layer, FILL))
                dve.sem_inc(seen_dve, 1)
                for e in range(2):
                    split_e(N_STREAM + e, e)
                experts(0, 0, slice(0, 2))
                with dve.Fori(0, LATE // 2 - 1) as it:
                    for k in range(2):
                        experts(it * 2 + (k + 1), 1 - k, bass.ds(it * 4 + 2 * (k + 1), 2))
                for e in range(2):
                    split_e(N_V - 2 + e, 2 + e)
                weigh(LATE - 1, 1, slice(2 * LATE - 2, 2 * LATE))
                dve.wait_ge(part_used.sem, part_used.at(layer, 64))
                dve.sem_inc(seen_dve, 1)
                with dve.Fori(0, KEPT // 2) as it:
                    for k in range(2):
                        at = bass.ds(it * 4 + (2 * LATE + 2 * k), 2)
                        dve.wait_ge(v_mm.sem, v_mm.at(layer, it * 2 + (LATE + k - 1)))
                        v.tensor_copy(wgt_hi[:, k, :].rearrange("p (a b) -> p a b", a=2), G[:, at, :]
                                      ).then_inc(dve_loop, 1)
                        dve.wait_ge(dve_loop, 1)
                        dve.sem_clear(dve_loop)
                        v.tensor_tensor(wgt_lo[:, k, :].rearrange("p (a b) -> p a b", a=2), G[:, at, :],
                                        wgt_hi[:, k, :].bitcast(F).rearrange("p (a b) -> p a b", a=2), ALU.subtract
                                        ).then_inc(wgt_ready.sem, 1)
                        for e in range(2):
                            split_e(it * SLOTS + (N_V + 2 * k + e), 2 * k + e)
                dve.wait_ge(v_mm.sem, v_mm.at(layer, PAIRS))
                for t in range(TT):
                    v.tensor_copy(x[:, t, :].rearrange("p (a b) -> p a b", a=2), ps[:, 4 + 2 * t:6 + 2 * t, :]
                                  ).then_inc(layer_done.sem, 1)
                dve.wait_ge(dve_chain, own.n)
                dve.sem_clear(dve_chain)
                own.n = 0


def kernel(x, norm1_g, w_in, a_qnorm_g, a_knorm_g, lam_q1, lam_k1, lam_q2, lam_k2, a_subln_g, b_qnorm_g,
           b_knorm_g, b_rel_bias, w_branch, w_out, norm2_g, peer_wq, peer_subkeys, peer_u, peer_v):
    import concourse.bacc as bacc
    from concourse.bass_utils import run_bass_kernel_spmd

    L = LAYERS
    f32 = np.float32

    def arr(a):
        return np.asarray(a)

    def chunk_pairs(w, blocks):
        return w.reshape(L, 4, 2, P, blocks, 512).transpose(0, 4, 1, 3, 2, 5).reshape(L, 4 * blocks, P, SLOT)

    def columns(w):
        n = w.shape[-1] // P
        return w.reshape(L, KC, P, n, P).transpose(0, 3, 2, 1, 4).reshape(L, n, P, SLOT)

    w_in, w_br = arr(w_in), arr(w_branch)
    stream = np.concatenate([
        chunk_pairs(w_in[:, :, :9 * 512], 9),
        columns(w_in[:, :, 9 * 512:]),
        w_br[:, UP_ORDER, :, :].reshape(L, 3, 4, P, 4, 256).transpose(0, 1, 4, 3, 2, 5).reshape(L, N_BR, P, SLOT),
        chunk_pairs(arr(w_out), 2),
        columns(arr(peer_wq)),
    ], axis=1).reshape(L * N_STREAM, P, SLOT)
    w_u = arr(peer_u).reshape(L, P, KEYS, KC, P).transpose(0, 2, 4, 3, 1).reshape(L * KEYS, P, SLOT)
    w_v = arr(peer_v).reshape(L, P, KEYS, SLOT)
    subk = arr(peer_subkeys).transpose(0, 4, 2, 1, 3).reshape(L, P, 16 * P)

    def everywhere(a):
        return np.broadcast_to(a[:, None, :], (L, P, a.shape[-1]))

    lam_init = np.array([0.8 - 0.6 * math.exp(-0.3 * i) for i in range(L)])
    half = HD // 8
    inv = 1.0 / (f32(500000.0) ** (np.arange(0, 2 * half, 2, dtype=f32) / f32(2 * half)))
    ang = np.arange(T, dtype=f32)[:, None] * inv[None, :].astype(f32)

    def table(a):
        return np.broadcast_to(a.astype(f32).reshape(TT, P, 8).transpose(1, 0, 2).reshape(1, P, 16), (L, P, 16))

    params = np.concatenate([
        arr(norm1_g).reshape(L, KC, P).transpose(0, 2, 1),
        arr(norm2_g).reshape(L, KC, P).transpose(0, 2, 1),
        arr(a_subln_g).reshape(L, P, 1),
        np.broadcast_to(lam_init.astype(f32)[:, None, None], (L, P, 1)),
        np.broadcast_to((1.0 - lam_init).astype(f32)[:, None, None], (L, P, 1)),
        table(np.cos(ang)), table(np.sin(ang)),
        *[everywhere(arr(a)) for a in (a_qnorm_g, a_knorm_g, b_qnorm_g, b_knorm_g, lam_q1, lam_q2, lam_k1, lam_k2)],
    ], axis=2)
    distance = np.clip(np.arange(P)[:, None] - np.arange(2 * P)[None, :] + P, -REL, REL) + REL
    arrays = {
        "x": arr(x).reshape(TT, P, D).transpose(1, 0, 2), "stream": stream, "w_u": w_u, "w_v": w_v, "subk": subk,
        "params": params, "bias": arr(b_rel_bias)[:, :, distance].transpose(0, 2, 1, 3).reshape(L, P, B_HEADS * 2 * P),
    }
    arrays = {f"in_{k}": np.ascontiguousarray(a) for k, a in arrays.items()}

    nc = bacc.Bacc("TRN2", target_bir_lowering=False, num_devices=1)
    args = [nc.dram_tensor(k, a.shape, mybir.dt.from_np(a.dtype), kind="ExternalInput").ap()
            for k, a in arrays.items()]
    out = nc.dram_tensor("out_0", (P, TT, D), mybir.dt.float32, kind="ExternalOutput").ap()
    build(nc, *args, out)
    r = run_bass_kernel_spmd(nc, [arrays], core_ids=[0])
    return r.results[0]["out_0"].transpose(1, 0, 2).reshape(1, T, D)
```
